# Optimizing a Trainium2 kernel written in Bass

```python
import math
import jax
import jax.numpy as jnp
from jax import lax
import numpy as np

D_MODEL = 1024
BATCH = 1
SEQ = 256
DEPTH = 2

GRID_W = 64
CTX_LEN = 256
N_MIXERS = 3
EPS = 1e-6
ROPE_BASE = 10000.0
Q_BLOCK = 128
N_MOD = 6

MLA_HEADS = 8
MLA_NOPE = 128
MLA_ROPE = 64
MLA_V = 128
MLA_Q_RANK = 384
MLA_KV_RANK = 256

HG_HEADS = 8
HG_DK = D_MODEL // HG_HEADS
HG_DV = D_MODEL // HG_HEADS
HG_CHUNK = 64

DF_HEADS = 8
DF_DQK = D_MODEL // (2 * DF_HEADS)
DF_DV = 2 * DF_DQK

D_FF = -(-(8 * D_MODEL) // (3 * 256)) * 256

N_MLA = (DEPTH + N_MIXERS - 1) // N_MIXERS
N_HG = (DEPTH + N_MIXERS - 2) // N_MIXERS
N_DF = DEPTH // N_MIXERS


def rms_norm(x, w):
    xf = x.astype(jnp.float32)
    y = xf * lax.rsqrt(jnp.mean(xf * xf, axis=-1, keepdims=True) + EPS)
    return (y * w.astype(jnp.float32)).astype(x.dtype)

def modulate(x, shift, scale):
    return x * (1 + scale) + shift

def swiglu(a, w1, w3, w2):
    return (jax.nn.silu(a @ w1) * (a @ w3)) @ w2

def split_heads(t, n_heads):
    b, n, _ = t.shape
    return t.reshape(b, n, n_heads, -1).transpose(0, 2, 1, 3)

def merge_heads(t):
    b, h, n, d = t.shape
    return t.transpose(0, 2, 1, 3).reshape(b, n, h * d)

def axial_rope_tables(rows, rot_dim):
    row = jnp.repeat(jnp.arange(rows, dtype=jnp.float32), GRID_W)
    col = jnp.tile(jnp.arange(GRID_W, dtype=jnp.float32), rows)
    axis_dim = rot_dim // 2
    inv_freq = jnp.power(ROPE_BASE, -jnp.arange(0, axis_dim, 2, dtype=jnp.float32) / axis_dim)
    ang_r = row[:, None] * inv_freq
    ang_c = col[:, None] * inv_freq
    ang = jnp.concatenate([ang_r, ang_r, ang_c, ang_c], axis=-1)
    return jnp.cos(ang), jnp.sin(ang)

def apply_axial_rope(t, cos, sin):
    t1, t2, t3, t4 = jnp.split(t, 4, axis=-1)
    rot = jnp.concatenate([-t2, t1, -t4, t3], axis=-1)
    return (t * cos + rot * sin).astype(t.dtype)

def softmax_attend(q, k, v, scale):
    s = jnp.einsum('bhqd,bhkd->bhqk', q, k, preferred_element_type=jnp.float32) * scale
    p = jax.nn.softmax(s, axis=-1)
    return jnp.einsum('bhqk,bhkd->bhqd', p.astype(v.dtype), v)

def sweep_query_blocks(fn, q):
    n, d = q.shape[-2], q.shape[-1]
    nb = n // Q_BLOCK
    qb = jnp.moveaxis(q.reshape(q.shape[:-2] + (nb, Q_BLOCK, d)), -3, 0)
    o = jnp.moveaxis(lax.map(fn, qb), 0, -3)
    return o.reshape(o.shape[:-3] + (n, o.shape[-1]))

def gla_chunk_scan(q, k, v, log_f, s0):
    b, h, n, _ = q.shape
    nc = n // HG_CHUNK

    def chunks(t):
        return jnp.moveaxis(t.reshape(b, h, nc, HG_CHUNK, t.shape[-1]), 2, 0)

    order = jnp.tril(jnp.ones((HG_CHUNK, HG_CHUNK), dtype=bool))[:, :, None]

    def step(state, inp):
        qc, kc, vc, lfc = inp
        cum = jnp.cumsum(lfc, axis=-2)
        rel = jnp.where(order, cum[..., :, None, :] - cum[..., None, :, :], -jnp.inf)
        att = jnp.einsum('bhtd,bhsd,bhtsd->bhts', qc, kc, jnp.exp(rel))
        o = (jnp.einsum('bhts,bhse->bhte', att, vc)
             + jnp.einsum('bhtd,bhde->bhte', qc * jnp.exp(cum), state))
        last = cum[..., -1:, :]
        state = (jnp.exp(last[..., 0, :])[..., None] * state
                 + jnp.einsum('bhsd,bhse->bhde', kc * jnp.exp(last - cum), vc))
        return state, o

    state, o = lax.scan(step, s0, (chunks(q), chunks(k), chunks(v), chunks(log_f)))
    o = jnp.moveaxis(o, 0, 2).reshape(b, h, n, v.shape[-1])
    return o, state

def mla_mixer(a_lat, a_ctx, rope, w_in, q_norm_w, kv_norm_w, w_uq, w_ukv, qn_w, qr_w, kn_w, kr_w, w_o, update_ctx):
    cos, sin = rope

    def project(a):
        b, n, _ = a.shape
        cq, ckv, kr = jnp.split(a @ w_in, [MLA_Q_RANK, MLA_Q_RANK + MLA_KV_RANK], axis=-1)
        q = split_heads(rms_norm(cq, q_norm_w) @ w_uq, MLA_HEADS)
        kv = split_heads(rms_norm(ckv, kv_norm_w) @ w_ukv, MLA_HEADS)
        q_nope = rms_norm(q[..., :MLA_NOPE], qn_w)
        q_rope = rms_norm(q[..., MLA_NOPE:], qr_w)
        k_nope = rms_norm(kv[..., :MLA_NOPE], kn_w)
        v = kv[..., MLA_NOPE:]
        k_rope = rms_norm(kr, kr_w)[:, None]
        return q_nope, q_rope, k_nope, k_rope, v

    def full_k(kn, kr):
        return jnp.concatenate([kn, jnp.broadcast_to(kr, kn.shape[:-1] + (MLA_ROPE,))], axis=-1)

    qn_l, qr_l, kn_l, kr_l, v_l = project(a_lat)
    qr_l = apply_axial_rope(qr_l, cos, sin)
    kr_l = apply_axial_rope(kr_l, cos, sin)
    qn_c, qr_c, kn_c, kr_c, v_c = project(a_ctx)
    k_c = full_k(kn_c, kr_c)
    k_all = jnp.concatenate([k_c, full_k(kn_l, kr_l)], axis=-2)
    v_all = jnp.concatenate([v_c, v_l], axis=-2)
    scale = 1.0 / math.sqrt(MLA_NOPE + MLA_ROPE)
    q_l = jnp.concatenate([qn_l, qr_l], axis=-1)
    o_l = sweep_query_blocks(lambda qb: softmax_attend(qb, k_all, v_all, scale), q_l)
    out_l = merge_heads(o_l) @ w_o
    out_c = None
    if update_ctx:
        q_c = jnp.concatenate([qn_c, qr_c], axis=-1)
        out_c = merge_heads(softmax_attend(q_c, k_c, v_c, scale)) @ w_o
    return out_l, out_c

def hgrn2_mixer(a_lat, a_ctx, layer_idx, w_in, lb_logits, o_norm_w, w_o, update_ctx):
    lb_cum = jnp.cumsum(jax.nn.softmax(lb_logits.astype(jnp.float32), axis=0), axis=0)
    lb = lb_cum[layer_idx] - lb_cum[0]

    def project(a):
        q, zf, zb, i, g = jnp.split(a @ w_in, 5, axis=-1)

        def heads(t):
            return split_heads(t, HG_HEADS).astype(jnp.float32)

        def log_forget(z, lbd):
            lbd = lbd.reshape(HG_HEADS, 1, HG_DK)
            return jnp.logaddexp(jnp.log(lbd), jnp.log1p(-lbd) + jax.nn.log_sigmoid(heads(z)))

        return heads(q), heads(i), log_forget(zf, lb[0]), log_forget(zb, lb[1]), g

    def scan_dir(q, i, log_f, s0):
        return gla_chunk_scan(q, -jnp.expm1(log_f), i, log_f, s0)

    def rev(t):
        return jnp.flip(t, axis=-2)

    def readout(o, g):
        o = rms_norm(o.astype(a_lat.dtype), o_norm_w)
        return (merge_heads(o) * jax.nn.silu(g)) @ w_o

    q_l, i_l, lf_l, lbk_l, g_l = project(a_lat)
    q_c, i_c, lf_c, lbk_c, g_c = project(a_ctx)
    s0 = jnp.zeros((a_ctx.shape[0], HG_HEADS, HG_DK, HG_DV), jnp.float32)
    o_cf, s_cf = scan_dir(q_c, i_c, lf_c, s0)
    o_cb, s_cb = scan_dir(rev(q_c), rev(i_c), rev(lbk_c), s0)
    o_lf, _ = scan_dir(q_l, i_l, lf_l, s_cf)
    o_lb, _ = scan_dir(rev(q_l), rev(i_l), rev(lbk_l), s_cb)
    out_l = readout(o_lf + rev(o_lb), g_l)
    out_c = readout(o_cf + rev(o_cb), g_c) if update_ctx else None
    return out_l, out_c

def diff_mixer(a_lat, a_ctx, rope, layer_idx, w_qkv, qn_w, kn_w, lam_vec, sub_norm_w, w_o, update_ctx):
    cos, sin = rope
    lam_init = 0.8 - 0.6 * math.exp(-0.3 * layer_idx)
    lv = lam_vec.astype(jnp.float32)
    lam = jnp.exp(jnp.sum(lv[0] * lv[1])) - jnp.exp(jnp.sum(lv[2] * lv[3])) + lam_init

    def project(a):
        b, n, _ = a.shape
        q, k, v = jnp.split(a @ w_qkv, 3, axis=-1)
        q = rms_norm(q.reshape(b, n, DF_HEADS, 2, DF_DQK).transpose(0, 2, 3, 1, 4), qn_w)
        k = rms_norm(k.reshape(b, n, DF_HEADS, 2, DF_DQK).transpose(0, 2, 3, 1, 4), kn_w)
        return q, k, split_heads(v, DF_HEADS)

    scale = 1.0 / math.sqrt(DF_DQK)

    def diff_attend(q, k, v):
        s = jnp.einsum('bhmqd,bhmkd->bhmqk', q, k, preferred_element_type=jnp.float32) * scale
        p = jax.nn.softmax(s, axis=-1)
        a = p[:, :, 0] - lam * p[:, :, 1]
        return jnp.einsum('bhqk,bhkd->bhqd', a.astype(v.dtype), v)

    def readout(o):
        return merge_heads(rms_norm(o, sub_norm_w) * (1.0 - lam_init)) @ w_o

    q_l, k_l, v_l = project(a_lat)
    q_l = apply_axial_rope(q_l, cos, sin)
    k_l = apply_axial_rope(k_l, cos, sin)
    q_c, k_c, v_c = project(a_ctx)
    k_all = jnp.concatenate([k_c, k_l], axis=-2)
    v_all = jnp.concatenate([v_c, v_l], axis=-2)
    out_l = readout(sweep_query_blocks(lambda qb: diff_attend(qb, k_all, v_all), q_l))
    out_c = readout(diff_attend(q_c, k_c, v_c)) if update_ctx else None
    return out_l, out_c

def first_inputs(seed: int = 0) -> dict:
    key = jax.random.key(seed)
    ks = iter(jax.random.split(key, 40))
    D = D_MODEL

    def nrm(shape, scale):
        return scale * jax.random.normal(next(ks), shape, jnp.float32)

    def gain(shape):
        return 1.0 + nrm(shape, 0.02)

    return {
        'x': nrm((BATCH, SEQ, D), 1.0),
        'c': nrm((BATCH, D), 1.0),
        'ctx': nrm((BATCH, CTX_LEN, D), 1.0),
        'c_ctx': nrm((D,), 1.0),
        'ada_w': nrm((DEPTH, D, N_MOD * D), 0.5 * D ** -0.5),
        'ada_b': nrm((DEPTH, N_MOD * D), 0.02),
        'norm1_w': gain((DEPTH, D)),
        'norm2_w': gain((DEPTH, D)),
        'ffn_w1': nrm((DEPTH, D, D_FF), D ** -0.5),
        'ffn_w3': nrm((DEPTH, D, D_FF), D ** -0.5),
        'ffn_w2': nrm((DEPTH, D_FF, D), D_FF ** -0.5),
        'mla_w_in': nrm((N_MLA, D, MLA_Q_RANK + MLA_KV_RANK + MLA_ROPE), D ** -0.5),
        'mla_q_norm_w': gain((N_MLA, MLA_Q_RANK)),
        'mla_kv_norm_w': gain((N_MLA, MLA_KV_RANK)),
        'mla_w_uq': nrm((N_MLA, MLA_Q_RANK, MLA_HEADS * (MLA_NOPE + MLA_ROPE)), MLA_Q_RANK ** -0.5),
        'mla_w_ukv': nrm((N_MLA, MLA_KV_RANK, MLA_HEADS * (MLA_NOPE + MLA_V)), MLA_KV_RANK ** -0.5),
        'mla_qn_w': gain((N_MLA, MLA_NOPE)),
        'mla_qr_w': gain((N_MLA, MLA_ROPE)),
        'mla_kn_w': gain((N_MLA, MLA_NOPE)),
        'mla_kr_w': gain((N_MLA, MLA_ROPE)),
        'mla_w_o': nrm((N_MLA, MLA_HEADS * MLA_V, D), (MLA_HEADS * MLA_V) ** -0.5),
        'hg_w_in': nrm((N_HG, D, 5 * D), D ** -0.5),
        'hg_lb_logits': nrm((DEPTH, 2, D), 1.0),
        'hg_o_norm_w': gain((N_HG, HG_DV)),
        'hg_w_o': nrm((N_HG, D, D), D ** -0.5),
        'df_w_qkv': nrm((N_DF, D, 3 * D), D ** -0.5),
        'df_qn_w': gain((N_DF, DF_DQK)),
        'df_kn_w': gain((N_DF, DF_DQK)),
        'df_lambda': nrm((N_DF, 4, DF_DQK), 0.1),
        'df_sub_norm_w': gain((N_DF, DF_DV)),
        'df_w_o': nrm((N_DF, D, D), D ** -0.5),
    }

def first_block(x, c, ctx, c_ctx, ada_w, ada_b, norm1_w, norm2_w, ffn_w1, ffn_w3, ffn_w2,
              mla_w_in, mla_q_norm_w, mla_kv_norm_w, mla_w_uq, mla_w_ukv, mla_qn_w, mla_qr_w, mla_kn_w,
              mla_kr_w, mla_w_o, hg_w_in, hg_lb_logits, hg_o_norm_w, hg_w_o,
              df_w_qkv, df_qn_w, df_kn_w, df_lambda, df_sub_norm_w, df_w_o):
    rows = x.shape[1] // GRID_W
    rope_mla = axial_rope_tables(rows, MLA_ROPE)
    rope_df = axial_rope_tables(rows, DF_DQK)
    h_ctx = ctx
    for i in range(DEPTH):
        kind, j = i % N_MIXERS, i // N_MIXERS
        update_ctx = i < DEPTH - 1
        mod_l = jnp.split((jax.nn.silu(c) @ ada_w[i] + ada_b[i])[:, None, :], N_MOD, axis=-1)
        mod_c = jnp.split((jax.nn.silu(c_ctx) @ ada_w[i] + ada_b[i])[None, None, :], N_MOD, axis=-1)
        a_l = modulate(rms_norm(x, norm1_w[i]), mod_l[0], mod_l[1])
        a_c = modulate(rms_norm(h_ctx, norm1_w[i]), mod_c[0], mod_c[1])
        if kind == 0:
            o_l, o_c = mla_mixer(a_l, a_c, rope_mla, mla_w_in[j], mla_q_norm_w[j], mla_kv_norm_w[j],
                                 mla_w_uq[j], mla_w_ukv[j], mla_qn_w[j], mla_qr_w[j], mla_kn_w[j],
                                 mla_kr_w[j], mla_w_o[j], update_ctx)
        elif kind == 1:
            o_l, o_c = hgrn2_mixer(a_l, a_c, i, hg_w_in[j], hg_lb_logits, hg_o_norm_w[j], hg_w_o[j], update_ctx)
        else:
            o_l, o_c = diff_mixer(a_l, a_c, rope_df, i, df_w_qkv[j], df_qn_w[j], df_kn_w[j], df_lambda[j],
                                  df_sub_norm_w[j], df_w_o[j], update_ctx)
        x = x + mod_l[2] * o_l
        x = x + mod_l[5] * swiglu(modulate(rms_norm(x, norm2_w[i]), mod_l[3], mod_l[4]),
                                  ffn_w1[i], ffn_w3[i], ffn_w2[i])
        if update_ctx:
            h_ctx = h_ctx + mod_c[2] * o_c
            h_ctx = h_ctx + mod_c[5] * swiglu(modulate(rms_norm(h_ctx, norm2_w[i]), mod_c[3], mod_c[4]),
                                              ffn_w1[i], ffn_w3[i], ffn_w2[i])
    return x


A_HEADS = 8
A_KV_HEADS = 2
A_GROUP = A_HEADS // A_KV_HEADS
A_HEAD_DIM = 64
A_WIDTH = A_HEADS * A_HEAD_DIM
A_KV_WIDTH = A_KV_HEADS * A_HEAD_DIM
A_SCALE = A_HEAD_DIM ** -0.5
ROPE_THETA = 10000.0
ROPE_FREQS = A_HEAD_DIM // 4

B_GROUPS = 4
B_WIDTH = D_MODEL // 2
B_GROUP_DIM = B_WIDTH // B_GROUPS
POOL_WINDOWS = (2, 4, 8, 16)

EVEN_IN = A_WIDTH + 2 * A_KV_WIDTH + B_WIDTH
EVEN_OUT = A_WIDTH + B_WIDTH

C_HEADS = 16
C_HEAD_DIM = D_MODEL // C_HEADS
C_WIDTH = C_HEADS * C_HEAD_DIM
C_SCALE = C_HEAD_DIM ** -0.5
NA_ROWS_MAX = 8
NA_COLS = 16

N_GROUPS = 4
E_PER_GROUP = 8
N_EXPERTS = N_GROUPS * E_PER_GROUP
TOP_K = 2
D_EXPERT = D_MODEL // 2
MOE_BLOCK = 128


def rmsnorm(x, g):
    xf = x.astype(jnp.float32)
    y = xf * lax.rsqrt(jnp.mean(xf * xf, axis=-1, keepdims=True) + EPS)
    return (y * g.astype(jnp.float32)).astype(x.dtype)

def modulate_2(h, shift, scale):
    return h * (1 + scale) + shift

def axial_rope_tables_2(n_tok):
    t = jnp.arange(n_tok, dtype=jnp.int32)
    pos = jnp.stack([t // GRID_W, t % GRID_W], axis=-1).astype(jnp.float32)
    inv = ROPE_THETA ** (-jnp.arange(ROPE_FREQS, dtype=jnp.float32) / ROPE_FREQS)
    ang = pos[:, :, None] * inv
    return jnp.cos(ang), jnp.sin(ang)

def apply_axial_rope_2(x, cos, sin):
    sh = x.shape
    xr = x.reshape(sh[:-1] + (2, 2, ROPE_FREQS)).astype(jnp.float32)
    x1, x2 = xr[..., 0, :], xr[..., 1, :]
    out = jnp.stack([x1 * cos - x2 * sin, x1 * sin + x2 * cos], axis=-2)
    return out.reshape(sh).astype(x.dtype)

def gqa_queries(q, gain):
    B, L, _ = q.shape
    q = rmsnorm(q.reshape(B, L, A_KV_HEADS, A_GROUP, A_HEAD_DIM), gain)
    return q.transpose(0, 2, 3, 1, 4)

def gqa_keys(k, gain):
    B, L, _ = k.shape
    return rmsnorm(k.reshape(B, L, A_KV_HEADS, A_HEAD_DIM), gain).transpose(0, 2, 1, 3)

def gqa_values(v):
    B, L, _ = v.shape
    return v.reshape(B, L, A_KV_HEADS, A_HEAD_DIM).transpose(0, 2, 1, 3)

def pool_mixer(u, pool_w, pool_scale):
    B, L, _ = u.shape
    ug = u.reshape(B, L, B_GROUPS, B_GROUP_DIM).astype(jnp.float32)
    cs = jnp.concatenate([jnp.zeros((B, 1, B_GROUPS, B_GROUP_DIM), jnp.float32), jnp.cumsum(ug, axis=1)], axis=1)
    t = jnp.arange(L, dtype=jnp.int32)
    means = []
    for g, w in enumerate(POOL_WINDOWS):
        lo = jnp.clip(t - w // 2, 0, L)
        hi = jnp.clip(t - w // 2 + w, 0, L)
        cnt = (hi - lo).astype(jnp.float32)
        cs_g = cs[:, :, g]
        means.append((cs_g[:, hi] - cs_g[:, lo]) / cnt[None, :, None])
    pooled = (jnp.stack(means, axis=2) - ug).astype(u.dtype)
    mixed = jnp.einsum('blgc,gcd->blgd', pooled, pool_w)
    return mixed.reshape(B, L, B_WIDTH) * pool_scale

def even_mixer(h, hc, w_in, w_out, q_gain, k_gain, pool_w, pool_scale, cos, sin, ctx_out):
    B, S, _ = h.shape
    cuts = (A_WIDTH, A_WIDTH + A_KV_WIDTH, A_WIDTH + 2 * A_KV_WIDTH)
    q, k, v, u = jnp.split(h @ w_in, cuts, axis=-1)
    if ctx_out:
        qc, kc, vc, uc = jnp.split(hc @ w_in, cuts, axis=-1)
    else:
        kc, vc = jnp.split(hc @ w_in[:, A_WIDTH:A_WIDTH + 2 * A_KV_WIDTH], 2, axis=-1)
    kc_h = gqa_keys(kc, k_gain)
    vc_h = gqa_values(vc)
    q_h = apply_axial_rope_2(gqa_queries(q, q_gain), cos, sin)
    k_h = apply_axial_rope_2(gqa_keys(k, k_gain), cos, sin)
    k_all = jnp.concatenate([kc_h, k_h], axis=2)
    v_all = jnp.concatenate([vc_h, gqa_values(v)], axis=2)
    nb = S // Q_BLOCK
    qb = q_h.reshape(B, A_KV_HEADS, A_GROUP, nb, Q_BLOCK, A_HEAD_DIM).transpose(3, 0, 1, 2, 4, 5)

    def attend_block(qblk):
        s = jnp.einsum('bhgqd,bhkd->bhgqk', qblk, k_all).astype(jnp.float32) * A_SCALE
        p = jax.nn.softmax(s, axis=-1).astype(v_all.dtype)
        return jnp.einsum('bhgqk,bhkd->bhgqd', p, v_all)

    o = lax.map(attend_block, qb)
    a_lat = o.transpose(1, 0, 4, 2, 3, 5).reshape(B, S, A_WIDTH)
    b_lat = pool_mixer(u, pool_w, pool_scale)
    y = jnp.concatenate([a_lat, b_lat], axis=-1) @ w_out
    if not ctx_out:
        return y, None
    Lc = hc.shape[1]
    qc_h = gqa_queries(qc, q_gain)
    s = jnp.einsum('bhgqd,bhkd->bhgqk', qc_h, kc_h).astype(jnp.float32) * A_SCALE
    p = jax.nn.softmax(s, axis=-1).astype(vc_h.dtype)
    a_ctx = jnp.einsum('bhgqk,bhkd->bhgqd', p, vc_h).transpose(0, 3, 1, 2, 4).reshape(B, Lc, A_WIDTH)
    b_ctx = pool_mixer(uc, pool_w, pool_scale)
    yc = jnp.concatenate([a_ctx, b_ctx], axis=-1) @ w_out
    return y, yc

def c_heads(t):
    B, L, _ = t.shape
    return t.reshape(B, L, C_HEADS, C_HEAD_DIM).transpose(0, 2, 1, 3)

def odd_mixer(h, hc, w_in, w_out, rel_bias, ctx_out):
    B, S, _ = h.shape
    rows = S // GRID_W
    kh = min(NA_ROWS_MAX, rows)
    q, k, v = jnp.split(h @ w_in, 3, axis=-1)
    if ctx_out:
        qc, kc, vc = jnp.split(hc @ w_in, 3, axis=-1)
    else:
        kc, vc = jnp.split(hc @ w_in[:, C_WIDTH:], 2, axis=-1)
    kc_h, vc_h = c_heads(kc), c_heads(vc)

    def grid(t):
        return t.reshape(B, rows, GRID_W, C_HEADS, C_HEAD_DIM).transpose(0, 3, 1, 2, 4)

    qg, kg, vg = grid(q), grid(k), grid(v)
    cols = jnp.arange(GRID_W, dtype=jnp.int32)
    col_start = jnp.clip(cols - NA_COLS // 2, 0, GRID_W - NA_COLS)
    col_idx = col_start[:, None] + jnp.arange(NA_COLS, dtype=jnp.int32)[None, :]
    col_off = col_idx - cols[:, None] + (NA_COLS - 1)
    n_loc = kh * NA_COLS

    def row_block(r):
        rs = jnp.clip(r - kh // 2, 0, rows - kh)
        qr = lax.dynamic_index_in_dim(qg, r, axis=2, keepdims=False)
        kr = lax.dynamic_slice_in_dim(kg, rs, kh, axis=2)
        vr = lax.dynamic_slice_in_dim(vg, rs, kh, axis=2)
        kw = kr[:, :, :, col_idx]
        vw = vr[:, :, :, col_idx]
        row_off = rs + jnp.arange(kh, dtype=jnp.int32) - r + (NA_ROWS_MAX - 1)
        bias = rel_bias[:, row_off][:, :, col_off].transpose(0, 2, 1, 3)
        s_loc = jnp.einsum('bhqd,bhiqjd->bhqij', qr, kw).astype(jnp.float32) * C_SCALE + bias.astype(jnp.float32)
        s_ctx = jnp.einsum('bhqd,bhkd->bhqk', qr, kc_h).astype(jnp.float32) * C_SCALE
        s = jnp.concatenate([s_loc.reshape(B, C_HEADS, GRID_W, n_loc), s_ctx], axis=-1)
        p = jax.nn.softmax(s, axis=-1).astype(vw.dtype)
        p_loc = p[..., :n_loc].reshape(B, C_HEADS, GRID_W, kh, NA_COLS)
        return (jnp.einsum('bhqij,bhiqjd->bhqd', p_loc, vw)
                + jnp.einsum('bhqk,bhkd->bhqd', p[..., n_loc:], vc_h))

    o = lax.map(row_block, jnp.arange(rows, dtype=jnp.int32))
    y = o.transpose(1, 0, 3, 2, 4).reshape(B, S, C_WIDTH) @ w_out
    if not ctx_out:
        return y, None
    Lc = hc.shape[1]
    qc_h = c_heads(qc)
    s = jnp.einsum('bhqd,bhkd->bhqk', qc_h, kc_h).astype(jnp.float32) * C_SCALE
    p = jax.nn.softmax(s, axis=-1).astype(vc_h.dtype)
    yc = jnp.einsum('bhqk,bhkd->bhqd', p, vc_h).transpose(0, 2, 1, 3).reshape(B, Lc, C_WIDTH) @ w_out
    return y, yc

def hier_moe(xt, wg, bg, we, be, w1, w3, w2):
    T, D = xt.shape
    xf = xt.astype(jnp.float32)
    g_logits = xf @ wg.astype(jnp.float32) + bg.astype(jnp.float32)
    g_prob = jax.nn.softmax(g_logits, axis=-1)
    g_idx = jnp.argmax(g_logits, axis=-1)
    g_w = jnp.take_along_axis(g_prob, g_idx[:, None], axis=1)[:, 0]
    e_logits = (xf @ we.astype(jnp.float32) + be.astype(jnp.float32)).reshape(T, N_GROUPS, E_PER_GROUP)
    e_logits = jnp.take_along_axis(e_logits, g_idx[:, None, None], axis=1)[:, 0]
    top_p, top_e = lax.top_k(jax.nn.softmax(e_logits, axis=-1), TOP_K)
    top_p = top_p / jnp.sum(top_p, axis=-1, keepdims=True)
    weights = (g_w[:, None] * top_p).reshape(-1)
    flat_e = (g_idx[:, None] * E_PER_GROUP + top_e).reshape(-1)
    n_assign = T * TOP_K
    order = jnp.argsort(flat_e)
    sorted_e = flat_e[order]
    tok = order // TOP_K
    counts = jnp.bincount(flat_e, length=N_EXPERTS)
    start = jnp.cumsum(counts) - counts
    padded = (counts + MOE_BLOCK - 1) // MOE_BLOCK * MOE_BLOCK
    pend = jnp.cumsum(padded)
    pstart = pend - padded
    dest = pstart[sorted_e] + jnp.arange(n_assign, dtype=jnp.int32) - start[sorted_e]
    n_blocks = -(-n_assign // MOE_BLOCK) + N_EXPERTS
    xpad = jnp.zeros((n_blocks * MOE_BLOCK, D), xt.dtype).at[dest].set(xt[tok])
    block_e = jnp.minimum(jnp.searchsorted(pend, jnp.arange(n_blocks, dtype=jnp.int32) * MOE_BLOCK, side='right'), N_EXPERTS - 1)

    def expert_block(args):
        xb, e = args
        hb = jax.nn.silu(xb @ w1[e]) * (xb @ w3[e])
        return hb @ w2[e]

    ypad = lax.map(expert_block, (xpad.reshape(n_blocks, MOE_BLOCK, D), block_e))
    y = ypad.reshape(-1, D)[dest] * weights[order][:, None].astype(xt.dtype)
    return jnp.zeros_like(xt).at[tok].add(y)

def second_inputs(seed: int = 0) -> dict:
    key = jax.random.key(seed)
    ks = iter(jax.random.split(key, 32))
    n_even = (DEPTH + 1) // 2
    n_odd = DEPTH // 2
    D = D_MODEL

    def nrm(shape, scale):
        return jax.random.normal(next(ks), shape, jnp.float32) * scale

    return {
        'x': nrm((BATCH, SEQ, D), 1.0),
        'c': nrm((BATCH, D), 1.0),
        'ctx': nrm((BATCH, CTX_LEN, D), 1.0),
        'c_ctx': nrm((D,), 1.0),
        'ada_w': nrm((DEPTH, D, N_MOD * D), 0.5 * D ** -0.5),
        'ada_b': nrm((DEPTH, N_MOD * D), 0.02),
        'norm_mix_g': 1.0 + nrm((DEPTH, D), 0.1),
        'norm_ffn_g': 1.0 + nrm((DEPTH, D), 0.1),
        'even_w_in': nrm((n_even, D, EVEN_IN), D ** -0.5),
        'even_w_out': nrm((n_even, EVEN_OUT, D), EVEN_OUT ** -0.5),
        'a_q_gain': 1.0 + nrm((n_even, A_HEAD_DIM), 0.1),
        'a_k_gain': 1.0 + nrm((n_even, A_HEAD_DIM), 0.1),
        'pool_w': nrm((n_even, B_GROUPS, B_GROUP_DIM, B_GROUP_DIM), B_GROUP_DIM ** -0.5),
        'pool_scale': 1.0 + nrm((n_even, B_WIDTH), 0.1),
        'odd_w_in': nrm((n_odd, D, 3 * C_WIDTH), D ** -0.5),
        'odd_w_out': nrm((n_odd, C_WIDTH, D), C_WIDTH ** -0.5),
        'na_rel_bias': nrm((n_odd, C_HEADS, 2 * NA_ROWS_MAX - 1, 2 * NA_COLS - 1), 0.5),
        'moe_w_group': nrm((DEPTH, D, N_GROUPS), D ** -0.5),
        'moe_b_group': nrm((DEPTH, N_GROUPS), 0.01),
        'moe_w_expert': nrm((DEPTH, D, N_EXPERTS), D ** -0.5),
        'moe_b_expert': nrm((DEPTH, N_EXPERTS), 0.01),
        'moe_w1': nrm((DEPTH, N_EXPERTS, D, D_EXPERT), D ** -0.5),
        'moe_w3': nrm((DEPTH, N_EXPERTS, D, D_EXPERT), D ** -0.5),
        'moe_w2': nrm((DEPTH, N_EXPERTS, D_EXPERT, D), D_EXPERT ** -0.5),
        'final_g': 1.0 + nrm((D,), 0.1),
    }

def second_block(x, c, ctx, c_ctx, ada_w, ada_b, norm_mix_g, norm_ffn_g, even_w_in, even_w_out, a_q_gain, a_k_gain,
              pool_w, pool_scale, odd_w_in, odd_w_out, na_rel_bias, moe_w_group, moe_b_group, moe_w_expert,
              moe_b_expert, moe_w1, moe_w3, moe_w2, final_g):
    B, S, D = x.shape
    Lc = ctx.shape[1]
    cos, sin = axial_rope_tables_2(S)
    for l in range(DEPTH):
        last = l == DEPTH - 1
        mod = jax.nn.silu(c) @ ada_w[l] + ada_b[l]
        mod_c = jax.nn.silu(c_ctx) @ ada_w[l] + ada_b[l]
        sh1, sc1, g1, sh2, sc2, g2 = jnp.split(mod[:, None, :], N_MOD, axis=-1)
        csh1, csc1, cg1, csh2, csc2, cg2 = jnp.split(mod_c, N_MOD, axis=-1)
        h = modulate_2(rmsnorm(x, norm_mix_g[l]), sh1, sc1)
        hc = modulate_2(rmsnorm(ctx, norm_mix_g[l]), csh1, csc1)
        if l % 2 == 0:
            i = l // 2
            y, yc = even_mixer(h, hc, even_w_in[i], even_w_out[i], a_q_gain[i], a_k_gain[i], pool_w[i],
                               pool_scale[i], cos, sin, not last)
        else:
            i = l // 2
            y, yc = odd_mixer(h, hc, odd_w_in[i], odd_w_out[i], na_rel_bias[i], not last)
        x = x + g1 * y
        h2 = modulate_2(rmsnorm(x, norm_ffn_g[l]), sh2, sc2)
        moe_args = (moe_w_group[l], moe_b_group[l], moe_w_expert[l], moe_b_expert[l], moe_w1[l], moe_w3[l], moe_w2[l])
        if not last:
            ctx = ctx + cg1 * yc
            hc2 = modulate_2(rmsnorm(ctx, norm_ffn_g[l]), csh2, csc2)
            f = hier_moe(jnp.concatenate([h2.reshape(B * S, D), hc2.reshape(B * Lc, D)], axis=0), *moe_args)
            x = x + g2 * f[:B * S].reshape(B, S, D)
            ctx = ctx + cg2 * f[B * S:].reshape(B, Lc, D)
        else:
            f = hier_moe(h2.reshape(B * S, D), *moe_args)
            x = x + g2 * f.reshape(B, S, D)
    return rmsnorm(x, final_g)


def setup_inputs(seed=0):
    out = dict(first_inputs(seed))
    for name, value in second_inputs(seed + 1).items():
        if name != "x":
            out[name + "_2"] = value
    return out


def reference(
    x, c, ctx, c_ctx, ada_w, ada_b, norm1_w, norm2_w, ffn_w1, ffn_w3, ffn_w2, mla_w_in,
    mla_q_norm_w, mla_kv_norm_w, mla_w_uq, mla_w_ukv, mla_qn_w, mla_qr_w, mla_kn_w, mla_kr_w,
    mla_w_o, hg_w_in, hg_lb_logits, hg_o_norm_w, hg_w_o, df_w_qkv, df_qn_w, df_kn_w, df_lambda,
    df_sub_norm_w, df_w_o, c_2, ctx_2, c_ctx_2, ada_w_2, ada_b_2, norm_mix_g_2, norm_ffn_g_2,
    even_w_in_2, even_w_out_2, a_q_gain_2, a_k_gain_2, pool_w_2, pool_scale_2, odd_w_in_2,
    odd_w_out_2, na_rel_bias_2, moe_w_group_2, moe_b_group_2, moe_w_expert_2, moe_b_expert_2,
    moe_w1_2, moe_w3_2, moe_w2_2, final_g_2,
):
    x = first_block(
        x, c, ctx, c_ctx, ada_w, ada_b, norm1_w, norm2_w, ffn_w1, ffn_w3, ffn_w2, mla_w_in,
        mla_q_norm_w, mla_kv_norm_w, mla_w_uq, mla_w_ukv, mla_qn_w, mla_qr_w, mla_kn_w,
        mla_kr_w, mla_w_o, hg_w_in, hg_lb_logits, hg_o_norm_w, hg_w_o, df_w_qkv, df_qn_w,
        df_kn_w, df_lambda, df_sub_norm_w, df_w_o,
    )
    return second_block(
        x, c_2, ctx_2, c_ctx_2, ada_w_2, ada_b_2, norm_mix_g_2, norm_ffn_g_2, even_w_in_2,
        even_w_out_2, a_q_gain_2, a_k_gain_2, pool_w_2, pool_scale_2, odd_w_in_2, odd_w_out_2,
        na_rel_bias_2, moe_w_group_2, moe_b_group_2, moe_w_expert_2, moe_b_expert_2, moe_w1_2,
        moe_w3_2, moe_w2_2, final_g_2,
    )


_drawn_inputs = setup_inputs


def setup_inputs(seed=0):
    import zlib

    import numpy as np

    out = dict(_drawn_inputs(seed))
    spreads = {}
    factors = {'norm1_w': 4.713,
     'norm2_w': 5.658,
     'mla_q_norm_w': 8.0,
     'mla_kv_norm_w': 8.0,
     'mla_qn_w': 8.0,
     'mla_qr_w': 8.0,
     'mla_kn_w': 8.0,
     'mla_kr_w': 8.0,
     'hg_o_norm_w': 25.567,
     'a_q_gain_2': 64.0,
     'a_k_gain_2': 63.711,
     'na_rel_bias_2': 27.593,
     'moe_b_group_2': 64.0,
     'moe_b_expert_2': 58.384,
     'ctx_2': 4.573,
     'c_ctx_2': 5.497,
     'ada_b_2': 8.0,
     'norm_mix_g_2': 6.349,
     'norm_ffn_g_2': 8.0,
     'pool_w_2': 4.028,
     'pool_scale_2': 8.0,
     'odd_w_in_2': 3.927,
     'odd_w_out_2': 3.906,
     'moe_w_group_2': 6.681,
     'moe_w_expert_2': 6.608,
     'moe_w1_2': 6.276,
     'moe_w3_2': 5.834,
     'moe_w2_2': 5.814}
    for name, (base, spread) in spreads.items():
        noise = np.random.default_rng([zlib.crc32(name.encode()), seed]).standard_normal(out[name].shape)
        drawn = base * np.exp(spread * noise) if base else spread * noise
        out[name] = jnp.asarray(drawn.astype(out[name].dtype))
    for name, factor in factors.items():
        out[name] = (out[name] * factor).astype(out[name].dtype)
    return out
```

```python
import math

import numpy as np

import concourse.bass as bass
from concourse import mybir

F32 = mybir.dt.float32
I32 = mybir.dt.int32
ALU = mybir.AluOpType
ACT = mybir.ActivationFunctionType
AX = mybir.AxisListType

P = 128
D = 1024
KD = D // P
S = 256
T = 2 * S
NT = T // P
GRID = 64
FF = 2816
FB = FF // P
HEADS = 8
QR, KVR, ROPE = 384, 256, 64
MLA_IN = QR + KVR + ROPE
HD = 64
EVEN_IN = 1280
POOLS = (2, 4, 8, 16)
NA_ROWS, NA_COLS = 8, 16
NG, EPG, DE = 4, 8, 512
NE = NG * EPG
NR = NG + NE
CAP = 64
EPS = 1e-6
LEVELS = 8
SLOTS = 6
SLOT = 2048
NEG = -1.0e30
FAR = 1.0e6
FIRST = 8

VECS = [("norm1", 2 * KD), ("norm2", 2 * KD), ("mla_q", 3), ("mla_kv", 2), ("mla_qn", 1), ("mla_qr", 1),
        ("mla_kn", 1), ("mla_kr", 1), ("hg_o", 1), ("hg_lb", 4 * KD), ("mix", 2 * KD), ("ffn", 2 * KD),
        ("a_q", 1), ("a_k", 1), ("pool", 4), ("final", KD), ("ada_b", 4 * 48), ("moe_b", 2 * NR)]
CONSTS = [("ident", P), ("ones", P), ("pair", P), ("turn", P), ("tri", P), ("cos", T), ("sin", T),
          ("decay", 2 * LEVELS * P), ("near", S), ("pools", 4 * 2 * S), ("slot", CAP),
          ("prior", EPG), ("rounds", 8), ("stream", 2), ("eps", 1)]


def places(table):
    at, out = 0, {}
    for name, n in table:
        out[name] = (at, at + n)
        at += n
    return out, at


VEC, NVEC = places(VECS)
CON, NCON = places(CONSTS)


def constants():
    c = np.zeros((P, NCON), np.float32)

    def put(name, value):
        a, b = CON[name]
        c[:, a:b] = np.asarray(value, np.float32).reshape(P, b - a)

    p = np.arange(P)
    put("ident", np.eye(P))
    put("ones", np.ones((P, P)))
    put("pair", p[:, None] // HD == p[None, :] // HD)
    turn = np.zeros((P, P))
    for m in range(P):
        if (m // 16) % 2 == 0:
            turn[m + 16, m] = -1
        else:
            turn[m - 16, m] = 1
    put("turn", turn)
    put("tri", p[:, None] < p[None, :])
    tok = np.arange(S)
    freq = np.power(np.float32(10000.0), -np.arange(16, dtype=np.float32) / np.float32(16)).astype(np.float32)
    q = p % HD
    where = np.where(q[:, None] < 32, tok[None, :] // GRID, tok[None, :] % GRID).astype(np.float32)
    angle = where * freq[q % 16][:, None]
    cos, sin = np.ones((P, T)), np.zeros((P, T))
    cos[:, :S], sin[:, :S] = np.cos(angle), np.sin(angle)
    put("cos", cos)
    put("sin", sin)
    masks = np.zeros((2, P, LEVELS, P))
    for l in range(LEVELS - 1):
        w = 64 >> l
        same = p[:, None] // (2 * w) == p[None, :] // (2 * w)
        late = (p // w) % 2 == 1
        masks[0, :, l] = same & ~late[:, None] & late[None, :]
        masks[1, :, l] = same & late[:, None] & ~late[None, :]
    masks[:, :, LEVELS - 1] = np.eye(P)
    put("decay", masks.transpose(1, 0, 2, 3))
    start = np.clip(p % GRID - NA_COLS // 2, 0, GRID - NA_COLS)
    kc = tok % GRID
    inside = (kc[None, :] >= start[:, None]) & (kc[None, :] < start[:, None] + NA_COLS)
    put("near", np.where(inside, 0.0, NEG))
    pools = np.zeros((4, S, S), np.float32)
    for g, w in enumerate(POOLS):
        for t in range(S):
            lo, hi = max(t - w // 2, 0), min(t - w // 2 + w, S)
            pools[g, lo:hi, t] = np.float32(1) / np.float32(hi - lo)
            pools[g, t, t] -= 1
    put("pools", pools.reshape(4, 2, P, S).transpose(2, 0, 1, 3))
    put("slot", np.tile(np.arange(CAP), (P, 1)))
    put("prior", np.tile(np.arange(EPG, 0, -1), (P, 1)))
    put("rounds", np.tile(np.arange(8) * CAP, (P, 1)))
    put("stream", p[:, None] % 32 == np.arange(2)[None, :])
    put("eps", np.full((P, 1), EPS))
    return c


class Signal:

    def __init__(self, nc, name):
        self.sem = nc.alloc_semaphore(name)
        self.base = FIRST

    def at(self, n):
        return n + self.base

    def passed(self, n):
        self.base += n


class Chain:

    def __init__(self, eng, signal, turn=0, each=0):
        self.eng, self.counts, self.turn, self.each, self.n = eng, signal, turn, each, 0

    def __call__(self, ins):
        self.n += 1
        ins.then_inc(self.counts.sem, 1)
        self.eng.wait_ge(self.counts.sem, self.counts.at(self.turn * self.each + self.n))


def build(nc, io, out, upto=99):
    act_, dve_, pe_ = nc.scalar, nc.vector, nc.tensor

    def sb(name, shape, dtype=F32):
        return nc.alloc_sbuf_tensor(name, shape, dtype)

    X = sb("X", [P, KD, T])
    A = sb("A", [P, KD, T])
    RING = sb("RING", [P, SLOTS, SLOT])
    BIG = sb("BIG", [P, FB * T])
    WORK = sb("WORK", [P, KD * T])
    ROOT = sb("ROOT", [P, 3, T])
    SIL = sb("SIL", [P, 2, T])
    MODS = sb("MODS", [P, 4, 48, 2])
    GAIN = sb("GAIN", [P, 2, KD])
    CST = sb("CST", [P, NCON])
    V = sb("V", [P, NVEC])
    CS = sb("CS", [P, 2, KD, 32])
    SMALL = sb("SMALL", [P, 640])
    ROUNDS = sb("ROUNDS", [1, 1], I32)
    PB = nc.alloc_psum_tensor("PB", [P, 8, T], F32)

    def con(name):
        return CST[:, CON[name][0]:CON[name][1]]

    def vec(name, a=0, b=None):
        x, y = VEC[name]
        return V[:, x + a:(y if b is None else x + b)]

    IDENT, ONES, PAIR, TURN, TRI = (con(n) for n in ("ident", "ones", "pair", "turn", "tri"))
    COS, SIN = con("cos"), con("sin")

    signals = {}

    def sig(name):
        if name not in signals:
            signals[name] = Signal(nc, name)
        return signals[name]

    loaded = [sig(f"loaded{s}") for s in range(SLOTS)]
    used = [sig(f"used{s}") for s in range(SLOTS)]
    for name in ("inputs_in", "stored", "dve_step", "act_step", "squared", "summed", "rooted", "normed",
                 "rotated", "roped", "mod_summed", "silu_made", "h_made", "drained", "projected",
                 "scored", "peaked", "exped", "shared", "flipped", "turned", "weighted", "carried",
                 "staged", "gated", "forgot", "logged", "summed_up", "decayed", "spread", "levelled",
                 "levels_ready", "kx_flipped", "kx_copied", "state_made", "state_copied", "products",
                 "attended", "read_out", "biased", "bias_in", "pooled", "pool_copied", "mixed",
                 "token_flipped", "token_copied", "routed", "group_exped", "second_exped", "ranked",
                 "rank_in", "picked", "gathered", "gather_copied", "expert_silu", "expert_h",
                 "slots_out", "pick_flipped", "pick_copied", "scattered", "added", "rounds_in",
                 "cleared", "absed", "mod_flipped", "inverted",
                 "xg_flipped", "xg_copied", "h_flipped", "h_copied", "y_copied", "weighed"):
        sig(name)

    def tile(s, k, n, at=0):
        return RING[:, s, at:at + k * n].rearrange("p (k n) -> p k n", k=k)

    def rows(w, a, b):
        return w[:, a:b].rearrange("(k p) n -> p k n", p=P)

    def passed(**counts):
        for name, n in counts.items():
            signals[name].passed(n)

    def half(w):
        return slice(w * S, (w + 1) * S)

    with nc.Block() as block:
        @block.sync
        def _(sp):
            for s in signals.values():
                sp.sem_inc(s.sem, FIRST)

    with nc.Block() as block:
        @block.sync
        def _(sp):
            for dst, name in ((CS, "cvec"), (V, "vecs"), (CST, "consts")):
                flat = dst[:] if len(dst.shape) == 2 else dst[:].rearrange("p a b c -> p (a b c)")
                sp.dma_start(flat, io[name]).then_inc(sig("inputs_in").sem, 16)
            for w, name in enumerate(("xT", "ctxT")):
                sp.dma_start(X[:, :, half(w)], io[name].rearrange("(k p) t -> p k t", p=P)) \
                    .then_inc(sig("inputs_in").sem, 16)

        @block.scalar
        def _(act):
            act.wait_ge(sig("inputs_in").sem, sig("inputs_in").at(5 * 16))
            act_.activation(CS[:], CS[:], ACT.Silu).then_inc(sig("staged").sem, 1)
    passed(inputs_in=80, staged=1)

    def modulations():
        turns, chunks = 4, SLOTS // 2
        layers = [(0, io["ada_w"][0]), (0, io["ada_w"][1]), (1, io["ada_w_2"][0]), (1, io["ada_w_2"][1])]
        ROW = BIG[:, 0:chunks * T].rearrange("p (j t) -> p j t", t=T)
        with nc.Block() as block:
            @block.sync
            def _(sp):
                for n, (_, w) in enumerate(layers):
                    cut = w.rearrange("(a k p) (n c) -> p n a k c", a=2, p=P, c=T)
                    with sp.Fori(0, turns) as i:
                        for s in range(SLOTS):
                            sp.wait_ge(used[s].sem, used[s].at(turns * n + i))
                            sp.dma_start(tile(s, 4, T), cut[:, chunks * i + s // 2, s % 2]).then_inc(loaded[s].sem, 16)

            @block.tensor
            def _(pe):
                for n, (b, _) in enumerate(layers):
                    with pe.Fori(0, turns) as i:
                        turn = turns * n + i

                        def multiply(j):
                            for a in range(2):
                                s = 2 * j + a
                                pe.wait_ge(loaded[s].sem, loaded[s].at(16 * (turn + 1)))
                                for k in range(4):
                                    last = pe_.matmul(PB[32 * k:32 * k + 32, 1 + j, :], CS[:, b, 4 * a + k, :],
                                                      tile(s, 4, T)[:, k, :], start=a == 0, stop=a == 1)
                                last.then_inc(used[s].sem, 1)

                        def turn_over(j):
                            pe.wait_ge(sig("drained").sem, sig("drained").at(chunks * turn + j + 1))
                            for m in range(4):
                                at = 96 * n + (chunks * i + j) * 8 + 2 * m
                                last = pe_.matmul(PB[:, 0, bass.ds(at, 2)], ROW[:, j, m * P:(m + 1) * P],
                                                  con("stream"), start=True, stop=True)
                            last.then_inc(sig("mod_flipped").sem, 1)

                        multiply(0)
                        multiply(1)
                        turn_over(0)
                        multiply(2)
                        turn_over(1)
                        turn_over(2)

            @block.scalar
            def _(act):
                for n in range(len(layers)):
                    with act.Fori(0, turns) as i:
                        turn = turns * n + i
                        for j in range(chunks):
                            act.wait_ge(used[2 * j + 1].sem, used[2 * j + 1].at(turn + 1))
                            act.wait_ge(sig("mod_flipped").sem, sig("mod_flipped").at(chunks * (turn - 1) + j + 1))
                            act_.activation(ROW[:, j, :], PB[:, 1 + j, :], ACT.Copy).then_inc(sig("drained").sem, 1)

            @block.vector
            def _(dve):
                dve.wait_ge(sig("mod_flipped").sem, sig("mod_flipped").at(4 * turns * chunks))
                bias = vec("ada_b").unsqueeze(2).broadcast_to([P, 192, 2])
                dve_.tensor_tensor(MODS[:].rearrange("p l n w -> p (l n) w"),
                                   PB[:, 0, 0:384].rearrange("p (n w) -> p n w", w=2), bias, ALU.add) \
                    .then_inc(sig("mod_summed").sem, 1)
        for s in range(SLOTS):
            used[s].passed(4 * turns)
            loaded[s].passed(4 * turns * 16)
        passed(mod_summed=1, mod_flipped=4 * turns * chunks, drained=4 * turns * chunks)

    def piece(layer, i, k, w):
        return MODS[:, layer, KD * i + k, w:w + 1]

    def act_squares(items, n):
        j = 0
        for src, _, _, _, _, _, r in items:
            for x in src:
                w = x.shape[-1]
                last = act_.activation(WORK[0:r, j * T:j * T + w], x, ACT.Square)
                j += 1
        last.then_inc(sig("squared").sem, 1)

    def pe_sums(pe, items, n):
        pe.wait_ge(sig("squared").sem, sig("squared").at(n + 1))
        j = 0
        for src, _, _, total, ones, _, r in items:
            w = src[0].shape[-1]
            for i in range(len(src)):
                last = pe_.matmul(total, ones[0:r, 0:r], WORK[0:r, j * T:j * T + w],
                                  start=i == 0, stop=i == len(src) - 1)
                j += 1
        last.then_inc(sig("summed").sem, 1)

    def act_roots(act, items, n):
        act.wait_ge(sig("summed").sem, sig("summed").at(n + 1))
        for j, (src, _, _, total, _, width, r) in enumerate(items):
            w = src[0].shape[-1]
            last = act_.activation(ROOT[0:r, j, 0:w], total, ACT.Sqrt, bias=con("eps")[0:r], scale=1.0 / width)
        last.then_inc(sig("rooted").sem, 1)

    def dve_norms(dve, items, n):
        dve.wait_ge(sig("rooted").sem, sig("rooted").at(n + 1))
        for j, (src, *_, r) in enumerate(items):
            w = src[0].shape[-1]
            last = dve_.reciprocal(ROOT[0:r, j, 0:w], ROOT[0:r, j, 0:w])
        last.then_inc(sig("inverted").sem, 1)
        dve.wait_ge(sig("inverted").sem, sig("inverted").at(n + 1))
        for j, (src, dst, gains, _, _, _, r) in enumerate(items):
            w = src[0].shape[-1]
            for x, y, g in zip(src, dst, gains):
                last = dve_.scalar_tensor_tensor(out=y, in0=x, scalar=g[0:r], in1=ROOT[0:r, j, 0:w],
                                                 op0=ALU.mult, op1=ALU.mult)
        last.then_inc(sig("normed").sem, 1)

    def pe_turns(pe, items, norm, n):
        pe.wait_ge(sig("normed").sem, sig("normed").at(norm + 1))
        for x, y, r in items:
            last = pe_.matmul(y, TURN[0:r, 0:r], x, start=True, stop=True)
        last.then_inc(sig("rotated").sem, 1)

    def dve_ropes(dve, chain, items, n):
        dve.wait_ge(sig("rotated").sem, sig("rotated").at(n + 1))
        for j, (x, y, r) in enumerate(items):
            dve_.tensor_tensor(SIL[0:r, j, :], y, SIN[0:r], ALU.mult)
            last = dve_.tensor_tensor(x, x, COS[0:r], ALU.mult)
        chain(last)
        for j, (x, y, r) in enumerate(items):
            last = dve_.tensor_tensor(x, x, SIL[0:r, j, :], ALU.add)
        last.then_inc(sig("roped").sem, 1)

    def modulated_norm(gain, layer, shift, scale, t):
        items = [([X[:, k, 0:t] for k in range(KD)], None, None, PB[:, 0, 0:t], ONES, D, P)]
        streams = t // S
        with nc.Block() as block:
            @block.scalar
            def _(act):
                act_squares(items, 0)
                act_roots(act, items, 0)
                for w in range(1, streams):
                    for k in range(KD):
                        act.wait_ge(sig("spread").sem, sig("spread").at(k + 1))
                        act_.activation(A[:, k, half(w)], A[:, k, half(w)], ACT.Identity,
                                        bias=piece(layer, shift, k, w), scale=GAIN[:, w, k:k + 1])

            @block.tensor
            def _(pe):
                pe_sums(pe, items, 0)

            @block.vector
            def _(dve):
                chain = Chain(dve, sig("dve_step"))
                for w in range(2):
                    last = dve_.scalar_tensor_tensor(
                        out=GAIN[:, w, :], in0=MODS[:, layer, KD * scale:KD * scale + KD, w], scalar=1.0, in1=gain,
                        op0=ALU.add, op1=ALU.mult)
                chain(last)
                dve.wait_ge(sig("rooted").sem, sig("rooted").at(1))
                chain(dve_.reciprocal(ROOT[:, 0, 0:t], ROOT[:, 0, 0:t]))
                for k in range(KD):
                    last = dve_.tensor_tensor(A[:, k, 0:t], X[:, k, 0:t], ROOT[:, 0, 0:t], ALU.mult)
                    last.then_inc(sig("spread").sem, 1)
                dve.wait_ge(sig("spread").sem, sig("spread").at(KD))
                for k in range(KD):
                    last = dve_.tensor_scalar(A[:, k, half(0)], A[:, k, half(0)], GAIN[:, 0, k:k + 1],
                                              piece(layer, shift, k, 0), ALU.mult, ALU.add)
                last.then_inc(sig("normed").sem, 1)
        passed(squared=1, summed=1, rooted=1, dve_step=2, spread=KD, normed=1)

    def add_product(w, nk, src, layer, gate, t):
        n = nk // 2
        pairs = (n - 2) // 2
        cut = w.rearrange("(n k p) c -> n p k c", k=2, p=P)
        tail = list(range(1 + 2 * pairs, n))
        with nc.Block() as block:
            @block.sync
            def _(sp):
                def load(s, i, turn):
                    sp.wait_ge(used[s].sem, used[s].at(turn))
                    sp.dma_start(tile(s, 2, D), cut[i]).then_inc(loaded[s].sem, 16)
                load(0, 0, 0)
                with sp.Fori(0, pairs) as i:
                    for j in range(2):
                        load((1 + j) % 2, 2 * i + 1 + j, i + (1 + j) // 2)
                for i in tail:
                    load(i % 2, i, i // 2)

            @block.tensor
            def _(pe):
                def multiply(s, i, turn, first, final):
                    pe.wait_ge(loaded[s].sem, loaded[s].at(16 * (turn + 1)))
                    for r in range(2):
                        for m in range(KD):
                            last = pe_.matmul(PB[:, m, 0:t], tile(s, 2, D)[:, r, m * P:(m + 1) * P],
                                              src(2 * i + r), start=first and r == 0, stop=final and r == 1)
                    last.then_inc(used[s].sem, 1)
                multiply(0, 0, 0, True, False)
                with pe.Fori(0, pairs) as i:
                    for j in range(2):
                        multiply((1 + j) % 2, 2 * i + 1 + j, i + (1 + j) // 2, False, False)
                for i in tail:
                    multiply(i % 2, i, i // 2, False, i == n - 1)

            @block.vector
            def _(dve):
                s = (n - 1) % 2
                dve.wait_ge(used[s].sem, used[s].at((n - 1) // 2 + 1))
                for m in range(KD):
                    for c in range(t // S):
                        last = dve_.scalar_tensor_tensor(
                            out=X[:, m, half(c)], in0=PB[:, m, half(c)], scalar=piece(layer, gate, m, c),
                            in1=X[:, m, half(c)], op0=ALU.mult, op1=ALU.add)
                last.then_inc(sig("added").sem, 1)
        for s in range(2):
            count = (n + 1 - s) // 2
            used[s].passed(count)
            loaded[s].passed(16 * count)
        passed(added=1)

    def feed_forward(w1, w3, w2, layer, t):
        hidden = BIG[:, 0:FB * T].rearrange("p (n t) -> p n t", t=T)
        turns = FB // 2
        with nc.Block() as block:
            @block.sync
            def _(sp):
                cuts = [w.rearrange("(k p) (n c) -> p n k c", p=P, c=P) for w in (w1, w3)]
                with sp.Fori(0, turns) as i:
                    for s in range(2):
                        sp.wait_ge(used[s].sem, used[s].at(i))
                        for j, cut in enumerate(cuts):
                            sp.dma_start(tile(s, KD, P, j * KD * P), cut[:, 2 * i + s]).then_inc(loaded[s].sem, 16)

            @block.tensor
            def _(pe):
                with pe.Fori(0, turns) as i:
                    for s in range(2):
                        pe.wait_ge(loaded[s].sem, loaded[s].at(32 * (i + 1)))
                        pe.wait_ge(sig("h_made").sem, sig("h_made").at(2 * i + s - 1))
                        for j in range(2):
                            for k in range(KD):
                                last = pe_.matmul(PB[:, 2 * s + j, 0:t], tile(s, KD, P, j * KD * P)[:, k, :],
                                                  A[:, k, 0:t], start=k == 0, stop=k == KD - 1)
                        last.then_inc(used[s].sem, 1)

            @block.scalar
            def _(act):
                with act.Fori(0, turns) as i:
                    for s in range(2):
                        act.wait_ge(used[s].sem, used[s].at(i + 1))
                        act.wait_ge(sig("h_made").sem, sig("h_made").at(2 * i + s - 1))
                        act_.activation(SIL[:, s, 0:t], PB[:, 2 * s, 0:t], ACT.Silu).then_inc(sig("silu_made").sem, 1)

            @block.vector
            def _(dve):
                with dve.Fori(0, turns) as i:
                    for s in range(2):
                        dve.wait_ge(sig("silu_made").sem, sig("silu_made").at(2 * i + s + 1))
                        dve_.tensor_tensor(hidden[:, 2 * i + s, 0:t], PB[:, 2 * s + 1, 0:t], SIL[:, s, 0:t],
                                           ALU.mult).then_inc(sig("h_made").sem, 1)
        for s in range(2):
            used[s].passed(turns)
            loaded[s].passed(32 * turns)
        passed(silu_made=FB, h_made=FB)
        add_product(w2, FB, lambda i: hidden[:, i, 0:t], layer, 5, t)

    def store_streams(x):
        with nc.Block() as block:
            @block.sync
            def _(sp):
                sp.dma_start(out.rearrange("(k p) t -> p k t", p=P), x).then_inc(sig("stored").sem, 16)
                sp.wait_ge(sig("stored").sem, sig("stored").at(16))
        passed(stored=16)

    PR = WORK[:, 0:NT * T].rearrange("p (a b) -> p a b", a=NT)
    PT = WORK[:, NT * T:2 * NT * T].rearrange("p (a b) -> p a b", a=NT)
    OT = BIG[:, 0:KD * T].rearrange("p (k t) -> p k t", t=T)
    OWN = BIG[:, KD * T:FB * T]
    PEAK, SHARE = SMALL[:, 0:8], SMALL[:, 8:16]

    def own(at, k, n=T):
        a = OWN[:, at:at + k * n]
        return a if k == 1 else a.rearrange("p (k n) -> p k n", k=k)

    def first_key(t):
        return 0 if t < 2 else S

    def pe_attend(pe, n, tiles, pairs, values, r):
        for t in range(tiles):
            k0 = first_key(t)
            for j, (q, k) in enumerate(pairs):
                last = pe_.matmul(PB[:, t, k0:T], q[:, t * P:(t + 1) * P], k[:, k0:T],
                                  start=j == 0, stop=j == len(pairs) - 1)
        last.then_inc(sig("scored").sem, 1)
        pe.wait_ge(sig("shared").sem, sig("shared").at(n + 1))
        for kt in range(NT):
            for t in range(tiles):
                if kt * P >= first_key(t):
                    last = pe_.transpose(PB[:, 4 + kt, t * P:(t + 1) * P], PR[:, t, kt * P:(kt + 1) * P], IDENT)
        last.then_inc(sig("flipped").sem, 1)
        pe.wait_ge(sig("turned").sem, sig("turned").at(n + 1))
        for w in range(tiles // 2):
            kts = range(2 * w, NT)
            for kt in kts:
                last = pe_.matmul(PB[r, 0, half(w)], values(kt), PT[:, kt, half(w)],
                                  start=kt == kts[0], stop=kt == NT - 1)
        last.then_inc(sig("weighted").sem, 1)

    def dve_attend(dve, chain, n, tiles, scale, scores):
        for t in range(tiles):
            last = dve_.tensor_reduce(PEAK[:, t:t + 1], scores(t), AX.X, ALU.max, negate=True)
        chain(last)
        dve_.tensor_scalar(PEAK[:, 4:4 + tiles], PEAK[:, 0:tiles], scale, None, ALU.mult) \
            .then_inc(sig("peaked").sem, 1)
        dve.wait_ge(sig("exped").sem, sig("exped").at(n + 1))
        chain(dve_.reciprocal(SHARE[:, 4:4 + tiles], SHARE[:, 0:tiles]))
        for t in range(tiles):
            k0 = first_key(t)
            last = dve_.tensor_scalar(PR[:, t, k0:T], PR[:, t, k0:T], SHARE[:, 4 + t:5 + t], None, ALU.mult)
        last.then_inc(sig("shared").sem, 1)

    def act_attend(act, n, tiles, scale, scores, r, dst):
        act.wait_ge(sig("peaked").sem, sig("peaked").at(n + 1))
        for t in range(tiles):
            last = act_.activation(PR[:, t, first_key(t):T], scores(t), ACT.Exp, bias=PEAK[:, 4 + t:5 + t],
                                   scale=scale, accum_out=SHARE[:, t:t + 1])
        last.then_inc(sig("exped").sem, 1)
        act.wait_ge(sig("flipped").sem, sig("flipped").at(n + 1))
        for kt in range(NT):
            w = S if kt < 2 else tiles * P
            last = act_.activation(PT[:, kt, 0:w], PB[:, 4 + kt, 0:w], ACT.Copy)
        last.then_inc(sig("turned").sem, 1)
        act.wait_ge(sig("weighted").sem, sig("weighted").at(n + 1))
        act_.activation(dst, PB[r, 0, 0:tiles * P], ACT.Copy).then_inc(sig("carried").sem, 1)

    ATTEND = ("scored", "peaked", "exped", "shared", "flipped", "turned", "weighted", "carried")

    def psum_scores(t):
        return PB[:, t, first_key(t):T]

    def mla(gate_layer):
        CQ, CKV = own(0, 3), own(3 * T, 2)
        KRT, QN, KN, QRT, VB = own(5 * T, 1), own(6 * T, 1), own(7 * T, 1), own(8 * T, 1), own(9 * T, NT, P)
        w_in, w_uq, w_ukv = io["mla_w_in"][0], io["mla_w_uq"][0], io["mla_w_ukv"][0]
        widths = [S, S, MLA_IN - 2 * S]
        dims, scale = P + ROPE, 1.0 / math.sqrt(P + ROPE)
        all_rows = slice(0, P)
        latents = [([PB[:, i, :] for i in range(3)], [CQ[:, i, :] for i in range(3)],
                    [vec("mla_q", i, i + 1) for i in range(3)], PB[:, 6, :], ONES, QR, P),
                   ([PB[:, 3 + i, :] for i in range(2)], [CKV[:, i, :] for i in range(2)],
                    [vec("mla_kv", i, i + 1) for i in range(2)], PB[:, 7, :], ONES, KVR, P)]
        rotary = [([PB[0:ROPE, 5, :]], [KRT[0:ROPE]], [vec("mla_kr")], PB[0:ROPE, 6, :], ONES, ROPE, ROPE)]
        turned_key = [(KRT[0:ROPE], PB[0:ROPE, 7, :], ROPE)]
        head = [([PB[:, 0, :]], [QN], [vec("mla_qn")], PB[:, 4, :], ONES, P, P),
                ([PB[0:ROPE, 1, :]], [QRT[0:ROPE]], [vec("mla_qr")], PB[0:ROPE, 5, :], ONES, ROPE, ROPE),
                ([PB[:, 2, :]], [KN], [vec("mla_kn")], PB[:, 6, :], ONES, P, P)]
        turned_query = [(QRT[0:ROPE], PB[0:ROPE, 7, :], ROPE)]
        query_full = [(QRT, PB[:, 7, :], P)]
        each = 3
        with nc.Block() as block:
            @block.gpsimd
            def _(pool):
                nc.gpsimd.memset(QRT[ROPE:P], 0.0).then_inc(sig("cleared").sem, 1)

            @block.sync
            def _(sp):
                for s in range(3):
                    sp.dma_start(tile(s, KD, widths[s]), rows(w_in, s * S, s * S + widths[s])) \
                        .then_inc(loaded[s].sem, 16)
                cq = w_uq.rearrange("(k p) (h n) -> p h k n", p=P, n=dims)
                ckv = w_ukv.rearrange("(k p) (h n) -> p h k n", p=P, n=2 * P)
                with sp.Fori(0, HEADS) as h:
                    sp.wait_ge(used[0].sem, used[0].at(h + 1))
                    sp.dma_start(tile(0, 3, dims), cq[:, h]).then_inc(loaded[0].sem, 16)
                    sp.dma_start(tile(0, 2, 2 * P, 3 * dims), ckv[:, h]).then_inc(loaded[0].sem, 16)

            @block.tensor
            def _(pe):
                for m in range(6):
                    s, c = m // 2, (m % 2) * P
                    n = min(P, MLA_IN - m * P)
                    pe.wait_ge(loaded[s].sem, loaded[s].at(16))
                    w = tile(s, KD, widths[s])
                    for k in range(KD):
                        last = pe_.matmul(PB[0:n, m, :], w[:, k, c:c + n], A[:, k, :], start=k == 0, stop=k == KD - 1)
                    if m % 2:
                        last.then_inc(used[s].sem, 1)
                pe_sums(pe, latents, 0)
                pe.wait_ge(sig("normed").sem, sig("normed").at(1))
                pe_sums(pe, rotary, 1)
                pe_turns(pe, turned_key, 1, 0)
                pe.wait_ge(sig("roped").sem, sig("roped").at(1))
                pe.wait_ge(sig("cleared").sem, sig("cleared").at(1))
                with pe.Fori(0, HEADS) as h:
                    pe.wait_ge(loaded[0].sem, loaded[0].at(32 * h + 48))
                    pe.wait_ge(sig("carried").sem, sig("carried").at(h))
                    wq, wkv = tile(0, 3, dims), tile(0, 2, 2 * P, 3 * dims)
                    for bank, a, b in ((0, 0, P), (1, P, dims)):
                        for k in range(3):
                            pe_.matmul(PB[0:b - a, bank, :], wq[:, k, a:b], CQ[:, k, :], start=k == 0, stop=k == 2)
                    for k in range(2):
                        pe_.matmul(PB[:, 2, :], wkv[:, k, 0:P], CKV[:, k, :], start=k == 0, stop=k == 1)
                    for t in range(NT):
                        for k in range(2):
                            last = pe_.matmul(PB[:, 3, t * P:(t + 1) * P], CKV[:, k, t * P:(t + 1) * P],
                                              wkv[:, k, P:2 * P], start=k == 0, stop=k == 1)
                    last.then_inc(used[0].sem, 1)
                    pe_sums(pe, head, h + 2)
                    pe_turns(pe, query_full, h + 2, h + 1)
                    pe.wait_ge(sig("roped").sem, sig("roped").at(h + 2))
                    pe_attend(pe, h, NT, [(QN, KN), (QRT[0:ROPE], KRT[0:ROPE])], lambda kt: VB[:, kt, :], all_rows)

            @block.scalar
            def _(act):
                for s in range(3):
                    act.wait_ge(used[s].sem, used[s].at(1))
                act_squares(latents, 0)
                act_roots(act, latents, 0)
                act.wait_ge(sig("normed").sem, sig("normed").at(1))
                act_squares(rotary, 1)
                act_roots(act, rotary, 1)
                with act.Fori(0, HEADS) as h:
                    act.wait_ge(used[0].sem, used[0].at(h + 2))
                    act_.activation(VB.rearrange("p a b -> p (a b)"), PB[:, 3, :], ACT.Copy)
                    act_squares(head, 2)
                    act_roots(act, head, h + 2)
                    act_attend(act, h, NT, scale, psum_scores, all_rows, OT[:, h, :])

            @block.vector
            def _(dve):
                chain = Chain(dve, sig("dve_step"))
                dve_norms(dve, latents, 0)
                dve_norms(dve, rotary, 1)
                dve_ropes(dve, chain, turned_key, 0)
                assert chain.n == 1
                with dve.Fori(0, HEADS) as h:
                    turn = Chain(dve, sig("dve_step"), h, each)
                    turn.n = 1
                    dve_norms(dve, head, h + 2)
                    dve_ropes(dve, turn, turned_query, h + 1)
                    dve.wait_ge(sig("scored").sem, sig("scored").at(h + 1))
                    dve_attend(dve, turn, h, NT, scale, psum_scores)
                    assert turn.n == 1 + each
        for s in range(3):
            n = 1 + HEADS * (s == 0)
            used[s].passed(n)
            loaded[s].passed(16 + 32 * HEADS * (s == 0))
        passed(cleared=1, squared=HEADS + 2, summed=HEADS + 2, rooted=HEADS + 2, inverted=HEADS + 2, normed=HEADS + 2, rotated=HEADS + 1,
               roped=HEADS + 1, dve_step=1 + each * HEADS, **{n: HEADS for n in ATTEND})
        add_product(io["mla_w_o"][0], KD, lambda i: OT[:, i, :], gate_layer, 2, T)

    def even_mixer(layer):
        KG, VB, QP, U = own(0, 2), own(2 * T, NT, P), own(3 * T, 2), own(5 * T, NT)
        w_in = io["even_w_in_2"][0]
        scale = float(HD) ** -0.5
        keys = [([PB[:, g, :]], [KG[:, g, :]], [vec("a_k")], PB[:, 4 + g, :], PAIR, HD, P) for g in range(2)]
        turned_keys = [(KG[:, g, :], PB[:, 6 + g, :], P) for g in range(2)]
        queries = [([PB[:, j, :]], [QP[:, j, :]], [vec("a_q")], PB[:, 4 + j, :], PAIR, HD, P) for j in range(2)]
        turned_queries = [(QP[:, j, :], PB[:, 6 + j, :], P) for j in range(2)]
        MIX = own(0, 2)
        pool_w = SIL[:].rearrange("p a b -> p (a b)")[:, 0:4 * P].rearrange("p (g n) -> p g n", g=4)
        pools = con("pools").rearrange("p (g a t) -> p g a t", g=4, a=2)
        with nc.Block() as block:
            @block.sync
            def _(sp):
                for s, c in ((1, 2 * S), (2, 3 * S), (3, 4 * S)):
                    sp.dma_start(tile(s, KD, S), rows(w_in, c, c + S)).then_inc(loaded[s].sem, 16)
                for g in range(2):
                    sp.wait_ge(used[0].sem, used[0].at(g))
                    sp.dma_start(tile(0, KD, S), rows(w_in, g * S, (g + 1) * S)).then_inc(loaded[0].sem, 16)
                sp.wait_ge(sig("roped").sem, sig("roped").at(3))
                sp.dma_start(pool_w, io["pool_w_2"][0].rearrange("g c d -> c g d")).then_inc(sig("bias_in").sem, 16)

            @block.tensor
            def _(pe):
                pe.wait_ge(loaded[1].sem, loaded[1].at(16))
                w = tile(1, KD, S)
                for g in range(2):
                    for j in range(2):
                        for k in range(KD):
                            pe_.matmul(PB[j * HD:(j + 1) * HD, g, :], w[:, k, g * HD:(g + 1) * HD], A[:, k, :],
                                       start=k == 0, stop=k == KD - 1)
                for t in range(NT):
                    for k in range(KD):
                        last = pe_.matmul(PB[:, 2, t * P:(t + 1) * P], A[:, k, t * P:(t + 1) * P], w[:, k, P:2 * P],
                                          start=k == 0, stop=k == KD - 1)
                last.then_inc(used[1].sem, 1)
                pe_sums(pe, keys, 0)
                pe_turns(pe, turned_keys, 0, 0)
                pe.wait_ge(sig("roped").sem, sig("roped").at(1))
                for s in (2, 3):
                    pe.wait_ge(loaded[s].sem, loaded[s].at(16))
                    for t in range(NT):
                        for k in range(KD):
                            last = pe_.matmul(PB[:, 2 * s - 4 + t // 2, (t % 2) * S:(t % 2 + 1) * S],
                                              A[:, k, t * P:(t + 1) * P], tile(s, KD, S)[:, k, :],
                                              start=k == 0, stop=k == KD - 1)
                    last.then_inc(used[s].sem, 1)
                pe.wait_ge(sig("drained").sem, sig("drained").at(2))
                for g in range(2):
                    pe.wait_ge(loaded[0].sem, loaded[0].at(16 * (g + 1)))
                    if g:
                        pe.wait_ge(sig("carried").sem, sig("carried").at(4 * g))
                    for j in range(2):
                        for k in range(KD):
                            last = pe_.matmul(PB[:, j, :], tile(0, KD, S)[:, k, j * P:(j + 1) * P], A[:, k, :],
                                              start=k == 0, stop=k == KD - 1)
                    last.then_inc(used[0].sem, 1)
                    pe_sums(pe, queries, g + 1)
                    pe_turns(pe, turned_queries, g + 1, g + 1)
                    pe.wait_ge(sig("roped").sem, sig("roped").at(g + 2))
                    for j in range(2):
                        for i in range(2):
                            n = 4 * g + 2 * j + i
                            r = slice(i * HD, (i + 1) * HD)
                            if n:
                                pe.wait_ge(sig("carried").sem, sig("carried").at(n))
                            pe_attend(pe, n, NT, [(QP[r, j, :], KG[r, g, :])],
                                      lambda kt: VB[:, kt, g * HD:(g + 1) * HD], r)
                pe.wait_ge(sig("carried").sem, sig("carried").at(8))
                pe.wait_ge(sig("bias_in").sem, sig("bias_in").at(16))
                for g in range(4):
                    if g >= 2:
                        pe.wait_ge(sig("mixed").sem, sig("mixed").at(g - 1))
                    for w in range(2):
                        for a in range(2):
                            last = pe_.matmul(PB[:, g % 2, half(w)], U[:, 2 * w + a, g * P:(g + 1) * P],
                                              pools[:, g, a, :], start=a == 0, stop=a == 1)
                    last.then_inc(sig("pooled").sem, 1)
                    pe.wait_ge(sig("pool_copied").sem, sig("pool_copied").at(g + 1))
                    pe_.matmul(PB[:, 2 + g % 2, :], pool_w[:, g, :], MIX[:, g % 2, :], start=True, stop=True) \
                        .then_inc(sig("projected").sem, 1)

            @block.scalar
            def _(act):
                act.wait_ge(used[1].sem, used[1].at(1))
                act_.activation(VB.rearrange("p a b -> p (a b)"), PB[:, 2, :], ACT.Copy)
                act_squares(keys, 0)
                act_roots(act, keys, 0)
                for s in (2, 3):
                    act.wait_ge(used[s].sem, used[s].at(1))
                    act_.activation(U[:, :, (s - 2) * S:(s - 1) * S],
                                    PB[:, 2 * s - 4:2 * s - 2, :].rearrange("p a (b c) -> p (a b) c", b=2),
                                    ACT.Copy).then_inc(sig("drained").sem, 1)
                for g in range(2):
                    act.wait_ge(used[0].sem, used[0].at(g + 1))
                    act_squares(queries, g + 1)
                    act_roots(act, queries, g + 1)
                    for j in range(2):
                        for i in range(2):
                            r = slice(i * HD, (i + 1) * HD)
                            act_attend(act, 4 * g + 2 * j + i, NT, scale, psum_scores, r, OT[r, 2 * g + j, :])
                for g in range(4):
                    act.wait_ge(sig("pooled").sem, sig("pooled").at(g + 1))
                    act_.activation(MIX[:, g % 2, :], PB[:, g % 2, :], ACT.Copy).then_inc(sig("pool_copied").sem, 1)
                    act.wait_ge(sig("projected").sem, sig("projected").at(g + 1))
                    act_.activation(OT[:, 4 + g, :], PB[:, 2 + g % 2, :], ACT.Copy, scale=vec("pool", g, g + 1)) \
                        .then_inc(sig("mixed").sem, 1)

            @block.vector
            def _(dve):
                chain = Chain(dve, sig("dve_step"))
                dve_norms(dve, keys, 0)
                dve_ropes(dve, chain, turned_keys, 0)
                for g in range(2):
                    dve_norms(dve, queries, g + 1)
                    dve_ropes(dve, chain, turned_queries, g + 1)
                    for n in range(4 * g, 4 * g + 4):
                        dve.wait_ge(sig("scored").sem, sig("scored").at(n + 1))
                        dve_attend(dve, chain, n, NT, scale, psum_scores)
        used[0].passed(2)
        loaded[0].passed(32)
        for s in (1, 2, 3):
            used[s].passed(1)
            loaded[s].passed(16)
        passed(squared=3, summed=3, rooted=3, inverted=3, normed=3, rotated=3, roped=3, drained=2, bias_in=16, pooled=4,
               pool_copied=4, projected=4, mixed=4, dve_step=3 + 2 * 8, **{n: 8 for n in ATTEND})
        add_product(io["even_w_out_2"][0], KD, lambda i: OT[:, i, :], layer, 2, T)

    def odd_mixer(layer):
        QB, KB, VB, SC, BI = own(0, 1, S), own(S, 1), own(S + T, NT, P), own(S + 2 * T, 2), own(S + 4 * T, 4)
        w_in = io["odd_w_in_2"][0]
        scale = float(HD) ** -0.5
        parts = [w_in[:, i * D:(i + 1) * D].rearrange("(k p) (m n) -> p m k n", p=P, n=P) for i in range(3)]
        bias = io["bias"].rearrange("(m h) q k -> q m h k", h=4)
        near = con("near")
        each = 4
        with nc.Block() as block:
            @block.sync
            def _(sp):
                with sp.Fori(0, KD) as m:
                    sp.wait_ge(used[0].sem, used[0].at(m))
                    for j in range(2):
                        sp.dma_start(tile(0, KD, P, j * D), parts[j][:, m]).then_inc(loaded[0].sem, 16)
                    sp.wait_ge(used[1].sem, used[1].at(m))
                    sp.dma_start(tile(1, KD, P), parts[2][:, m]).then_inc(loaded[1].sem, 16)
                    sp.wait_ge(sig("biased").sem, sig("biased").at(2 * m))
                    sp.dma_start(BI[:, :, 0:S], bias[:, m]).then_inc(sig("bias_in").sem, 16)

            @block.tensor
            def _(pe):
                with pe.Fori(0, KD) as m:
                    pe.wait_ge(sig("carried").sem, sig("carried").at(2 * m))
                    pe.wait_ge(loaded[0].sem, loaded[0].at(32 * (m + 1)))
                    for k in range(KD):
                        pe_.matmul(PB[:, 4, 0:S], tile(0, KD, P)[:, k, :], A[:, k, 0:S], start=k == 0, stop=k == KD - 1)
                    for k in range(KD):
                        last = pe_.matmul(PB[:, 5, :], tile(0, KD, P, D)[:, k, :], A[:, k, :],
                                          start=k == 0, stop=k == KD - 1)
                    last.then_inc(used[0].sem, 1)
                    pe.wait_ge(loaded[1].sem, loaded[1].at(16 * (m + 1)))
                    for t in range(NT):
                        for k in range(KD):
                            last = pe_.matmul(PB[:, 6, t * P:(t + 1) * P], A[:, k, t * P:(t + 1) * P],
                                              tile(1, KD, P)[:, k, :], start=k == 0, stop=k == KD - 1)
                    last.then_inc(used[1].sem, 1)
                    pe.wait_ge(sig("staged").sem, sig("staged").at(m + 1))
                    for i in range(2):
                        r = slice(i * HD, (i + 1) * HD)
                        if i:
                            pe.wait_ge(sig("carried").sem, sig("carried").at(2 * m + 1))
                        pe_attend(pe, 2 * m + i, 2, [(QB[r], KB[r])], lambda kt: VB[:, kt, r], r)

            @block.scalar
            def _(act):
                with act.Fori(0, KD) as m:
                    act.wait_ge(used[0].sem, used[0].at(m + 1))
                    act_.activation(QB, PB[:, 4, 0:S], ACT.Copy)
                    act_.activation(KB, PB[:, 5, :], ACT.Copy)
                    act.wait_ge(used[1].sem, used[1].at(m + 1))
                    act_.activation(VB.rearrange("p a b -> p (a b)"), PB[:, 6, :], ACT.Copy) \
                        .then_inc(sig("staged").sem, 1)
                    for i in range(2):
                        r = slice(i * HD, (i + 1) * HD)
                        act_attend(act, 2 * m + i, 2, 1.0, lambda t: SC[:, t, :], r, OT[r, m, 0:S])

            @block.vector
            def _(dve):
                with dve.Fori(0, KD) as m:
                    chain = Chain(dve, sig("dve_step"), m, each)
                    dve.wait_ge(sig("bias_in").sem, sig("bias_in").at(16 * (m + 1)))
                    for i in range(2):
                        n = 2 * m + i
                        for t in range(2):
                            last = dve_.tensor_tensor(BI[:, 2 * i + t, 0:S], BI[:, 2 * i + t, 0:S], near, ALU.add)
                        last.then_inc(sig("act_step").sem, 1)
                        dve.wait_ge(sig("act_step").sem, sig("act_step").at(n + 1))
                        dve.wait_ge(sig("scored").sem, sig("scored").at(n + 1))
                        for t in range(2):
                            dve_.scalar_tensor_tensor(out=SC[:, t, 0:S], in0=PB[:, t, 0:S], scalar=scale,
                                                      in1=BI[:, 2 * i + t, 0:S], op0=ALU.mult, op1=ALU.add)
                            last = dve_.tensor_scalar(SC[:, t, S:T], PB[:, t, S:T], scale, None, ALU.mult)
                        last.then_inc(sig("biased").sem, 1)
                        dve.wait_ge(sig("biased").sem, sig("biased").at(n + 1))
                        dve_attend(dve, chain, n, 2, 1.0, lambda t: SC[:, t, :])
                    assert chain.n == each
        used[0].passed(KD)
        used[1].passed(KD)
        loaded[0].passed(32 * KD)
        loaded[1].passed(16 * KD)
        passed(biased=2 * KD, bias_in=16 * KD, staged=KD, act_step=2 * KD, dve_step=each * KD,
               **{n: 2 * KD for n in ATTEND})
        add_product(io["odd_w_out_2"][0], KD, lambda i: OT[:, i, 0:S], layer, 2, S)

    def hgrn2(layer):
        OTH = BIG[:, 0:KD * S].rearrange("p (k t) -> p k t", t=S)
        at = [KD * S]

        def take(k, n):
            a = BIG[:, at[0]:at[0] + k * n]
            at[0] += k * n
            return a if k == 1 else a.rearrange("p (k n) -> p k n", k=k)

        QS, SG, VB, KK, LF, CUM, EX = (take(1, S), take(1, S), take(NT, P), take(2, T), take(2, T), take(1, T),
                                       take(1, T))
        KX, KXT, ST, QI, KE, MP = take(1, S), take(2, P), take(2, P), take(2, S), take(LEVELS, S), take(1, 2 * T)
        LV = WORK[:, 0:LEVELS * S].rearrange("p (l t) -> p l t", l=LEVELS)
        QE = WORK[:, LEVELS * S:2 * LEVELS * S].rearrange("p (l t) -> p l t", l=LEVELS)
        AT = SIL[:].rearrange("p d (a t) -> p d a t", a=2)
        LB = SMALL[:, 0:2 * KD].rearrange("p (d k) -> p d k", d=2)
        OLB = SMALL[:, 2 * KD:4 * KD].rearrange("p (d k) -> p d k", d=2)
        LBD = SMALL[:, 4 * KD:6 * KD]
        flat = "p a b -> p (a b)"
        masks = con("decay").rearrange("p (d m) -> p d m", d=2)
        w_in = io["hg_w_in"][0].rearrange("(k p) (i h n) -> p i h k n", p=P, i=5, n=P)
        read = [([PB[:, 6, 0:S]], [EX[:, 0:S]], [vec("hg_o")], PB[:, 7, 0:S], ONES, P, P)]
        lb = vec("hg_lb")
        each = 8
        with nc.Block() as block:
            @block.sync
            def _(sp):
                with sp.Fori(0, HEADS) as h:
                    for s, parts in ((0, (0, 1)), (1, (2, 3)), (2, (4,))):
                        sp.wait_ge(used[s].sem, used[s].at(h))
                        for j, i in enumerate(parts):
                            sp.dma_start(tile(s, KD, P, j * D), w_in[:, i, h]).then_inc(loaded[s].sem, 16)

            @block.tensor
            def _(pe):
                def by_feature(dst, w, t):
                    for k in range(KD):
                        last = pe_.matmul(dst, w[:, k, :], A[:, k, 0:t], start=k == 0, stop=k == KD - 1)
                    return last

                with pe.Fori(0, HEADS) as h:
                    pe.wait_ge(sig("read_out").sem, sig("read_out").at(h))
                    pe.wait_ge(loaded[0].sem, loaded[0].at(32 * (h + 1)))
                    by_feature(PB[:, 0, 0:S], tile(0, KD, P), S)
                    by_feature(PB[:, 1, :], tile(0, KD, P, D), T).then_inc(used[0].sem, 1)
                    pe.wait_ge(loaded[1].sem, loaded[1].at(32 * (h + 1)))
                    by_feature(PB[:, 2, :], tile(1, KD, P), T)
                    for t in range(NT):
                        for k in range(KD):
                            last = pe_.matmul(PB[:, 3, t * P:(t + 1) * P], A[:, k, t * P:(t + 1) * P],
                                              tile(1, KD, P, D)[:, k, :], start=k == 0, stop=k == KD - 1)
                    last.then_inc(used[1].sem, 1)
                    pe.wait_ge(loaded[2].sem, loaded[2].at(16 * (h + 1)))
                    by_feature(PB[:, 0, S:T], tile(2, KD, P), S).then_inc(used[2].sem, 1)
                    for d in range(2):
                        n = 2 * h + d
                        pe.wait_ge(sig("decayed").sem, sig("decayed").at(n + 1))
                        for a in range(2):
                            last = pe_.transpose(PB[:, 4, a * P:(a + 1) * P], KX[:, a * P:(a + 1) * P], IDENT)
                        last.then_inc(sig("kx_flipped").sem, 1)
                        pe.wait_ge(sig("kx_copied").sem, sig("kx_copied").at(n + 1))
                        for a in range(2):
                            last = pe_.matmul(PB[:, 4, S:S + P], KXT[:, a, :], VB[:, 2 + a, :], start=a == 0, stop=a == 1)
                        last.then_inc(sig("state_made").sem, 1)
                        pe.wait_ge(sig("levels_ready").sem, sig("levels_ready").at(n + 1))
                        for a in range(2):
                            c = slice(a * P, (a + 1) * P)
                            for l in range(LEVELS):
                                lhs, rhs = (KE[:, l + 1, c], QE[:, l + 1, c]) if l < LEVELS - 1 else (KK[:, d, c], QS[:, c])
                                pe_.matmul(PB[:, 2 * a + l // 4, (l % 4) * P:(l % 4 + 1) * P], lhs, rhs,
                                           start=True, stop=True)
                        early, late = slice(d * P, (d + 1) * P), slice((1 - d) * P, (2 - d) * P)
                        pe_.matmul(PB[:, 5, 0:P], KE[:, 0, early], QE[:, 0, late], start=True, stop=True) \
                            .then_inc(sig("products").sem, 1)
                        pe.wait_ge(sig("state_copied").sem, sig("state_copied").at(n + 1))
                        pe_.matmul(PB[:, 6, 0:S], ST[:, d, :], QI[:, d, :], start=d == 0, stop=False)
                        pe.wait_ge(sig("attended").sem, sig("attended").at(n + 1))
                        pe_.matmul(PB[:, 6, 0:S], VB[:, d, :], AT[:, d, d, :], start=False, stop=False)
                        o = slice((1 - d) * P, (2 - d) * P)
                        last = pe_.matmul(PB[:, 6, o], VB[:, 1 - d, :], AT[:, d, 1 - d, o], start=False, stop=d == 1)
                    last.then_inc(sig("summed_up").sem, 1)
                    pe_sums(pe, read, h)

            @block.scalar
            def _(act):
                act.wait_ge(sig("act_step").sem, sig("act_step").at(1))
                act_.activation(SMALL[:, 0:2 * KD], LBD, ACT.Sigmoid)
                act_.activation(SMALL[:, 2 * KD:4 * KD], LBD, ACT.Sigmoid, scale=-1.0).then_inc(sig("staged").sem, 1)
                with act.Fori(0, HEADS) as h:
                    act.wait_ge(used[2].sem, used[2].at(h + 1))
                    act_.activation(QS, PB[:, 0, 0:S], ACT.Copy)
                    act_.activation(VB.rearrange(flat), PB[:, 3, :], ACT.Copy)
                    act_.activation(SG, PB[:, 0, S:T], ACT.Silu)
                    z = PB[:, 1:3, :]
                    act_.activation(LF, z, ACT.Sigmoid)
                    act_.activation(KK, z, ACT.Sigmoid, scale=-1.0).then_inc(sig("gated").sem, 1)
                    act.wait_ge(sig("forgot").sem, sig("forgot").at(h + 1))
                    act_.activation(LF, LF, ACT.Ln).then_inc(sig("logged").sem, 1)
                    for d in range(2):
                        n = 2 * h + d
                        act.wait_ge(sig("spread").sem, sig("spread").at(n + 1))
                        sign = -1.0 if d == 0 else 1.0
                        lat = dict(scale=1.0) if d == 0 else dict(scale=-1.0, bias=ROOT[:, 1, 0:1])
                        ctx = dict(scale=-1.0, bias=ROOT[:, 1, 1:2]) if d == 0 else dict(scale=1.0)
                        act_.activation(EX[:, 0:S], CUM[:, 0:S], ACT.Exp, **lat)
                        act_.activation(EX[:, S:T], CUM[:, S:T], ACT.Exp, **ctx).then_inc(sig("exped").sem, 1)
                        act.wait_ge(sig("levelled").sem, sig("levelled").at(n + 1))
                        act_.activation(LV, LV, ACT.Abs).then_inc(sig("absed").sem, 1)
                        act.wait_ge(sig("absed").sem, sig("absed").at(n + 1))
                        act_.activation(LV, LV, ACT.Exp, scale=-1.0).then_inc(sig("group_exped").sem, 1)
                        act.wait_ge(sig("kx_flipped").sem, sig("kx_flipped").at(n + 1))
                        act_.activation(KXT.rearrange(flat), PB[:, 4, 0:S], ACT.Copy).then_inc(sig("kx_copied").sem, 1)
                        act.wait_ge(sig("state_made").sem, sig("state_made").at(n + 1))
                        act_.activation(ST[:, d, :], PB[:, 4, S:S + P], ACT.Copy).then_inc(sig("state_copied").sem, 1)
                    act.wait_ge(sig("summed_up").sem, sig("summed_up").at(h + 1))
                    act_squares(read, h)
                    act_roots(act, read, h)

            @block.vector
            def _(dve):
                dve_.tensor_tensor(LBD, lb[:, 2 * KD:4 * KD], lb[:, 0:2 * KD], ALU.subtract) \
                    .then_inc(sig("act_step").sem, 1)
                dve.wait_ge(sig("staged").sem, sig("staged").at(1))
                dve_.memset(ROOT[:, 2, :], 1.0).then_inc(sig("added").sem, 1)
                dve.wait_ge(sig("added").sem, sig("added").at(1))
                with dve.Fori(0, HEADS) as h:
                    chain = Chain(dve, sig("dve_step"), h, each)
                    dve.wait_ge(sig("gated").sem, sig("gated").at(h + 1))
                    for d in range(2):
                        dve_.tensor_scalar(LF[:, d, :], LF[:, d, :], OLB[:, d, bass.ds(h, 1)], LB[:, d, bass.ds(h, 1)],
                                           ALU.mult, ALU.add)
                        last = dve_.tensor_scalar(KK[:, d, :], KK[:, d, :], OLB[:, d, bass.ds(h, 1)], None, ALU.mult)
                    chain(last)
                    dve_.tensor_scalar(LF, LF, 1.0e-19, None, ALU.max).then_inc(sig("forgot").sem, 1)
                    dve.wait_ge(sig("logged").sem, sig("logged").at(h + 1))
                    for d in range(2):
                        n = 2 * h + d
                        for w in range(2):
                            last = dve_.tensor_tensor_scan(CUM[:, half(w)], ROOT[:, 2, 0:S], LF[:, d, half(w)], 0.0,
                                                           ALU.mult, ALU.add)
                        chain(last)
                        last = dve_.tensor_copy(ROOT[:, 1, 0:2], CUM.rearrange("p (w t) -> p w t", w=2)[:, :, S - 1])
                        if d == 1:
                            chain(last)
                            last = dve_.tensor_tensor(CUM, CUM, LF[:, 1, :], ALU.subtract)
                        last.then_inc(sig("spread").sem, 1)
                        dve.wait_ge(sig("spread").sem, sig("spread").at(n + 1))
                        for l in range(LEVELS):
                            w = P >> l
                            b = CUM[:, 0:S].rearrange("p (b w) -> p b w", w=2 * w)
                            mid = b[:, :, w - 1:w].broadcast_to([P, P // w, 2 * w])
                            last = dve_.tensor_tensor(LV[:, l, :].rearrange("p (b w) -> p b w", w=2 * w), b, mid,
                                                      ALU.subtract)
                        last.then_inc(sig("levelled").sem, 1)
                        dve.wait_ge(sig("exped").sem, sig("exped").at(n + 1))
                        dve_.tensor_tensor(KX, KK[:, d, S:T], EX[:, S:T], ALU.mult)
                        dve_.tensor_tensor(QI[:, d, :], QS, EX[:, 0:S], ALU.mult).then_inc(sig("decayed").sem, 1)
                        dve.wait_ge(sig("group_exped").sem, sig("group_exped").at(n + 1))
                        dve_.tensor_tensor(QE, LV, QS.unsqueeze(1).broadcast_to([P, LEVELS, S]), ALU.mult)
                        dve_.tensor_tensor(KE, LV, KK[:, d, 0:S].unsqueeze(1).broadcast_to([P, LEVELS, S]), ALU.mult) \
                            .then_inc(sig("levels_ready").sem, 1)
                        dve.wait_ge(sig("products").sem, sig("products").at(n + 1))
                        for a in range(2):
                            chain(dve_.tensor_tensor(MP, PB[:, 2 * a:2 * a + 2, :].rearrange(flat), masks[:, d, :],
                                                     ALU.mult))
                            last = dve_.tensor_reduce(AT[:, d, a, a * P:(a + 1) * P],
                                                      MP.rearrange("p (l t) -> p t l", l=LEVELS), AX.X, ALU.add)
                            if a == 0:
                                last.then_inc(sig("routed").sem, 1)
                                dve.wait_ge(sig("routed").sem, sig("routed").at(n + 1))
                        dve_.tensor_copy(AT[:, d, d, (1 - d) * P:(2 - d) * P], PB[:, 5, 0:P]) \
                            .then_inc(sig("attended").sem, 1)
                    dve_norms(dve, read, h)
                    dve.wait_ge(sig("normed").sem, sig("normed").at(h + 1))
                    dve_.tensor_tensor(OTH[:, h, :], EX[:, 0:S], SG, ALU.mult).then_inc(sig("read_out").sem, 1)
                    assert chain.n == each, chain.n
        for s in range(3):
            used[s].passed(HEADS)
            loaded[s].passed((32, 32, 16)[s] * HEADS)
        n = HEADS
        passed(read_out=n, decayed=2 * n, kx_flipped=2 * n, kx_copied=2 * n, state_made=2 * n, levels_ready=2 * n,
               products=2 * n, state_copied=2 * n, attended=2 * n, summed_up=n, summed=n, act_step=1, staged=1,
               gated=n, forgot=n, logged=n, spread=2 * n, exped=2 * n, levelled=2 * n, group_exped=2 * n, squared=n,
               rooted=n, inverted=n, added=1, normed=n, routed=2 * n, absed=2 * n, dve_step=n * each)
        add_product(io["hg_w_o"][0], KD, lambda i: OTH[:, i, :], layer, 2, S)

    def experts(layer, moe, t):
        nt, streams = t // P, t // S
        ATK = BIG[:, 0:NT * D].rearrange("p (a n) -> p a n", a=NT)
        o = NT * D

        def take(n):
            nonlocal o
            o += n
            assert o <= FB * T
            return BIG[:, o - n:o]

        XGS = take(D)
        XGT = take(2 * D).rearrange("p (b k c) -> p b k c", b=2, k=KD)
        HS = take(2 * DE).rearrange("p (j n) -> p j n", j=2)
        HB = take(8 * CAP).rearrange("p (j k c) -> p j k c", j=2, k=4)
        Y2 = take(D)
        SWT = take(T)
        SEL = WORK[:, 0:NT * P].rearrange("p (a c) -> p a c", a=NT)
        SELW = WORK[:, NT * P:2 * NT * P].rearrange("p (a c) -> p a c", a=NT)
        W36 = SIL[:].rearrange("p a b -> p (a b)")[:, 0:KD * NR].rearrange("p (k n) -> p k n", n=NR)
        free = [2 * NT * P]

        def small(*shape):
            n = int(np.prod(shape))
            a = WORK[:, free[0]:free[0] + n]
            free[0] += n
            if len(shape) == 2:
                return a.rearrange("p (a b) -> p a b", a=shape[0])
            if len(shape) == 3:
                return a.rearrange("p (a b c) -> p a b c", a=shape[0], b=shape[1])
            return a

        LG, GS, G1, GW = small(nt, NR), small(nt, NG), small(nt, NG), small(nt, 1)
        M1, M2, E2 = small(nt, 1), small(nt, 1), small(nt, 1)
        PI, LE, LE2, O1, O2 = small(nt, EPG), small(nt, EPG), small(nt, EPG), small(nt, EPG), small(nt, EPG)
        WIDE, MEM, WT, RK = small(nt, NG, EPG), small(nt, NG, EPG), small(nt, NG, EPG), small(nt, NE + 4)
        CNT, NRF = small(1), small(8)
        EXPO = small(nt, NG)

        router_steps = 34

        def wide(x, shape, axis):
            return x.unsqueeze(axis).broadcast_to([P] + shape)

        def across(x, n):
            return x.broadcast_to([P, nt, n])

        with nc.Block() as block:
            @block.sync
            def _(sp):
                sp.dma_start(W36, io["router"][moe].rearrange("(k p) n -> p k n", p=P)).then_inc(sig("bias_in").sem, 16)

            @block.tensor
            def _(pe):
                pe.wait_ge(sig("bias_in").sem, sig("bias_in").at(16))
                for a in range(nt):
                    for k in range(KD):
                        last = pe_.matmul(PB[:, 0, a * NR:(a + 1) * NR], A[:, k, a * P:(a + 1) * P], W36[:, k, :],
                                          start=k == 0, stop=k == KD - 1)
                last.then_inc(sig("projected").sem, 1)
                for a in range(nt):
                    if a >= 2:
                        pe.wait_ge(sig("token_copied").sem, sig("token_copied").at(a - 1))
                    for k in range(KD):
                        last = pe_.transpose(PB[:, 2 + 2 * (a % 2) + k // 4, (k % 4) * P:(k % 4 + 1) * P],
                                             A[:, k, a * P:(a + 1) * P], IDENT)
                    last.then_inc(sig("token_flipped").sem, 1)
                pe.wait_ge(sig("routed").sem, sig("routed").at(1))
                for a in range(nt):
                    for b in range(a + 1):
                        pe_.matmul(PB[:, 1, a * NE:(a + 1) * NE], TRI if b == a else ONES,
                                   MEM[:, b].rearrange("p a b -> p (a b)"), start=b == 0, stop=b == a)
                for b in range(nt):
                    last = pe_.matmul(PB[:, 1, NT * NE:(NT + 1) * NE], ONES, MEM[:, b].rearrange("p a b -> p (a b)"),
                                      start=b == 0, stop=b == nt - 1)
                last.then_inc(sig("ranked").sem, 1)

            @block.scalar
            def _(act):
                for a in range(nt):
                    act.wait_ge(sig("token_flipped").sem, sig("token_flipped").at(a + 1))
                    act_.activation(ATK[:, a, :], PB[:, 2 + 2 * (a % 2):4 + 2 * (a % 2), :].rearrange("p a b -> p (a b)"),
                                    ACT.Copy).then_inc(sig("token_copied").sem, 1)
                act.wait_ge(sig("peaked").sem, sig("peaked").at(1))
                act_.activation(EXPO, EXPO, ACT.Exp).then_inc(sig("group_exped").sem, 1)
                act.wait_ge(sig("picked").sem, sig("picked").at(1))
                act_.activation(E2, E2, ACT.Exp).then_inc(sig("second_exped").sem, 1)

            @block.vector
            def _(dve):
                c = Chain(dve, sig("dve_step"))
                dve.wait_ge(sig("projected").sem, sig("projected").at(1))
                bias = vec("moe_b", moe * NR, (moe + 1) * NR).unsqueeze(1).broadcast_to([P, nt, NR])
                c(dve_.tensor_tensor(LG, PB[:, 0, 0:nt * NR].rearrange("p (a n) -> p a n", a=nt), bias, ALU.add))
                G, L = LG[:, :, 0:NG], LG[:, :, NG:NR].rearrange("p a (g e) -> p a g e", g=NG)
                prior = con("prior").unsqueeze(1).broadcast_to([P, nt, EPG])

                def first_of(src, top, dst, n):
                    c(dve_.tensor_reduce(top, src, AX.X, ALU.max))
                    c(dve_.tensor_tensor(PI[:, :, 0:n], src, across(top, n), ALU.is_equal))
                    c(dve_.tensor_tensor(PI[:, :, 0:n], PI[:, :, 0:n], prior[:, :, 0:n], ALU.mult))
                    c(dve_.tensor_reduce(GS[:, :, 0:1], PI[:, :, 0:n], AX.X, ALU.max))
                    c(dve_.tensor_tensor(dst, PI[:, :, 0:n], across(GS[:, :, 0:1], n), ALU.is_equal))

                first_of(G, M1, G1, NG)
                dve_.tensor_tensor(EXPO, G, across(M1, NG), ALU.subtract).then_inc(sig("peaked").sem, 1)
                dve.wait_ge(sig("group_exped").sem, sig("group_exped").at(1))
                c(dve_.tensor_reduce(GW, EXPO, AX.X, ALU.add))
                c(dve_.reciprocal(GW, GW))
                full = [nt, NG, EPG]
                c(dve_.tensor_tensor(WIDE, L, wide(G1, full, 3), ALU.mult))
                c(dve_.tensor_reduce(LE, WIDE.rearrange("p a g e -> p a e g"), AX.X, ALU.add))
                first_of(LE, M1, O1, EPG)
                c(dve_.scalar_tensor_tensor(out=LE2, in0=O1, scalar=NEG, in1=LE, op0=ALU.mult, op1=ALU.add))
                first_of(LE2, M2, O2, EPG)
                dve_.tensor_tensor(E2, M2, M1, ALU.subtract).then_inc(sig("picked").sem, 1)
                dve.wait_ge(sig("second_exped").sem, sig("second_exped").at(1))
                c(dve_.tensor_scalar(M1, E2, 1.0, None, ALU.add))
                c(dve_.reciprocal(M1, M1))
                c(dve_.tensor_tensor(M1, M1, GW, ALU.mult))
                c(dve_.tensor_tensor(M2, M1, E2, ALU.mult))
                c(dve_.tensor_tensor(LE, O1, across(M1, EPG), ALU.mult))
                c(dve_.tensor_tensor(LE2, O2, across(M2, EPG), ALU.mult))
                c(dve_.tensor_tensor(LE, LE, LE2, ALU.add))
                c(dve_.tensor_tensor(O1, O1, O2, ALU.add))
                for g in range(NG):
                    dve_.tensor_tensor(WT[:, :, g, :], LE, across(G1[:, :, g:g + 1], EPG), ALU.mult)
                    last = dve_.tensor_tensor(MEM[:, :, g, :], O1, across(G1[:, :, g:g + 1], EPG), ALU.mult)
                last.then_inc(sig("routed").sem, 1)
                dve.wait_ge(sig("routed").sem, sig("routed").at(1))
                flat = MEM.rearrange("p a g e -> p a (g e)")
                c(dve_.tensor_scalar(WIDE, MEM, -FAR, FAR, ALU.mult, ALU.add))
                dve.wait_ge(sig("ranked").sem, sig("ranked").at(1))
                c(dve_.tensor_reduce(CNT, PB[:, 1, NT * NE:(NT + 1) * NE], AX.X, ALU.max))
                c(dve_.tensor_scalar(NRF, con("rounds"), CNT, None, ALU.is_lt))
                c(dve_.tensor_reduce(CNT, NRF, AX.X, ALU.add))
                dve_.tensor_copy(ROUNDS[:], CNT[0:1])
                c(dve_.tensor_tensor(RK[:, :, 0:NE], PB[:, 1, 0:nt * NE].rearrange("p (a n) -> p a n", a=nt),
                                     WIDE.rearrange("p a g e -> p a (g e)"), ALU.add))
                dve_.tensor_scalar(RK[:, :, NE:NE + 4], RK[:, :, 0:4], -float(CAP), None, ALU.add) \
                    .then_inc(sig("rank_in").sem, 1)
                assert c.n == router_steps, c.n
        passed(bias_in=16, projected=1, token_flipped=nt, token_copied=nt, routed=1, ranked=1, peaked=1,
               group_exped=1, picked=1, second_exped=1, dve_step=router_steps, rank_in=1)

        w1, w3 = (io[n][moe].rearrange("e (a k p) c -> e p a k c", a=2, p=P) for n in ("moe_w1_2", "moe_w3_2"))
        w2 = io["moe_w2_2"][moe].rearrange("e (a k p) c -> e p a k c", k=2, p=P)
        WTF = WT.rearrange("p a g e -> p a (g e)")
        pairs = NE // 2

        with nc.Block() as block:
            def rounds(eng):
                return eng.value_load(ROUNDS[0:1, 0:1], min_val=1, max_val=t // CAP)

            def slots_of(j):
                return slice(j * CAP, (j + 1) * CAP)

            @block.gpsimd
            def _(pool):
                nc.gpsimd.memset(A[:], 0.0).then_inc(sig("cleared").sem, 1)
                nc.gpsimd.memset(Y2, 0.0).then_inc(sig("cleared").sem, 1)
                nc.gpsimd.memset(SWT, 0.0).then_inc(sig("cleared").sem, 1)

            @block.sync
            def _(sp):
                with sp.Fori(0, rounds(sp)) as r, sp.Fori(0, pairs) as i:
                    for j in range(2):
                        n = 2 * (pairs * r + i) + j
                        for s, src in enumerate((w1, w3, w1, w3, w2, w2)):
                            sp.wait_ge(used[s].sem, used[s].at(n))
                            dst = tile(s, 4, T) if s < 4 else tile(s, 2, D)
                            sp.dma_start(dst, src[2 * i + j, :, s // 2 if s < 4 else s - 4]).then_inc(loaded[s].sem, 16)

            @block.tensor
            def _(pe):
                def gather(g):
                    pe.wait_ge(sig("picked").sem, sig("picked").at(g + 1))
                    for a in range(nt):
                        for m in range(2):
                            last = pe_.matmul(PB[:, 4 + m, :], SEL[:, a, :], ATK[:, a, m * T:(m + 1) * T],
                                              start=a == 0, stop=a == nt - 1)
                    last.then_inc(sig("gathered").sem, 1)

                def turn_gathered(g):
                    pe.wait_ge(sig("gather_copied").sem, sig("gather_copied").at(g + 1))
                    for k in range(KD):
                        last = pe_.transpose(PB[:, 4 + k // 4, (k % 4) * P:(k % 4 + 1) * P], XGS[:, k * P:(k + 1) * P],
                                             IDENT)
                    last.then_inc(sig("xg_flipped").sem, 1)

                def hidden(n, j, b):
                    pe.wait_ge(sig("expert_h").sem, sig("expert_h").at(n))
                    for k in range(KD):
                        for m in range(2):
                            s = 2 * (k // 4) + m
                            if k % 4 == 0:
                                pe.wait_ge(loaded[s].sem, loaded[s].at(16 * (n + 1)))
                            last = pe_.matmul(PB[m * CAP:(m + 1) * CAP, 0, :], XGT[:, b, k, slots_of(j)],
                                              tile(s, 4, T)[:, k % 4, :], start=k == 0, stop=k == KD - 1)
                            if k % 4 == 3:
                                last.then_inc(used[s].sem, 1)

                def turn_hidden(n, j):
                    pe.wait_ge(sig("expert_h").sem, sig("expert_h").at(n + 1))
                    for k in range(4):
                        last = pe_.transpose(PB[:, 1, k * P:(k + 1) * P], HS[:, j, k * P:(k + 1) * P], IDENT)
                    last.then_inc(sig("h_flipped").sem, 1)

                def outputs(n, j):
                    pe.wait_ge(sig("h_copied").sem, sig("h_copied").at(n + 1))
                    pe.wait_ge(sig("y_copied").sem, sig("y_copied").at(n))
                    for k in range(4):
                        s = 4 + k // 2
                        if k % 2 == 0:
                            pe.wait_ge(loaded[s].sem, loaded[s].at(16 * (n + 1)))
                        for m in range(2):
                            last = pe_.matmul(PB[m * CAP:(m + 1) * CAP, 2, :], HB[:, j, k, :],
                                              tile(s, 2, D)[:, k % 2, m * T:(m + 1) * T], start=k == 0, stop=k == 3)
                        if k % 2:
                            last.then_inc(used[s].sem, 1)

                def scatter(g):
                    pe.wait_ge(sig("y_copied").sem, sig("y_copied").at(2 * g))
                    pe.wait_ge(sig("pick_copied").sem, sig("pick_copied").at(g))
                    for m in range(KD):
                        pe.wait_ge(sig("added").sem, sig("added").at(KD * g + m - 1))
                        pe_.matmul(PB[:, 6 + m % 2, 0:t], Y2[:, m * P:(m + 1) * P], SWT[:, 0:t], start=True, stop=True) \
                            .then_inc(sig("scattered").sem, 1)

                pe.wait_ge(sig("cleared").sem, sig("cleared").at(3))
                gather(0)
                turn_gathered(0)
                every = rounds(pe)
                with pe.Fori(0, every) as r, pe.Fori(0, pairs // 2) as i:
                    for b in range(2):
                        g = pairs * r + 2 * i + b
                        pe.wait_ge(sig("xg_copied").sem, sig("xg_copied").at(g + 1))
                        hidden(2 * g, 0, b)
                        scatter(g)
                        turn_hidden(2 * g, 0)
                        gather(g + 1)
                        outputs(2 * g, 0)
                        hidden(2 * g + 1, 1, b)
                        turn_gathered(g + 1)
                        pe.wait_ge(sig("weighed").sem, sig("weighed").at(g + 1))
                        for a in range(nt):
                            last = pe_.transpose(PB[:, 3, a * P:(a + 1) * P], SELW[:, a, :], IDENT)
                        last.then_inc(sig("pick_flipped").sem, 1)
                        turn_hidden(2 * g + 1, 1)
                        outputs(2 * g + 1, 1)
                scatter(every * pairs)

            @block.scalar
            def _(act):
                def gathered(g, b):
                    act.wait_ge(sig("gathered").sem, sig("gathered").at(g + 1))
                    act_.activation(XGS, PB[:, 4:6, :].rearrange("p a b -> p (a b)"), ACT.Copy) \
                        .then_inc(sig("gather_copied").sem, 1)

                def turned(g, b):
                    act.wait_ge(sig("xg_flipped").sem, sig("xg_flipped").at(g + 1))
                    act_.activation(XGT[:, b].rearrange("p k c -> p (k c)"), PB[:, 4:6, :].rearrange("p a b -> p (a b)"),
                                    ACT.Copy).then_inc(sig("xg_copied").sem, 1)

                def silu(n, j):
                    act.wait_ge(used[3].sem, used[3].at(n + 1))
                    act_.activation(HS[CAP:P, j, :], PB[0:CAP, 0, :], ACT.Silu).then_inc(sig("expert_silu").sem, 1)

                def h_turned(n, j):
                    act.wait_ge(sig("h_flipped").sem, sig("h_flipped").at(n + 1))
                    act_.activation(HB[:, j], PB[:, 1, :].rearrange("p (k c) -> p k c", k=4)[:, :, 0:CAP], ACT.Copy) \
                        .then_inc(sig("h_copied").sem, 1)

                def y_out(n, j):
                    act.wait_ge(used[5].sem, used[5].at(n + 1))
                    for m in range(2):
                        last = act_.activation(Y2[slots_of(j), m * T:(m + 1) * T], PB[m * CAP:(m + 1) * CAP, 2, :],
                                               ACT.Copy)
                    last.then_inc(sig("y_copied").sem, 1)

                gathered(0, 0)
                turned(0, 0)
                with act.Fori(0, rounds(act)) as r, act.Fori(0, pairs // 2) as i:
                    for b in range(2):
                        g = pairs * r + 2 * i + b
                        silu(2 * g, 0)
                        h_turned(2 * g, 0)
                        gathered(g + 1, 1 - b)
                        y_out(2 * g, 0)
                        silu(2 * g + 1, 1)
                        turned(g + 1, 1 - b)
                        act.wait_ge(sig("pick_flipped").sem, sig("pick_flipped").at(g + 1))
                        act_.activation(SWT[:, 0:t], PB[:, 3, 0:t], ACT.Copy).then_inc(sig("pick_copied").sem, 1)
                        h_turned(2 * g + 1, 1)
                        y_out(2 * g + 1, 1)

            @block.vector
            def _(dve):
                def pick(p):
                    for j in range(2):
                        for a in range(nt):
                            last = dve_.tensor_scalar(SEL[:, a, slots_of(j)], con("slot"),
                                                      RK[:, a, bass.ds(2 * p + j, 1)], None, ALU.is_equal)
                    last.then_inc(sig("picked").sem, 1)

                def multiply(n, j):
                    dve.wait_ge(sig("expert_silu").sem, sig("expert_silu").at(n + 1))
                    dve_.tensor_tensor(HS[0:CAP, j, :], HS[CAP:P, j, :], PB[CAP:P, 0, :], ALU.mult) \
                        .then_inc(sig("expert_h").sem, 1)

                def add(g):
                    for m in range(KD):
                        dve.wait_ge(sig("scattered").sem, sig("scattered").at(KD * g + m + 1))
                        dve_.tensor_tensor(A[:, m, 0:t], A[:, m, 0:t], PB[:, 6 + m % 2, 0:t], ALU.add) \
                            .then_inc(sig("added").sem, 1)

                dve.wait_ge(sig("cleared").sem, sig("cleared").at(3))
                pick(0)
                dve.wait_ge(sig("gathered").sem, sig("gathered").at(1))
                pick(1)
                every = rounds(dve)
                with dve.Fori(0, every) as r:
                    with dve.Fori(0, pairs // 2) as i:
                        for b in range(2):
                            p = 2 * i + b
                            g = pairs * r + p
                            multiply(2 * g, 0)
                            add(g)
                            dve.wait_ge(sig("pick_flipped").sem, sig("pick_flipped").at(g))
                            for j in range(2):
                                e = bass.ds(2 * p + j, 1)
                                for a in range(nt):
                                    last = dve_.tensor_scalar(SELW[:, a, slots_of(j)], con("slot"), RK[:, a, e],
                                                              WTF[:, a, e], ALU.is_equal, ALU.mult)
                            last.then_inc(sig("weighed").sem, 1)
                            multiply(2 * g + 1, 1)
                            dve.wait_ge(sig("gathered").sem, sig("gathered").at(g + 2))
                            pick(p + 2)
                    dve.wait_ge(sig("picked").sem, sig("picked").at(pairs * r + pairs + 2))
                    dve.wait_ge(sig("weighed").sem, sig("weighed").at(pairs * r + pairs))
                    dve_.tensor_scalar(RK, RK, -float(CAP), None, ALU.add).then_inc(sig("rank_in").sem, 1)
                    dve.wait_ge(sig("rank_in").sem, sig("rank_in").at(r + 1))
                add(every * pairs)
                dve.wait_ge(sig("added").sem, sig("added").at(every * (pairs * KD) + KD))
                for m in range(KD):
                    for c in range(streams):
                        last = dve_.scalar_tensor_tensor(
                            out=X[:, m, half(c)], in0=A[:, m, half(c)], scalar=piece(2 + moe, 5, m, c),
                            in1=X[:, m, half(c)], op0=ALU.mult, op1=ALU.add)
                last.then_inc(sig("normed").sem, 1)
        passed(normed=1, cleared=3)
        counted = used + loaded + [sig(n) for n in ("picked", "gathered", "gather_copied", "xg_flipped", "xg_copied",
                                                    "expert_silu", "expert_h", "h_flipped", "h_copied", "y_copied",
                                                    "weighed", "pick_flipped", "pick_copied", "scattered", "added",
                                                    "rank_in")]
        with nc.Block() as block:
            @block.sync
            def _(sp):
                for s in counted:
                    sp.sem_clear(s.sem)
                    sp.sem_inc(s.sem, FIRST)
        for s in counted:
            s.base = FIRST

    def new_context():
        with nc.Block() as block:
            @block.sync
            def _(sp):
                sp.dma_start(X[:, :, half(1)], io["ctxT_2"].rearrange("(k p) t -> p k t", p=P)) \
                    .then_inc(sig("inputs_in").sem, 16)
                sp.wait_ge(sig("inputs_in").sem, sig("inputs_in").at(16))
        passed(inputs_in=16)

    def final_norm():
        items = [([X[:, k, 0:S] for k in range(KD)], [A[:, k, 0:S] for k in range(KD)],
                  [vec("final", k, k + 1) for k in range(KD)], PB[:, 0, 0:S], ONES, D, P)]
        with nc.Block() as block:
            @block.scalar
            def _(act):
                act_squares(items, 0)
                act_roots(act, items, 0)

            @block.tensor
            def _(pe):
                pe_sums(pe, items, 0)

            @block.vector
            def _(dve):
                dve_norms(dve, items, 0)
        passed(squared=1, summed=1, rooted=1, normed=1, inverted=1)

    stages = [
        lambda: (modulations(), modulated_norm(vec("norm1", 0, KD), 0, 0, 1, T)),
        lambda: mla(0),
        lambda: (modulated_norm(vec("norm2", 0, KD), 0, 3, 4, T),
                 feed_forward(io["ffn_w1"][0], io["ffn_w3"][0], io["ffn_w2"][0], 0, T)),
        lambda: (modulated_norm(vec("norm1", KD, 2 * KD), 1, 0, 1, T), hgrn2(1)),
        lambda: (modulated_norm(vec("norm2", KD, 2 * KD), 1, 3, 4, S),
                 feed_forward(io["ffn_w1"][1], io["ffn_w3"][1], io["ffn_w2"][1], 1, S)),
        lambda: (new_context(), modulated_norm(vec("mix", 0, KD), 2, 0, 1, T), even_mixer(2)),
        lambda: (modulated_norm(vec("ffn", 0, KD), 2, 3, 4, T), experts(2, 0, T)),
        lambda: (modulated_norm(vec("mix", KD, 2 * KD), 3, 0, 1, T), odd_mixer(3)),
        lambda: (modulated_norm(vec("ffn", KD, 2 * KD), 3, 3, 4, S), experts(3, 1, S)),
    ]
    for n, stage in enumerate(stages):
        stage()
        if n == upto:
            store_streams(X[:])
            return
    final_norm()
    store_streams(A[:, :, 0:S])


def layouts(i):
    def blocks(a):
        return np.ascontiguousarray(a.reshape(-1, P).T)

    def twice(a):
        return np.ascontiguousarray(np.tile(a.reshape(-1, HD), (1, 2)).T)

    def everywhere(a):
        return np.ascontiguousarray(np.tile(a.reshape(1, -1), (P, 1)))

    vecs = {
        "norm1": blocks(i["norm1_w"]), "norm2": blocks(i["norm2_w"]), "mla_q": blocks(i["mla_q_norm_w"]),
        "mla_kv": blocks(i["mla_kv_norm_w"]), "mla_qn": blocks(i["mla_qn_w"]), "mla_qr": twice(i["mla_qr_w"]),
        "mla_kn": blocks(i["mla_kn_w"]), "mla_kr": twice(i["mla_kr_w"]), "hg_o": blocks(i["hg_o_norm_w"]),
        "hg_lb": blocks(i["hg_lb_logits"]), "mix": blocks(i["norm_mix_g_2"]), "ffn": blocks(i["norm_ffn_g_2"]),
        "a_q": twice(i["a_q_gain_2"]), "a_k": twice(i["a_k_gain_2"]), "pool": blocks(i["pool_scale_2"]),
        "final": blocks(i["final_g_2"]), "ada_b": np.concatenate([blocks(i["ada_b"]), blocks(i["ada_b_2"])], axis=1),
        "moe_b": everywhere(np.concatenate([i["moe_b_group_2"], i["moe_b_expert_2"]], axis=1)),
    }
    pair = [np.stack([i["c"][0], i["c_ctx"]]), np.stack([i["c_2"][0], i["c_ctx_2"]])]
    padded = np.concatenate([np.stack(pair), np.zeros((2, 30, D), np.float32)], axis=1)
    tok = np.arange(S)
    row = tok[None, :] // GRID - tok[:, None] // GRID + NA_ROWS - 1
    col = np.clip(tok[None, :] % GRID - tok[:, None] % GRID + NA_COLS - 1, 0, 2 * NA_COLS - 2)
    bias = i["na_rel_bias_2"][0][:, row, col]
    given = {
        "xT": i["x"][0].T, "ctxT": i["ctx"][0].T, "ctxT_2": i["ctx_2"][0].T,
        "vecs": np.concatenate([vecs[n] for n, _ in VECS], axis=1),
        "cvec": padded.reshape(2, 32, KD, P).transpose(3, 0, 2, 1).reshape(P, -1),
        "router": np.concatenate([i["moe_w_group_2"], i["moe_w_expert_2"]], axis=2),
        "bias": bias.reshape(2 * 16, P, S),
        "consts": constants(),
    }
    for n in ("ada_w", "ada_w_2", "ffn_w1", "ffn_w3", "ffn_w2", "mla_w_in", "mla_w_uq", "mla_w_ukv", "mla_w_o",
              "hg_w_in", "hg_w_o", "even_w_in_2", "even_w_out_2", "pool_w_2", "odd_w_in_2", "odd_w_out_2",
              "moe_w1_2", "moe_w3_2", "moe_w2_2"):
        given[n] = i[n]
    return {n: np.ascontiguousarray(a) for n, a in given.items()}


def kernel(**inputs):
    import concourse.bacc as bacc
    from concourse.bass_utils import run_bass_kernel_spmd

    arrays = layouts({n: np.asarray(a) for n, a in inputs.items()})
    nc = bacc.Bacc("TRN2", target_bir_lowering=False, num_devices=1)
    io = {n: nc.dram_tensor(n, a.shape, mybir.dt.from_np(a.dtype), kind="ExternalInput").ap()
          for n, a in arrays.items()}
    out = nc.dram_tensor("y", (D, S), F32, kind="ExternalOutput").ap()
    build(nc, io, out)
    r = run_bass_kernel_spmd(nc, [arrays], core_ids=[0])
    return np.ascontiguousarray(r.results[0]["y"].T)[None]
```

```python
import math

import numpy as np

import concourse.bass as bass
from concourse import mybir

F32 = mybir.dt.float32
I32 = mybir.dt.int32
ALU = mybir.AluOpType
ACT = mybir.ActivationFunctionType
AX = mybir.AxisListType

P = 128
D = 1024
KD = D // P
S = 256
T = 2 * S
NT = T // P
GRID = 64
FF = 2816
FB = FF // P
HEADS = 8
QR, KVR, ROPE = 384, 256, 64
MLA_IN = QR + KVR + ROPE
HD = 64
EVEN_IN = 1280
POOLS = (2, 4, 8, 16)
NA_ROWS, NA_COLS = 8, 16
NG, EPG, DE = 4, 8, 512
NE = NG * EPG
NR = NG + NE
CAP = 64
EPS = 1e-6
LEVELS = 8
SLOTS = 6
SLOT = 2048
NEG = -1.0e30
FAR = 1.0e6
FIRST = 8

VECS = [("norm1", 2 * KD), ("norm2", 2 * KD), ("mla_q", 3), ("mla_kv", 2), ("mla_qn", 1), ("mla_qr", 1),
        ("mla_kn", 1), ("mla_kr", 1), ("hg_o", 1), ("hg_lb", 4 * KD), ("mix", 2 * KD), ("ffn", 2 * KD),
        ("a_q", 1), ("a_k", 1), ("pool", 4), ("final", KD), ("ada_b", 4 * 48), ("moe_b", 2 * NR)]
CONSTS = [("ident", P), ("ones", P), ("pair", P), ("turn", P), ("tri", P), ("cos", T), ("sin", T),
          ("decay", 2 * LEVELS * P), ("near", S), ("pools", 4 * 2 * S), ("slot", CAP),
          ("prior", EPG), ("rounds", 8), ("stream", 2), ("eps", 1)]


def places(table):
    at, out = 0, {}
    for name, n in table:
        out[name] = (at, at + n)
        at += n
    return out, at


VEC, NVEC = places(VECS)
CON, NCON = places(CONSTS)


def constants():
    c = np.zeros((P, NCON), np.float32)

    def put(name, value):
        a, b = CON[name]
        c[:, a:b] = np.asarray(value, np.float32).reshape(P, b - a)

    p = np.arange(P)
    put("ident", np.eye(P))
    put("ones", np.ones((P, P)))
    put("pair", p[:, None] // HD == p[None, :] // HD)
    turn = np.zeros((P, P))
    for m in range(P):
        if (m // 16) % 2 == 0:
            turn[m + 16, m] = -1
        else:
            turn[m - 16, m] = 1
    put("turn", turn)
    put("tri", p[:, None] < p[None, :])
    tok = np.arange(S)
    freq = np.power(np.float32(10000.0), -np.arange(16, dtype=np.float32) / np.float32(16)).astype(np.float32)
    q = p % HD
    where = np.where(q[:, None] < 32, tok[None, :] // GRID, tok[None, :] % GRID).astype(np.float32)
    angle = where * freq[q % 16][:, None]
    cos, sin = np.ones((P, T)), np.zeros((P, T))
    cos[:, :S], sin[:, :S] = np.cos(angle), np.sin(angle)
    put("cos", cos)
    put("sin", sin)
    masks = np.zeros((2, P, LEVELS, P))
    for l in range(LEVELS - 1):
        w = 64 >> l
        same = p[:, None] // (2 * w) == p[None, :] // (2 * w)
        late = (p // w) % 2 == 1
        masks[0, :, l] = same & ~late[:, None] & late[None, :]
        masks[1, :, l] = same & late[:, None] & ~late[None, :]
    masks[:, :, LEVELS - 1] = np.eye(P)
    put("decay", masks.transpose(1, 0, 2, 3))
    start = np.clip(p % GRID - NA_COLS // 2, 0, GRID - NA_COLS)
    kc = tok % GRID
    inside = (kc[None, :] >= start[:, None]) & (kc[None, :] < start[:, None] + NA_COLS)
    put("near", np.where(inside, 0.0, NEG))
    pools = np.zeros((4, S, S), np.float32)
    for g, w in enumerate(POOLS):
        for t in range(S):
            lo, hi = max(t - w // 2, 0), min(t - w // 2 + w, S)
            pools[g, lo:hi, t] = np.float32(1) / np.float32(hi - lo)
            pools[g, t, t] -= 1
    put("pools", pools.reshape(4, 2, P, S).transpose(2, 0, 1, 3))
    put("slot", np.tile(np.arange(CAP), (P, 1)))
    put("prior", np.tile(np.arange(EPG, 0, -1), (P, 1)))
    put("rounds", np.tile(np.arange(8) * CAP, (P, 1)))
    put("stream", p[:, None] % 32 == np.arange(2)[None, :])
    put("eps", np.full((P, 1), EPS))
    return c


class Signal:

    def __init__(self, nc, name):
        self.sem = nc.alloc_semaphore(name)
        self.base = FIRST

    def at(self, n):
        return n + self.base

    def passed(self, n):
        self.base += n


class Chain:

    def __init__(self, eng, signal, turn=0, each=0):
        self.eng, self.counts, self.turn, self.each, self.n = eng, signal, turn, each, 0

    def __call__(self, ins):
        self.n += 1
        ins.then_inc(self.counts.sem, 1)
        self.eng.wait_ge(self.counts.sem, self.counts.at(self.turn * self.each + self.n))


def build(nc, io, out, upto=99):
    act_, dve_, pe_ = nc.scalar, nc.vector, nc.tensor

    def sb(name, shape, dtype=F32):
        return nc.alloc_sbuf_tensor(name, shape, dtype)

    X = sb("X", [P, KD, T])
    A = sb("A", [P, KD, T])
    RING = sb("RING", [P, SLOTS, SLOT])
    BIG = sb("BIG", [P, FB * T])
    WORK = sb("WORK", [P, KD * T])
    MORE = sb("MORE", [P, KD * T])
    ROOT = sb("ROOT", [P, 3, T])
    SIL = sb("SIL", [P, 2, T])
    MODS = sb("MODS", [P, 4, 48, 2])
    GAIN = sb("GAIN", [P, 2, KD])
    CST = sb("CST", [P, NCON])
    V = sb("V", [P, NVEC])
    CS = sb("CS", [P, 2, KD, 32])
    SMALL = sb("SMALL", [P, 640])
    ROUNDS = sb("ROUNDS", [1, 1], I32)
    PB = nc.alloc_psum_tensor("PB", [P, 8, T], F32)

    def con(name):
        return CST[:, CON[name][0]:CON[name][1]]

    def vec(name, a=0, b=None):
        x, y = VEC[name]
        return V[:, x + a:(y if b is None else x + b)]

    IDENT, ONES, PAIR, TURN, TRI = (con(n) for n in ("ident", "ones", "pair", "turn", "tri"))
    COS, SIN = con("cos"), con("sin")

    signals = {}

    def sig(name):
        if name not in signals:
            signals[name] = Signal(nc, name)
        return signals[name]

    loaded = [sig(f"loaded{s}") for s in range(SLOTS + 1)]
    used = [sig(f"used{s}") for s in range(SLOTS + 1)]
    for name in ("inputs_in", "stored", "dve_step", "act_step", "squared", "summed", "rooted", "normed",
                 "rotated", "roped", "mod_summed", "silu_made", "h_made", "drained", "projected",
                 "scored", "peaked", "exped", "shared", "flipped", "turned", "weighted", "carried",
                 "staged", "gated", "forgot", "logged", "summed_up", "decayed", "spread", "levelled",
                 "levels_ready", "kx_flipped", "kx_copied", "state_made", "state_copied", "products",
                 "attended", "read_out", "biased", "bias_in", "pooled", "pool_copied", "mixed",
                 "token_flipped", "token_copied", "routed", "group_exped", "second_exped", "ranked",
                 "rank_in", "picked", "gathered", "gather_copied", "expert_silu", "expert_h",
                 "slots_out", "pick_flipped", "pick_copied", "scattered", "added", "rounds_in",
                 "cleared", "absed", "mod_flipped", "inverted",
                 "xg_flipped", "xg_copied", "h_flipped", "h_copied", "y_copied", "weighed"):
        sig(name)

    def tile(s, k, n, at=0):
        return RING[:, s, at:at + k * n].rearrange("p (k n) -> p k n", k=k)

    def rows(w, a, b):
        return w[:, a:b].rearrange("(k p) n -> p k n", p=P)

    def passed(**counts):
        for name, n in counts.items():
            signals[name].passed(n)

    def half(w):
        return slice(w * S, (w + 1) * S)

    with nc.Block() as block:
        @block.sync
        def _(sp):
            for s in signals.values():
                sp.sem_inc(s.sem, FIRST)

    with nc.Block() as block:
        @block.sync
        def _(sp):
            for dst, name in ((CS, "cvec"), (V, "vecs"), (CST, "consts")):
                flat = dst[:] if len(dst.shape) == 2 else dst[:].rearrange("p a b c -> p (a b c)")
                sp.dma_start(flat, io[name]).then_inc(sig("inputs_in").sem, 16)
            for w, name in enumerate(("xT", "ctxT")):
                sp.dma_start(X[:, :, half(w)], io[name].rearrange("(k p) t -> p k t", p=P)) \
                    .then_inc(sig("inputs_in").sem, 16)

        @block.scalar
        def _(act):
            act.wait_ge(sig("inputs_in").sem, sig("inputs_in").at(5 * 16))
            act_.activation(CS[:], CS[:], ACT.Silu).then_inc(sig("staged").sem, 1)
    passed(inputs_in=80, staged=1)

    def modulations():
        turns, chunks = 4, SLOTS // 2
        layers = [(0, io["ada_w"][0])]
        ROW = BIG[:, 0:chunks * T].rearrange("p (j t) -> p j t", t=T)
        with nc.Block() as block:
            @block.sync
            def _(sp):
                for n, (_, w) in enumerate(layers):
                    cut = w.rearrange("(a k p) (n c) -> p n a k c", a=2, p=P, c=T)
                    with sp.Fori(0, turns) as i:
                        for s in range(SLOTS):
                            sp.wait_ge(used[s].sem, used[s].at(turns * n + i))
                            sp.dma_start(tile(s, 4, T), cut[:, chunks * i + s // 2, s % 2]).then_inc(loaded[s].sem, 16)

            @block.tensor
            def _(pe):
                for n, (layer, _) in enumerate(layers):
                    with pe.Fori(0, turns) as i:
                        turn = turns * n + i

                        def multiply(j):
                            for a in range(2):
                                s = 2 * j + a
                                pe.wait_ge(loaded[s].sem, loaded[s].at(16 * (turn + 1)))
                                for k in range(4):
                                    last = pe_.matmul(PB[32 * k:32 * k + 32, 1 + j, :], CS[:, layer // 2, 4 * a + k, :],
                                                      tile(s, 4, T)[:, k, :], start=a == 0, stop=a == 1)
                                last.then_inc(used[s].sem, 1)

                        def turn_over(j):
                            pe.wait_ge(sig("drained").sem, sig("drained").at(chunks * turn + j + 1))
                            for m in range(4):
                                at = 96 * layer + (chunks * i + j) * 8 + 2 * m
                                last = pe_.matmul(PB[:, 0, bass.ds(at, 2)], ROW[:, j, m * P:(m + 1) * P],
                                                  con("stream"), start=True, stop=True)
                            last.then_inc(sig("mod_flipped").sem, 1)

                        multiply(0)
                        multiply(1)
                        turn_over(0)
                        multiply(2)
                        turn_over(1)
                        turn_over(2)

            @block.scalar
            def _(act):
                for n in range(len(layers)):
                    with act.Fori(0, turns) as i:
                        turn = turns * n + i
                        for j in range(chunks):
                            act.wait_ge(used[2 * j + 1].sem, used[2 * j + 1].at(turn + 1))
                            act.wait_ge(sig("mod_flipped").sem, sig("mod_flipped").at(chunks * (turn - 1) + j + 1))
                            act_.activation(ROW[:, j, :], PB[:, 1 + j, :], ACT.Copy).then_inc(sig("drained").sem, 1)

            @block.vector
            def _(dve):
                dve.wait_ge(sig("mod_flipped").sem, sig("mod_flipped").at(len(layers) * turns * chunks))
                for layer, _ in layers:
                    bias = vec("ada_b", 48 * layer, 48 * layer + 48).unsqueeze(2).broadcast_to([P, 48, 2])
                    sums = PB[:, 0, 96 * layer:96 * layer + 96].rearrange("p (n w) -> p n w", w=2)
                    last = dve_.tensor_tensor(MODS[:, layer], sums, bias, ALU.add)
                last.then_inc(sig("mod_summed").sem, 1)
        for s in range(SLOTS):
            used[s].passed(len(layers) * turns)
            loaded[s].passed(len(layers) * turns * 16)
        n = len(layers) * turns * chunks
        passed(mod_summed=1, mod_flipped=n, drained=n)

    def piece(layer, i, k, w):
        return MODS[:, layer, KD * i + k, w:w + 1]

    def act_squares(items, n):
        j = 0
        for src, _, _, _, _, _, r in items:
            for x in src:
                w = x.shape[-1]
                last = act_.activation(WORK[0:r, j * T:j * T + w], x, ACT.Square)
                j += 1
        last.then_inc(sig("squared").sem, 1)

    def pe_sums(pe, items, n):
        pe.wait_ge(sig("squared").sem, sig("squared").at(n + 1))
        j = 0
        for src, _, _, total, ones, _, r in items:
            w = src[0].shape[-1]
            for i in range(len(src)):
                last = pe_.matmul(total, ones[0:r, 0:r], WORK[0:r, j * T:j * T + w],
                                  start=i == 0, stop=i == len(src) - 1)
                j += 1
        last.then_inc(sig("summed").sem, 1)

    def act_roots(act, items, n):
        act.wait_ge(sig("summed").sem, sig("summed").at(n + 1))
        for j, (src, _, _, total, _, width, r) in enumerate(items):
            w = src[0].shape[-1]
            last = act_.activation(ROOT[0:r, j, 0:w], total, ACT.Sqrt, bias=con("eps")[0:r], scale=1.0 / width)
        last.then_inc(sig("rooted").sem, 1)

    def dve_norms(dve, items, n):
        dve.wait_ge(sig("rooted").sem, sig("rooted").at(n + 1))
        for j, (src, *_, r) in enumerate(items):
            w = src[0].shape[-1]
            last = dve_.reciprocal(ROOT[0:r, j, 0:w], ROOT[0:r, j, 0:w])
        last.then_inc(sig("inverted").sem, 1)
        dve.wait_ge(sig("inverted").sem, sig("inverted").at(n + 1))
        for j, (src, dst, gains, _, _, _, r) in enumerate(items):
            w = src[0].shape[-1]
            for x, y, g in zip(src, dst, gains):
                last = dve_.scalar_tensor_tensor(out=y, in0=x, scalar=g[0:r], in1=ROOT[0:r, j, 0:w],
                                                 op0=ALU.mult, op1=ALU.mult)
        last.then_inc(sig("normed").sem, 1)

    def pe_turns(pe, items, norm, n):
        pe.wait_ge(sig("normed").sem, sig("normed").at(norm + 1))
        for x, y, r in items:
            last = pe_.matmul(y, TURN[0:r, 0:r], x, start=True, stop=True)
        last.then_inc(sig("rotated").sem, 1)

    def dve_ropes(dve, chain, items, n):
        dve.wait_ge(sig("rotated").sem, sig("rotated").at(n + 1))
        for j, (x, y, r) in enumerate(items):
            dve_.tensor_tensor(SIL[0:r, j, :], y, SIN[0:r], ALU.mult)
            last = dve_.tensor_tensor(x, x, COS[0:r], ALU.mult)
        chain(last)
        for j, (x, y, r) in enumerate(items):
            last = dve_.tensor_tensor(x, x, SIL[0:r, j, :], ALU.add)
        last.then_inc(sig("roped").sem, 1)

    def modulated_norm(gain, layer, shift, scale, t):
        items = [([X[:, k, 0:t] for k in range(KD)], None, None, PB[:, 0, 0:t], ONES, D, P)]
        streams = t // S
        with nc.Block() as block:
            @block.scalar
            def _(act):
                for k in range(0, KD, 2):
                    act_.activation(WORK[:, k * T:k * T + t], X[:, k, 0:t], ACT.Square).then_inc(sig("squared").sem, 1)
                act_roots(act, items, 0)
                for w in range(1, streams):
                    for k in range(KD):
                        act.wait_ge(sig("spread").sem, sig("spread").at(k + 1))
                        act_.activation(A[:, k, half(w)], A[:, k, half(w)], ACT.Identity,
                                        bias=piece(layer, shift, k, w), scale=GAIN[:, w, k:k + 1])

            @block.tensor
            def _(pe):
                for k in range(KD):
                    if k % 2 == 0:
                        pe.wait_ge(sig("squared").sem, sig("squared").at(k // 2 + 1))
                    else:
                        pe.wait_ge(sig("staged").sem, sig("staged").at(k // 2 + 1))
                    last = pe_.matmul(PB[:, 0, 0:t], ONES, WORK[:, k * T:k * T + t], start=k == 0, stop=k == KD - 1)
                last.then_inc(sig("summed").sem, 1)

            @block.vector
            def _(dve):
                chain = Chain(dve, sig("dve_step"))
                for k in range(1, KD, 2):
                    dve_.tensor_tensor(WORK[:, k * T:k * T + t], X[:, k, 0:t], X[:, k, 0:t], ALU.mult) \
                        .then_inc(sig("staged").sem, 1)
                for w in range(2):
                    last = dve_.scalar_tensor_tensor(
                        out=GAIN[:, w, :], in0=MODS[:, layer, KD * scale:KD * scale + KD, w], scalar=1.0, in1=gain,
                        op0=ALU.add, op1=ALU.mult)
                chain(last)
                dve.wait_ge(sig("rooted").sem, sig("rooted").at(1))
                chain(dve_.reciprocal(ROOT[:, 0, 0:t], ROOT[:, 0, 0:t]))
                for k in range(KD):
                    last = dve_.tensor_tensor(A[:, k, 0:t], X[:, k, 0:t], ROOT[:, 0, 0:t], ALU.mult)
                    last.then_inc(sig("spread").sem, 1)
                dve.wait_ge(sig("spread").sem, sig("spread").at(KD))
                for k in range(KD):
                    last = dve_.tensor_scalar(A[:, k, half(0)], A[:, k, half(0)], GAIN[:, 0, k:k + 1],
                                              piece(layer, shift, k, 0), ALU.mult, ALU.add)
                last.then_inc(sig("normed").sem, 1)
        passed(squared=KD // 2, staged=KD // 2, summed=1, rooted=1, dve_step=2, spread=KD, normed=1)

    def row_tiles(w):
        return w.rearrange("(n k p) c -> n p k c", k=2, p=P)

    def first_rows(sp, w, before):
        sp.wait_ge(used[0].sem, used[0].at(before))
        sp.dma_start(tile(0, 2, D), row_tiles(w)[0]).then_inc(loaded[0].sem, 16)

    def add_product(w, nk, src, layer, gate, t):
        n = nk // 2
        pairs = (n - 2) // 2
        cut = row_tiles(w)
        tail = list(range(1 + 2 * pairs, n))
        with nc.Block() as block:
            @block.sync
            def _(sp):
                def load(s, i, turn):
                    sp.wait_ge(used[s].sem, used[s].at(turn))
                    sp.dma_start(tile(s, 2, D), cut[i]).then_inc(loaded[s].sem, 16)
                with sp.Fori(0, pairs) as i:
                    for j in range(2):
                        load((1 + j) % 2, 2 * i + 1 + j, i + (1 + j) // 2)
                for i in tail:
                    load(i % 2, i, i // 2)

            @block.tensor
            def _(pe):
                def multiply(s, i, turn, first, final):
                    pe.wait_ge(loaded[s].sem, loaded[s].at(16 * (turn + 1)))
                    for r in range(2):
                        for m in range(KD):
                            last = pe_.matmul(PB[:, m, 0:t], tile(s, 2, D)[:, r, m * P:(m + 1) * P],
                                              src(2 * i + r), start=first and r == 0, stop=final and r == 1)
                    last.then_inc(used[s].sem, 1)
                multiply(0, 0, 0, True, False)
                with pe.Fori(0, pairs) as i:
                    for j in range(2):
                        multiply((1 + j) % 2, 2 * i + 1 + j, i + (1 + j) // 2, False, False)
                for i in tail:
                    multiply(i % 2, i, i // 2, False, i == n - 1)

            @block.vector
            def _(dve):
                s = (n - 1) % 2
                dve.wait_ge(used[s].sem, used[s].at((n - 1) // 2 + 1))
                for m in range(KD):
                    for c in range(t // S):
                        last = dve_.scalar_tensor_tensor(
                            out=X[:, m, half(c)], in0=PB[:, m, half(c)], scalar=piece(layer, gate, m, c),
                            in1=X[:, m, half(c)], op0=ALU.mult, op1=ALU.add)
                last.then_inc(sig("added").sem, 1)
        for s in range(2):
            count = (n + 1 - s) // 2
            used[s].passed(count)
            loaded[s].passed(16 * count)
        passed(added=1)

    def feed_forward(w1, w3, w2, layer, t):
        hidden = BIG[:, 0:FB * T].rearrange("p (n t) -> p n t", t=T)
        turns = FB // 2
        with nc.Block() as block:
            @block.sync
            def _(sp):
                cuts = [w.rearrange("(k p) (n c) -> p n k c", p=P, c=P) for w in (w1, w3)]
                with sp.Fori(0, turns) as i:
                    for s in range(2):
                        sp.wait_ge(used[s].sem, used[s].at(i))
                        for j, cut in enumerate(cuts):
                            sp.dma_start(tile(s, KD, P, j * KD * P), cut[:, 2 * i + s]).then_inc(loaded[s].sem, 16)
                first_rows(sp, w2, turns)

            @block.tensor
            def _(pe):
                with pe.Fori(0, turns) as i:
                    for s in range(2):
                        pe.wait_ge(loaded[s].sem, loaded[s].at(32 * (i + 1)))
                        pe.wait_ge(sig("h_made").sem, sig("h_made").at(2 * i + s - 1))
                        for j in range(2):
                            for k in range(KD):
                                last = pe_.matmul(PB[:, 2 * s + j, 0:t], tile(s, KD, P, j * KD * P)[:, k, :],
                                                  A[:, k, 0:t], start=k == 0, stop=k == KD - 1)
                        last.then_inc(used[s].sem, 1)

            @block.scalar
            def _(act):
                with act.Fori(0, turns) as i:
                    for s in range(2):
                        act.wait_ge(used[s].sem, used[s].at(i + 1))
                        act.wait_ge(sig("h_made").sem, sig("h_made").at(2 * i + s - 1))
                        act_.activation(SIL[:, s, 0:t], PB[:, 2 * s, 0:t], ACT.Silu).then_inc(sig("silu_made").sem, 1)

            @block.vector
            def _(dve):
                with dve.Fori(0, turns) as i:
                    for s in range(2):
                        dve.wait_ge(sig("silu_made").sem, sig("silu_made").at(2 * i + s + 1))
                        dve_.tensor_tensor(hidden[:, 2 * i + s, 0:t], PB[:, 2 * s + 1, 0:t], SIL[:, s, 0:t],
                                           ALU.mult).then_inc(sig("h_made").sem, 1)
        for s in range(2):
            used[s].passed(turns)
            loaded[s].passed(32 * turns)
        passed(silu_made=FB, h_made=FB)
        add_product(w2, FB, lambda i: hidden[:, i, 0:t], layer, 5, t)

    def store_streams(x):
        with nc.Block() as block:
            @block.sync
            def _(sp):
                sp.dma_start(out.rearrange("(k p) t -> p k t", p=P), x).then_inc(sig("stored").sem, 16)
                sp.wait_ge(sig("stored").sem, sig("stored").at(16))
        passed(stored=16)

    PR, PT = ([w[:, i * NT * T:(i + 1) * NT * T].rearrange("p (a b) -> p a b", a=NT) for w in (WORK, MORE)]
              for i in range(2))
    OT = BIG[:, 0:KD * T].rearrange("p (k t) -> p k t", t=T)
    OWN = BIG[:, KD * T:FB * T]
    PEAK, SHARE = [SMALL[:, 0:8], SMALL[:, 16:24]], [SMALL[:, 8:16], SMALL[:, 24:32]]

    def own(at, k, n=T):
        a = OWN[:, at:at + k * n]
        return a if k == 1 else a.rearrange("p (k n) -> p k n", k=k)

    def first_key(t):
        return 0 if t < 2 else S

    def flip_place(tiles, b, kt):
        if tiles == NT:
            return PB[:, NT * b + kt, :]
        return PB[:, 2 * b + kt // 2, (kt % 2) * S:(kt % 2 + 1) * S]

    def pe_scores(pe, n, tiles, pairs, b):
        for t in range(tiles):
            k0 = first_key(t)
            for j, (q, k) in enumerate(pairs):
                last = pe_.matmul(PB[:, tiles * b + t, k0:T], q[:, t * P:(t + 1) * P], k[:, k0:T],
                                  start=j == 0, stop=j == len(pairs) - 1)
        last.then_inc(sig("scored").sem, 1)

    def pe_apply(pe, n, tiles, values, r, b):
        pe.wait_ge(sig("shared").sem, sig("shared").at(n + 1))
        for kt in range(NT):
            for t in range(tiles):
                if kt * P >= first_key(t):
                    last = pe_.transpose(flip_place(tiles, b, kt)[:, t * P:(t + 1) * P], PR[b][:, t, kt * P:(kt + 1) * P], IDENT)
        last.then_inc(sig("flipped").sem, 1)
        pe.wait_ge(sig("turned").sem, sig("turned").at(n + 1))
        for w in range(tiles // 2):
            kts = range(2 * w, NT)
            for kt in kts:
                last = pe_.matmul(PB[r, tiles * b, half(w)], values(kt), PT[b][:, kt, half(w)],
                                  start=kt == kts[0], stop=kt == NT - 1)
        last.then_inc(sig("weighted").sem, 1)

    def dve_peaks(dve, chain, n, tiles, scale, scores, b):
        dve.wait_ge(sig("scored").sem, sig("scored").at(n + 1))
        for t in range(tiles):
            last = dve_.tensor_reduce(PEAK[b][:, t:t + 1], scores(t, b), AX.X, ALU.max, negate=True)
        chain(last)
        dve_.tensor_scalar(PEAK[b][:, 4:4 + tiles], PEAK[b][:, 0:tiles], scale, None, ALU.mult) \
            .then_inc(sig("peaked").sem, 1)

    def dve_shares(dve, chain, n, tiles, b):
        dve.wait_ge(sig("exped").sem, sig("exped").at(n + 1))
        chain(dve_.reciprocal(SHARE[b][:, 4:4 + tiles], SHARE[b][:, 0:tiles]))
        for t in range(tiles):
            k0 = first_key(t)
            last = dve_.tensor_scalar(PR[b][:, t, k0:T], PR[b][:, t, k0:T], SHARE[b][:, 4 + t:5 + t], None, ALU.mult)
        last.then_inc(sig("shared").sem, 1)

    def act_exps(act, n, tiles, scale, scores, b):
        act.wait_ge(sig("peaked").sem, sig("peaked").at(n + 1))
        for t in range(tiles):
            last = act_.activation(PR[b][:, t, first_key(t):T], scores(t, b), ACT.Exp, bias=PEAK[b][:, 4 + t:5 + t],
                                   scale=scale, accum_out=SHARE[b][:, t:t + 1])
        last.then_inc(sig("exped").sem, 1)

    def act_turned(act, n, tiles, b):
        act.wait_ge(sig("flipped").sem, sig("flipped").at(n + 1))
        for kt in range(NT):
            w = S if kt < 2 else tiles * P
            last = act_.activation(PT[b][:, kt, 0:w], flip_place(tiles, b, kt)[:, 0:w], ACT.Copy)
        last.then_inc(sig("turned").sem, 1)

    def act_carry(act, n, tiles, r, dst, b):
        act.wait_ge(sig("weighted").sem, sig("weighted").at(n + 1))
        act_.activation(dst, PB[r, tiles * b, 0:tiles * P], ACT.Copy).then_inc(sig("carried").sem, 1)

    ATTEND = ("scored", "peaked", "exped", "shared", "flipped", "turned", "weighted", "carried")

    def psum_scores(t, b):
        return PB[:, 4 * b + t, first_key(t):T]

    def mla(gate_layer):
        CQ, CKV = own(0, 3), own(3 * T, 2)
        KRT, QN, KN, QRT, VB = own(5 * T, 1), own(6 * T, 1), own(7 * T, 1), own(8 * T, 1), own(9 * T, NT, P)
        w_in, w_uq, w_ukv = io["mla_w_in"][0], io["mla_w_uq"][0], io["mla_w_ukv"][0]
        widths = [S, S, MLA_IN - 2 * S]
        dims, scale = P + ROPE, 1.0 / math.sqrt(P + ROPE)
        all_rows = slice(0, P)
        ROW = own(10 * T, 3)
        middle = {1: io["ada_w"][1], 2: io["ada_w_2"][0]}

        def side_slot(h, j, a):
            return (1 + a, 1 + 2 * h + j // 2) if j != 1 else (3 + a, h)

        latents = [([PB[:, i, :] for i in range(3)], [CQ[:, i, :] for i in range(3)],
                    [vec("mla_q", i, i + 1) for i in range(3)], PB[:, 6, :], ONES, QR, P),
                   ([PB[:, 3 + i, :] for i in range(2)], [CKV[:, i, :] for i in range(2)],
                    [vec("mla_kv", i, i + 1) for i in range(2)], PB[:, 7, :], ONES, KVR, P)]
        rotary = [([PB[0:ROPE, 5, :]], [KRT[0:ROPE]], [vec("mla_kr")], PB[0:ROPE, 6, :], ONES, ROPE, ROPE)]
        turned_key = [(KRT[0:ROPE], PB[0:ROPE, 7, :], ROPE)]
        head = [([PB[:, 4, :]], [QN], [vec("mla_qn")], PB[:, 1, :], ONES, P, P),
                ([PB[0:ROPE, 5, :]], [QRT[0:ROPE]], [vec("mla_qr")], PB[0:ROPE, 2, :], ONES, ROPE, ROPE),
                ([PB[:, 6, :]], [KN], [vec("mla_kn")], PB[:, 3, :], ONES, P, P)]
        turned_query = [(QRT[0:ROPE], PB[0:ROPE, 0, :], ROPE)]
        query_full = [(QRT, PB[:, 0, :], P)]
        each = 3
        with nc.Block() as block:
            @block.gpsimd
            def _(pool):
                nc.gpsimd.memset(QRT[ROPE:P], 0.0).then_inc(sig("cleared").sem, 1)

            @block.sync
            def _(sp):
                for s in range(3):
                    sp.dma_start(tile(s, KD, widths[s]), rows(w_in, s * S, s * S + widths[s])) \
                        .then_inc(loaded[s].sem, 16)
                cq = w_uq.rearrange("(k p) (h n) -> p h k n", p=P, n=dims)
                ckv = w_ukv.rearrange("(k p) (h n) -> p h k n", p=P, n=2 * P)
                for layer, w in middle.items():
                    chunk = w.rearrange("(a k p) (n c) -> p n a k c", a=2, p=P, c=T)
                    with sp.Fori(4 * layer - 4, 4 * layer) as h:
                        sp.wait_ge(used[0].sem, used[0].at(h + 1))
                        sp.dma_start(tile(0, 3, dims), cq[:, h]).then_inc(loaded[0].sem, 16)
                        sp.dma_start(tile(0, 2, 2 * P, 3 * dims), ckv[:, h]).then_inc(loaded[0].sem, 16)
                        for j in range(3):
                            for a in range(2):
                                s, n = side_slot(h, j, a)
                                sp.wait_ge(used[s].sem, used[s].at(n))
                                sp.dma_start(tile(s, 4, T), chunk[:, 3 * (h - 4 * layer + 4) + j, a]) \
                                    .then_inc(loaded[s].sem, 16)
                first_rows(sp, io["mla_w_o"][0], 1 + HEADS)

            @block.tensor
            def _(pe):
                for m in range(6):
                    s, c = m // 2, (m % 2) * P
                    n = min(P, MLA_IN - m * P)
                    pe.wait_ge(loaded[s].sem, loaded[s].at(16))
                    w = tile(s, KD, widths[s])
                    for k in range(KD):
                        last = pe_.matmul(PB[0:n, m, :], w[:, k, c:c + n], A[:, k, :], start=k == 0, stop=k == KD - 1)
                    if m % 2:
                        last.then_inc(used[s].sem, 1)
                pe_sums(pe, latents, 0)
                pe.wait_ge(sig("normed").sem, sig("normed").at(1))
                pe_sums(pe, rotary, 1)
                pe_turns(pe, turned_key, 1, 0)
                pe.wait_ge(sig("roped").sem, sig("roped").at(1))
                pe.wait_ge(sig("cleared").sem, sig("cleared").at(1))

                def project(h):
                    pe.wait_ge(loaded[0].sem, loaded[0].at(32 * h + 48))
                    wq, wkv = tile(0, 3, dims), tile(0, 2, 2 * P, 3 * dims)
                    for bank, a, b in ((4, 0, P), (5, P, dims)):
                        for k in range(3):
                            pe_.matmul(PB[0:b - a, bank, :], wq[:, k, a:b], CQ[:, k, :], start=k == 0, stop=k == 2)
                    for k in range(2):
                        pe_.matmul(PB[:, 6, :], wkv[:, k, 0:P], CKV[:, k, :], start=k == 0, stop=k == 1)
                    for t in range(NT):
                        for k in range(2):
                            last = pe_.matmul(PB[:, 7, t * P:(t + 1) * P], CKV[:, k, t * P:(t + 1) * P],
                                              wkv[:, k, P:2 * P], start=k == 0, stop=k == 1)
                    last.then_inc(used[0].sem, 1)

                def side_products(h, layer, j, bank):
                    for a in range(2):
                        s, n = side_slot(h, j, a)
                        pe.wait_ge(loaded[s].sem, loaded[s].at(16 * (n + 1)))
                        for k in range(4):
                            last = pe_.matmul(PB[32 * k:32 * k + 32, bank, :], CS[:, layer // 2, 4 * a + k, :],
                                              tile(s, 4, T)[:, k, :], start=a == 0, stop=a == 1)
                        last.then_inc(used[s].sem, 1)

                def side_turn(h, j):
                    pe.wait_ge(sig("drained").sem, sig("drained").at(3 * h + j + 1))
                    for m in range(4):
                        last = pe_.matmul(PB[:, 1, 8 * j + 2 * m:8 * j + 2 * m + 2], ROW[:, j, m * P:(m + 1) * P],
                                          con("stream"), start=True, stop=True)
                    last.then_inc(sig("mod_flipped").sem, 1)

                def ready(h, layer):
                    pe_sums(pe, head, h + 2)
                    pe.wait_ge(sig("carried").sem, sig("carried").at(h))
                    side_products(h, layer, 0, 0)
                    pe.wait_ge(sig("rooted").sem, sig("rooted").at(h + 3))
                    side_products(h, layer, 1, 7)
                    side_turn(h, 0)
                    side_products(h, layer, 2, 0)
                    side_turn(h, 1)
                    side_turn(h, 2)
                    pe_turns(pe, query_full, h + 2, h + 1)
                    pe.wait_ge(sig("roped").sem, sig("roped").at(h + 2))

                scores = [(QN, KN), (QRT[0:ROPE], KRT[0:ROPE])]
                project(0)
                ready(0, 1)
                for layer, heads in ((1, (0, 3)), (2, (3, HEADS - 1))):
                    with pe.Fori(*heads) as h:
                        pe_scores(pe, h, NT, scores, 0)
                        project(h + 1)
                        pe_apply(pe, h, NT, lambda kt: VB[:, kt, :], all_rows, 0)
                        ready(h + 1, layer)
                pe_scores(pe, HEADS - 1, NT, scores, 0)
                pe_apply(pe, HEADS - 1, NT, lambda kt: VB[:, kt, :], all_rows, 0)

            @block.scalar
            def _(act):
                def values(h):
                    act_.activation(VB.rearrange("p a b -> p (a b)"), PB[:, 7, :], ACT.Copy)
                    act_roots(act, head, h + 2)
                    for j, bank in enumerate((0, 7, 0)):
                        s, n = side_slot(h, j, 1)
                        act.wait_ge(used[s].sem, used[s].at(n + 1))
                        act_.activation(ROW[:, j, :], PB[:, bank, :], ACT.Copy).then_inc(sig("drained").sem, 1)

                def squares(h):
                    act.wait_ge(used[0].sem, used[0].at(h + 2))
                    act_squares(head, 2)

                for s in range(3):
                    act.wait_ge(used[s].sem, used[s].at(1))
                act_squares(latents, 0)
                act_roots(act, latents, 0)
                act.wait_ge(sig("normed").sem, sig("normed").at(1))
                act_squares(rotary, 1)
                act_roots(act, rotary, 1)
                squares(0)
                values(0)
                with act.Fori(0, HEADS - 1) as h:
                    act_exps(act, h, NT, scale, psum_scores, 0)
                    act_turned(act, h, NT, 0)
                    squares(h + 1)
                    act_carry(act, h, NT, all_rows, OT[:, h, :], 0)
                    values(h + 1)
                act_exps(act, HEADS - 1, NT, scale, psum_scores, 0)
                act_turned(act, HEADS - 1, NT, 0)
                act_carry(act, HEADS - 1, NT, all_rows, OT[:, HEADS - 1, :], 0)

            @block.vector
            def _(dve):
                chain = Chain(dve, sig("dve_step"))
                dve_norms(dve, latents, 0)
                dve_norms(dve, rotary, 1)
                dve_ropes(dve, chain, turned_key, 0)
                assert chain.n == 1
                for layer in middle:
                    with dve.Fori(4 * layer - 4, 4 * layer) as h:
                        turn = Chain(dve, sig("dve_step"), h, each)
                        turn.n = 1
                        dve_norms(dve, head, h + 2)
                        dve.wait_ge(sig("mod_flipped").sem, sig("mod_flipped").at(3 * h + 3))
                        at = 12 * (h - 4 * layer + 4)
                        x = VEC["ada_b"][0] + 48 * layer
                        dve_.tensor_tensor(MODS[:, layer, bass.ds(at, 12), :],
                                           PB[:, 1, 0:24].rearrange("p (n w) -> p n w", w=2),
                                           V[:, bass.ds(at + x, 12)].unsqueeze(2).broadcast_to([P, 12, 2]), ALU.add)
                        dve_ropes(dve, turn, turned_query, h + 1)
                        dve_peaks(dve, turn, h, NT, scale, psum_scores, 0)
                        dve_shares(dve, turn, h, NT, 0)
                        assert turn.n == 1 + each
        for s in (1, 2, 3, 4):
            n = (1 + 2 * HEADS) if s < 3 else HEADS
            used[s].passed(n)
            loaded[s].passed(16 * n)
        used[0].passed(1 + HEADS)
        loaded[0].passed(16 + 32 * HEADS)
        passed(cleared=1, mod_flipped=3 * HEADS, drained=3 * HEADS, squared=HEADS + 2, summed=HEADS + 2, rooted=HEADS + 2, inverted=HEADS + 2, normed=HEADS + 2, rotated=HEADS + 1,
               roped=HEADS + 1, dve_step=1 + each * HEADS, **{n: HEADS for n in ATTEND})
        add_product(io["mla_w_o"][0], KD, lambda i: OT[:, i, :], gate_layer, 2, T)

    def even_mixer(layer):
        KG, VB, QP, U = own(0, 2), own(2 * T, NT, P), own(3 * T, 2), own(5 * T, NT)
        w_in = io["even_w_in_2"][0]
        scale = float(HD) ** -0.5
        keys = [([PB[:, g, :]], [KG[:, g, :]], [vec("a_k")], PB[:, 4 + g, :], PAIR, HD, P) for g in range(2)]
        turned_keys = [(KG[:, g, :], PB[:, 6 + g, :], P) for g in range(2)]
        queries = [([PB[:, j, :]], [QP[:, j, :]], [vec("a_q")], PB[:, 4 + j, :], PAIR, HD, P) for j in range(2)]
        turned_queries = [(QP[:, j, :], PB[:, 6 + j, :], P) for j in range(2)]
        MIX = own(0, 2)
        pool_w = SIL[:].rearrange("p a b -> p (a b)")[:, 0:4 * P].rearrange("p (g n) -> p g n", g=4)
        pools = con("pools").rearrange("p (g a t) -> p g a t", g=4, a=2)
        with nc.Block() as block:
            @block.sync
            def _(sp):
                for s, c in ((1, 2 * S), (2, 3 * S), (3, 4 * S)):
                    sp.dma_start(tile(s, KD, S), rows(w_in, c, c + S)).then_inc(loaded[s].sem, 16)
                for g in range(2):
                    sp.wait_ge(used[0].sem, used[0].at(g))
                    sp.dma_start(tile(0, KD, S), rows(w_in, g * S, (g + 1) * S)).then_inc(loaded[0].sem, 16)
                first_rows(sp, io["even_w_out_2"][0], 2)
                sp.wait_ge(sig("roped").sem, sig("roped").at(3))
                sp.dma_start(pool_w, io["pool_w_2"][0].rearrange("g c d -> c g d")).then_inc(sig("bias_in").sem, 16)

            @block.tensor
            def _(pe):
                pe.wait_ge(loaded[1].sem, loaded[1].at(16))
                w = tile(1, KD, S)
                for g in range(2):
                    for j in range(2):
                        for k in range(KD):
                            pe_.matmul(PB[j * HD:(j + 1) * HD, g, :], w[:, k, g * HD:(g + 1) * HD], A[:, k, :],
                                       start=k == 0, stop=k == KD - 1)
                for t in range(NT):
                    for k in range(KD):
                        last = pe_.matmul(PB[:, 2, t * P:(t + 1) * P], A[:, k, t * P:(t + 1) * P], w[:, k, P:2 * P],
                                          start=k == 0, stop=k == KD - 1)
                last.then_inc(used[1].sem, 1)
                pe_sums(pe, keys, 0)
                pe_turns(pe, turned_keys, 0, 0)
                pe.wait_ge(sig("roped").sem, sig("roped").at(1))
                for s in (2, 3):
                    pe.wait_ge(loaded[s].sem, loaded[s].at(16))
                    for t in range(NT):
                        for k in range(KD):
                            last = pe_.matmul(PB[:, 2 * s - 4 + t // 2, (t % 2) * S:(t % 2 + 1) * S],
                                              A[:, k, t * P:(t + 1) * P], tile(s, KD, S)[:, k, :],
                                              start=k == 0, stop=k == KD - 1)
                    last.then_inc(used[s].sem, 1)
                pe.wait_ge(sig("drained").sem, sig("drained").at(2))
                for g in range(2):
                    pe.wait_ge(loaded[0].sem, loaded[0].at(16 * (g + 1)))
                    if g:
                        pe.wait_ge(sig("carried").sem, sig("carried").at(4 * g))
                    for j in range(2):
                        for k in range(KD):
                            last = pe_.matmul(PB[:, j, :], tile(0, KD, S)[:, k, j * P:(j + 1) * P], A[:, k, :],
                                              start=k == 0, stop=k == KD - 1)
                    last.then_inc(used[0].sem, 1)
                    pe_sums(pe, queries, g + 1)
                    pe_turns(pe, turned_queries, g + 1, g + 1)
                    pe.wait_ge(sig("roped").sem, sig("roped").at(g + 2))
                    for j in range(2):
                        n = 4 * g + 2 * j
                        if j:
                            pe.wait_ge(sig("carried").sem, sig("carried").at(n))
                        for i in range(2):
                            r = slice(i * HD, (i + 1) * HD)
                            pe_scores(pe, n + i, NT, [(QP[r, j, :], KG[r, g, :])], i)
                        for i in range(2):
                            pe_apply(pe, n + i, NT, lambda kt: VB[:, kt, g * HD:(g + 1) * HD],
                                     slice(i * HD, (i + 1) * HD), i)
                pe.wait_ge(sig("carried").sem, sig("carried").at(8))
                pe.wait_ge(sig("bias_in").sem, sig("bias_in").at(16))
                for g in range(4):
                    if g >= 2:
                        pe.wait_ge(sig("mixed").sem, sig("mixed").at(g - 1))
                    for w in range(2):
                        for a in range(2):
                            last = pe_.matmul(PB[:, g % 2, half(w)], U[:, 2 * w + a, g * P:(g + 1) * P],
                                              pools[:, g, a, :], start=a == 0, stop=a == 1)
                    last.then_inc(sig("pooled").sem, 1)
                    pe.wait_ge(sig("pool_copied").sem, sig("pool_copied").at(g + 1))
                    pe_.matmul(PB[:, 2 + g % 2, :], pool_w[:, g, :], MIX[:, g % 2, :], start=True, stop=True) \
                        .then_inc(sig("projected").sem, 1)

            @block.scalar
            def _(act):
                act.wait_ge(used[1].sem, used[1].at(1))
                act_.activation(VB.rearrange("p a b -> p (a b)"), PB[:, 2, :], ACT.Copy)
                act_squares(keys, 0)
                act_roots(act, keys, 0)
                for s in (2, 3):
                    act.wait_ge(used[s].sem, used[s].at(1))
                    act_.activation(U[:, :, (s - 2) * S:(s - 1) * S],
                                    PB[:, 2 * s - 4:2 * s - 2, :].rearrange("p a (b c) -> p (a b) c", b=2),
                                    ACT.Copy).then_inc(sig("drained").sem, 1)
                for g in range(2):
                    act.wait_ge(used[0].sem, used[0].at(g + 1))
                    act_squares(queries, g + 1)
                    act_roots(act, queries, g + 1)
                    for j in range(2):
                        n = 4 * g + 2 * j
                        for i in range(2):
                            act_exps(act, n + i, NT, scale, psum_scores, i)
                        for i in range(2):
                            r = slice(i * HD, (i + 1) * HD)
                            act_turned(act, n + i, NT, i)
                            act_carry(act, n + i, NT, r, OT[r, 2 * g + j, :], i)
                for g in range(4):
                    act.wait_ge(sig("pooled").sem, sig("pooled").at(g + 1))
                    act_.activation(MIX[:, g % 2, :], PB[:, g % 2, :], ACT.Copy).then_inc(sig("pool_copied").sem, 1)
                    act.wait_ge(sig("projected").sem, sig("projected").at(g + 1))
                    act_.activation(OT[:, 4 + g, :], PB[:, 2 + g % 2, :], ACT.Copy, scale=vec("pool", g, g + 1)) \
                        .then_inc(sig("mixed").sem, 1)

            @block.vector
            def _(dve):
                chain = Chain(dve, sig("dve_step"))
                dve_norms(dve, keys, 0)
                dve_ropes(dve, chain, turned_keys, 0)
                for g in range(2):
                    dve_norms(dve, queries, g + 1)
                    dve_ropes(dve, chain, turned_queries, g + 1)
                    for n in range(4 * g, 4 * g + 4, 2):
                        for i in range(2):
                            dve_peaks(dve, chain, n + i, NT, scale, psum_scores, i)
                        for i in range(2):
                            dve_shares(dve, chain, n + i, NT, i)
        used[0].passed(2)
        loaded[0].passed(32)
        for s in (1, 2, 3):
            used[s].passed(1)
            loaded[s].passed(16)
        passed(squared=3, summed=3, rooted=3, inverted=3, normed=3, rotated=3, roped=3, drained=2, bias_in=16, pooled=4,
               pool_copied=4, projected=4, mixed=4, dve_step=3 + 2 * 8, **{n: 8 for n in ATTEND})
        add_product(io["even_w_out_2"][0], KD, lambda i: OT[:, i, :], layer, 2, T)

    def odd_mixer(layer):
        QB, KB, VB, SC, BI = own(0, 1, S), own(S, 1), own(S + T, NT, P), own(S + 2 * T, 4), own(S + 6 * T, 4)
        w_in = io["odd_w_in_2"][0]
        scale = float(HD) ** -0.5
        parts = [w_in[:, i * D:(i + 1) * D].rearrange("(k p) (m n) -> p m k n", p=P, n=P) for i in range(3)]
        bias = io["bias"].rearrange("(m h) q k -> q m h k", h=4)
        near = con("near")

        def biased(t, b):
            return SC[:, 2 * b + t, :]

        each = 4
        with nc.Block() as block:
            @block.sync
            def _(sp):
                with sp.Fori(0, KD) as m:
                    sp.wait_ge(used[0].sem, used[0].at(m))
                    for j in range(2):
                        sp.dma_start(tile(0, KD, P, j * D), parts[j][:, m]).then_inc(loaded[0].sem, 16)
                    sp.wait_ge(used[1].sem, used[1].at(m))
                    sp.dma_start(tile(1, KD, P), parts[2][:, m]).then_inc(loaded[1].sem, 16)
                    sp.wait_ge(sig("biased").sem, sig("biased").at(2 * m))
                    sp.dma_start(BI[:, :, 0:S], bias[:, m]).then_inc(sig("bias_in").sem, 16)
                first_rows(sp, io["odd_w_out_2"][0], KD)

            @block.tensor
            def _(pe):
                def project(m):
                    pe.wait_ge(loaded[0].sem, loaded[0].at(32 * (m + 1)))
                    for k in range(KD):
                        pe_.matmul(PB[:, 4, 0:S], tile(0, KD, P)[:, k, :], A[:, k, 0:S], start=k == 0, stop=k == KD - 1)
                    for k in range(KD):
                        last = pe_.matmul(PB[:, 5, :], tile(0, KD, P, D)[:, k, :], A[:, k, :],
                                          start=k == 0, stop=k == KD - 1)
                    last.then_inc(used[0].sem, 1)
                    pe.wait_ge(loaded[1].sem, loaded[1].at(16 * (m + 1)))
                    for t in range(NT):
                        for k in range(KD):
                            last = pe_.matmul(PB[:, 6, t * P:(t + 1) * P], A[:, k, t * P:(t + 1) * P],
                                              tile(1, KD, P)[:, k, :], start=k == 0, stop=k == KD - 1)
                    last.then_inc(used[1].sem, 1)

                def attend(m, more):
                    pe.wait_ge(sig("staged").sem, sig("staged").at(m + 1))
                    pe.wait_ge(sig("carried").sem, sig("carried").at(2 * m))
                    for i in range(2):
                        r = slice(i * HD, (i + 1) * HD)
                        pe_scores(pe, 2 * m + i, 2, [(QB[r], KB[r])], i)
                    if more:
                        project(m + 1)
                    for i in range(2):
                        r = slice(i * HD, (i + 1) * HD)
                        pe_apply(pe, 2 * m + i, 2, lambda kt: VB[:, kt, r], r, i)

                project(0)
                with pe.Fori(0, KD - 1) as m:
                    attend(m, True)
                attend(KD - 1, False)

            @block.scalar
            def _(act):
                with act.Fori(0, KD) as m:
                    act.wait_ge(used[0].sem, used[0].at(m + 1))
                    act_.activation(QB, PB[:, 4, 0:S], ACT.Copy)
                    act_.activation(KB, PB[:, 5, :], ACT.Copy)
                    act.wait_ge(used[1].sem, used[1].at(m + 1))
                    act_.activation(VB.rearrange("p a b -> p (a b)"), PB[:, 6, :], ACT.Copy) \
                        .then_inc(sig("staged").sem, 1)
                    for i in range(2):
                        act_exps(act, 2 * m + i, 2, 1.0, biased, i)
                    for i in range(2):
                        r = slice(i * HD, (i + 1) * HD)
                        act_turned(act, 2 * m + i, 2, i)
                        act_carry(act, 2 * m + i, 2, r, OT[r, m, 0:S], i)

            @block.vector
            def _(dve):
                with dve.Fori(0, KD) as m:
                    chain = Chain(dve, sig("dve_step"), m, each)
                    dve.wait_ge(sig("bias_in").sem, sig("bias_in").at(16 * (m + 1)))
                    for i in range(2):
                        n = 2 * m + i
                        for t in range(2):
                            last = dve_.tensor_tensor(BI[:, 2 * i + t, 0:S], BI[:, 2 * i + t, 0:S], near, ALU.add)
                        last.then_inc(sig("act_step").sem, 1)
                        dve.wait_ge(sig("act_step").sem, sig("act_step").at(n + 1))
                        dve.wait_ge(sig("scored").sem, sig("scored").at(n + 1))
                        for t in range(2):
                            dve_.scalar_tensor_tensor(out=SC[:, 2 * i + t, 0:S], in0=PB[:, 2 * i + t, 0:S], scalar=scale,
                                                      in1=BI[:, 2 * i + t, 0:S], op0=ALU.mult, op1=ALU.add)
                            last = dve_.tensor_scalar(SC[:, 2 * i + t, S:T], PB[:, 2 * i + t, S:T], scale, None, ALU.mult)
                        last.then_inc(sig("biased").sem, 1)
                        dve.wait_ge(sig("biased").sem, sig("biased").at(n + 1))
                        dve_peaks(dve, chain, n, 2, 1.0, biased, i)
                    for i in range(2):
                        dve_shares(dve, chain, 2 * m + i, 2, i)
                    assert chain.n == each
        used[0].passed(KD)
        used[1].passed(KD)
        loaded[0].passed(32 * KD)
        loaded[1].passed(16 * KD)
        passed(biased=2 * KD, bias_in=16 * KD, staged=KD, act_step=2 * KD, dve_step=each * KD,
               **{n: 2 * KD for n in ATTEND})
        add_product(io["odd_w_out_2"][0], KD, lambda i: OT[:, i, 0:S], layer, 2, S)

    def hgrn2(layer):
        OTH = BIG[:, 0:KD * S].rearrange("p (k t) -> p k t", t=S)
        at = [KD * S]

        def take(k, n):
            a = BIG[:, at[0]:at[0] + k * n]
            at[0] += k * n
            return a if k == 1 else a.rearrange("p (k n) -> p k n", k=k)

        QS, SG, VB, KK, LF, CUM, EX = (take(1, S), take(1, S), take(NT, P), take(2, T), take(2, T), take(1, T),
                                       take(1, T))
        KX, KXT, ST, QI, KE, MP = take(1, S), take(2, P), take(2, P), take(2, S), take(LEVELS, S), take(1, 2 * T)
        LV = WORK[:, 0:LEVELS * S].rearrange("p (l t) -> p l t", l=LEVELS)
        QE = WORK[:, LEVELS * S:2 * LEVELS * S].rearrange("p (l t) -> p l t", l=LEVELS)
        AT = SIL[:].rearrange("p d (a t) -> p d a t", a=2)
        LB = SMALL[:, 0:2 * KD].rearrange("p (d k) -> p d k", d=2)
        OLB = SMALL[:, 2 * KD:4 * KD].rearrange("p (d k) -> p d k", d=2)
        LBD = SMALL[:, 4 * KD:6 * KD]
        flat = "p a b -> p (a b)"
        masks = con("decay").rearrange("p (d m) -> p d m", d=2)
        w_in = io["hg_w_in"][0].rearrange("(k p) (i h n) -> p i h k n", p=P, i=5, n=P)
        read = [([PB[:, 7, 0:S]], [EX[:, 0:S]], [vec("hg_o")], PB[:, 7, S:T], ONES, P, P)]
        lb = vec("hg_lb")
        ROW = MORE[:, 0:2 * T].rearrange("p (j t) -> p j t", j=2)
        sides = 6

        def side_slot(h, j, a):
            s = 3 + 2 * j + a
            return s, (tile(s, 4, T) if s < SLOTS else MORE[:, SLOT:2 * SLOT].rearrange("p (k n) -> p k n", k=4))

        each = 8
        with nc.Block() as block:
            @block.sync
            def _(sp):
                chunk = io["ada_w_2"][1].rearrange("(a k p) (n c) -> p n a k c", a=2, p=P, c=T)

                def weights(h):
                    for s, parts in ((0, (0, 1)), (1, (2, 3)), (2, (4,))):
                        sp.wait_ge(used[s].sem, used[s].at(h))
                        for j, i in enumerate(parts):
                            sp.dma_start(tile(s, KD, P, j * D), w_in[:, i, h]).then_inc(loaded[s].sem, 16)

                weights(0)
                with sp.Fori(0, sides) as h:
                    for j in range(2):
                        for a in range(2):
                            s, dst = side_slot(h, j, a)
                            sp.wait_ge(used[s].sem, used[s].at(h))
                            sp.dma_start(dst, chunk[:, 2 * h + j, a]).then_inc(loaded[s].sem, 16)
                    weights(h + 1)
                weights(HEADS - 1)
                first_rows(sp, io["hg_w_o"][0], HEADS)

            @block.tensor
            def _(pe):
                def by_feature(dst, w, t):
                    for k in range(KD):
                        last = pe_.matmul(dst, w[:, k, :], A[:, k, 0:t], start=k == 0, stop=k == KD - 1)
                    return last

                def project_first(h):
                    pe.wait_ge(loaded[0].sem, loaded[0].at(32 * (h + 1)))
                    by_feature(PB[:, 0, 0:S], tile(0, KD, P), S)
                    by_feature(PB[:, 1, :], tile(0, KD, P, D), T).then_inc(used[0].sem, 1)

                def project_rest(h):
                    pe.wait_ge(loaded[1].sem, loaded[1].at(32 * (h + 1)))
                    by_feature(PB[:, 2, :], tile(1, KD, P), T)
                    for t in range(NT):
                        for k in range(KD):
                            last = pe_.matmul(PB[:, 3, t * P:(t + 1) * P], A[:, k, t * P:(t + 1) * P],
                                              tile(1, KD, P, D)[:, k, :], start=k == 0, stop=k == KD - 1)
                    last.then_inc(used[1].sem, 1)
                    pe.wait_ge(loaded[2].sem, loaded[2].at(16 * (h + 1)))
                    by_feature(PB[:, 0, S:T], tile(2, KD, P), S).then_inc(used[2].sem, 1)

                def side(h):
                    for j in range(2):
                        for a in range(2):
                            s, w = side_slot(h, j, a)
                            pe.wait_ge(loaded[s].sem, loaded[s].at(16 * (h + 1)))
                            for k in range(4):
                                last = pe_.matmul(PB[32 * k:32 * k + 32, 4 + j, :], CS[:, 1, 4 * a + k, :],
                                                  w[:, k, :], start=a == 0, stop=a == 1)
                            last.then_inc(used[s].sem, 1)
                    for j in range(2):
                        pe.wait_ge(sig("drained").sem, sig("drained").at(2 * h + j + 1))
                        for m in range(4):
                            last = pe_.matmul(PB[:, 6, 8 * j + 2 * m:8 * j + 2 * m + 2], ROW[:, j, m * P:(m + 1) * P],
                                              con("stream"), start=True, stop=True)
                        last.then_inc(sig("mod_flipped").sem, 1)

                def head(h, more, beside):
                    if more:
                        pe.wait_ge(sig("gated").sem, sig("gated").at(h + 1))
                        project_first(h + 1)
                    for d in range(2):
                        n = 2 * h + d
                        pe.wait_ge(sig("decayed").sem, sig("decayed").at(n + 1))
                        for a in range(2):
                            last = pe_.transpose(PB[:, 6, a * P:(a + 1) * P], KX[:, a * P:(a + 1) * P], IDENT)
                        last.then_inc(sig("kx_flipped").sem, 1)
                        pe.wait_ge(sig("kx_copied").sem, sig("kx_copied").at(n + 1))
                        for a in range(2):
                            last = pe_.matmul(PB[:, 6, S:S + P], KXT[:, a, :], VB[:, 2 + a, :], start=a == 0, stop=a == 1)
                        last.then_inc(sig("state_made").sem, 1)
                        pe.wait_ge(sig("levels_ready").sem, sig("levels_ready").at(n + 1))
                        for a in range(2):
                            c = slice(a * P, (a + 1) * P)
                            if a:
                                pe.wait_ge(sig("routed").sem, sig("routed").at(n + 1))
                            for l in range(LEVELS):
                                lhs, rhs = (KE[:, l + 1, c], QE[:, l + 1, c]) if l < LEVELS - 1 else (KK[:, d, c], QS[:, c])
                                last = pe_.matmul(PB[:, 4 + l // 4, (l % 4) * P:(l % 4 + 1) * P], lhs, rhs,
                                                  start=True, stop=True)
                            if a == 0:
                                last.then_inc(sig("products").sem, 1)
                        pe.wait_ge(sig("state_copied").sem, sig("state_copied").at(n + 1))
                        early, late = slice(d * P, (d + 1) * P), slice((1 - d) * P, (2 - d) * P)
                        pe_.matmul(PB[:, 6, S + P:T], KE[:, 0, early], QE[:, 0, late], start=True, stop=True) \
                            .then_inc(sig("products").sem, 1)
                        if d == 0 and more:
                            project_rest(h + 1)
                        if d == 0:
                            pe.wait_ge(sig("read_out").sem, sig("read_out").at(h))
                        pe_.matmul(PB[:, 7, 0:S], ST[:, d, :], QI[:, d, :], start=d == 0, stop=False)
                        pe.wait_ge(sig("attended").sem, sig("attended").at(n + 1))
                        pe_.matmul(PB[:, 7, 0:S], VB[:, d, :], AT[:, d, d, :], start=False, stop=False)
                        o = slice((1 - d) * P, (2 - d) * P)
                        last = pe_.matmul(PB[:, 7, o], VB[:, 1 - d, :], AT[:, d, 1 - d, o], start=False, stop=d == 1)
                    last.then_inc(sig("summed_up").sem, 1)
                    pe_sums(pe, read, h)
                    if beside:
                        side(h)

                project_first(0)
                project_rest(0)
                with pe.Fori(0, sides) as h:
                    head(h, True, True)
                head(HEADS - 2, True, False)
                head(HEADS - 1, False, False)

            @block.scalar
            def _(act):
                act.wait_ge(sig("act_step").sem, sig("act_step").at(1))
                act_.activation(SMALL[:, 0:2 * KD], LBD, ACT.Sigmoid)
                act_.activation(SMALL[:, 2 * KD:4 * KD], LBD, ACT.Sigmoid, scale=-1.0).then_inc(sig("staged").sem, 1)

                def head(h, beside):
                    act.wait_ge(used[2].sem, used[2].at(h + 1))
                    act.wait_ge(sig("read_out").sem, sig("read_out").at(h))
                    act_.activation(QS, PB[:, 0, 0:S], ACT.Copy)
                    act_.activation(VB.rearrange(flat), PB[:, 3, :], ACT.Copy)
                    act_.activation(SG, PB[:, 0, S:T], ACT.Silu)
                    z = PB[:, 1:3, :]
                    act_.activation(LF, z, ACT.Sigmoid)
                    act_.activation(KK, z, ACT.Sigmoid, scale=-1.0).then_inc(sig("gated").sem, 1)
                    act.wait_ge(sig("forgot").sem, sig("forgot").at(h + 1))
                    act_.activation(LF, LF, ACT.Ln).then_inc(sig("logged").sem, 1)
                    for d in range(2):
                        n = 2 * h + d
                        act.wait_ge(sig("spread").sem, sig("spread").at(n + 1))
                        sign = -1.0 if d == 0 else 1.0
                        lat = dict(scale=1.0) if d == 0 else dict(scale=-1.0, bias=ROOT[:, 1, 0:1])
                        ctx = dict(scale=-1.0, bias=ROOT[:, 1, 1:2]) if d == 0 else dict(scale=1.0)
                        act_.activation(EX[:, 0:S], CUM[:, 0:S], ACT.Exp, **lat)
                        act_.activation(EX[:, S:T], CUM[:, S:T], ACT.Exp, **ctx).then_inc(sig("exped").sem, 1)
                        act.wait_ge(sig("levelled").sem, sig("levelled").at(n + 1))
                        act_.activation(LV, LV, ACT.Abs).then_inc(sig("absed").sem, 1)
                        act.wait_ge(sig("absed").sem, sig("absed").at(n + 1))
                        act_.activation(LV, LV, ACT.Exp, scale=-1.0).then_inc(sig("group_exped").sem, 1)
                        act.wait_ge(sig("kx_flipped").sem, sig("kx_flipped").at(n + 1))
                        act_.activation(KXT.rearrange(flat), PB[:, 6, 0:S], ACT.Copy).then_inc(sig("kx_copied").sem, 1)
                        act.wait_ge(sig("state_made").sem, sig("state_made").at(n + 1))
                        act_.activation(ST[:, d, :], PB[:, 6, S:S + P], ACT.Copy).then_inc(sig("state_copied").sem, 1)
                    act.wait_ge(sig("summed_up").sem, sig("summed_up").at(h + 1))
                    act_squares(read, h)
                    act_roots(act, read, h)
                    if beside:
                        for j in range(2):
                            s, _ = side_slot(h, j, 1)
                            act.wait_ge(used[s].sem, used[s].at(h + 1))
                            act_.activation(ROW[:, j, :], PB[:, 4 + j, :], ACT.Copy).then_inc(sig("drained").sem, 1)

                with act.Fori(0, sides) as h:
                    head(h, True)
                with act.Fori(sides, HEADS) as h:
                    head(h, False)

            @block.vector
            def _(dve):
                dve_.tensor_tensor(LBD, lb[:, 2 * KD:4 * KD], lb[:, 0:2 * KD], ALU.subtract) \
                    .then_inc(sig("act_step").sem, 1)
                dve.wait_ge(sig("staged").sem, sig("staged").at(1))
                dve_.memset(ROOT[:, 2, :], 1.0).then_inc(sig("added").sem, 1)
                dve.wait_ge(sig("added").sem, sig("added").at(1))

                def head(h, beside):
                    chain = Chain(dve, sig("dve_step"), h, each)
                    dve.wait_ge(sig("gated").sem, sig("gated").at(h + 1))
                    for d in range(2):
                        dve_.tensor_scalar(LF[:, d, :], LF[:, d, :], OLB[:, d, bass.ds(h, 1)], LB[:, d, bass.ds(h, 1)],
                                           ALU.mult, ALU.add)
                        last = dve_.tensor_scalar(KK[:, d, :], KK[:, d, :], OLB[:, d, bass.ds(h, 1)], None, ALU.mult)
                    chain(last)
                    dve_.tensor_scalar(LF, LF, 1.0e-19, None, ALU.max).then_inc(sig("forgot").sem, 1)
                    dve.wait_ge(sig("logged").sem, sig("logged").at(h + 1))

                    def levels(d):
                        n = 2 * h + d
                        for w in range(2):
                            last = dve_.tensor_tensor_scan(CUM[:, half(w)], ROOT[:, 2, 0:S], LF[:, d, half(w)], 0.0,
                                                           ALU.mult, ALU.add)
                        chain(last)
                        last = dve_.tensor_copy(ROOT[:, 1, 0:2], CUM.rearrange("p (w t) -> p w t", w=2)[:, :, S - 1])
                        if d == 1:
                            chain(last)
                            last = dve_.tensor_tensor(CUM, CUM, LF[:, 1, :], ALU.subtract)
                        last.then_inc(sig("spread").sem, 1)
                        dve.wait_ge(sig("spread").sem, sig("spread").at(n + 1))
                        for l in range(LEVELS):
                            w = P >> l
                            b = CUM[:, 0:S].rearrange("p (b w) -> p b w", w=2 * w)
                            mid = b[:, :, w - 1:w].broadcast_to([P, P // w, 2 * w])
                            last = dve_.tensor_tensor(LV[:, l, :].rearrange("p (b w) -> p b w", w=2 * w), b, mid,
                                                      ALU.subtract)
                        last.then_inc(sig("levelled").sem, 1)

                    def decay(d):
                        n = 2 * h + d
                        dve.wait_ge(sig("exped").sem, sig("exped").at(n + 1))
                        dve_.tensor_tensor(KX, KK[:, d, S:T], EX[:, S:T], ALU.mult)
                        dve_.tensor_tensor(QI[:, d, :], QS, EX[:, 0:S], ALU.mult).then_inc(sig("decayed").sem, 1)
                        dve.wait_ge(sig("group_exped").sem, sig("group_exped").at(n + 1))
                        dve_.tensor_tensor(QE, LV, QS.unsqueeze(1).broadcast_to([P, LEVELS, S]), ALU.mult)
                        dve_.tensor_tensor(KE, LV, KK[:, d, 0:S].unsqueeze(1).broadcast_to([P, LEVELS, S]), ALU.mult) \
                            .then_inc(sig("levels_ready").sem, 1)

                    def mask(d):
                        n = 2 * h + d
                        for a in range(2):
                            dve.wait_ge(sig("products").sem, sig("products").at(2 * n + a + 1))
                            chain(dve_.tensor_tensor(MP, PB[:, 4:6, :].rearrange(flat), masks[:, d, :], ALU.mult))
                            last = dve_.tensor_reduce(AT[:, d, a, a * P:(a + 1) * P],
                                                      MP.rearrange("p (l t) -> p t l", l=LEVELS), AX.X, ALU.add)
                            if a == 0:
                                last.then_inc(sig("routed").sem, 1)
                                dve.wait_ge(sig("routed").sem, sig("routed").at(n + 1))
                        dve_.tensor_copy(AT[:, d, d, (1 - d) * P:(2 - d) * P], PB[:, 6, S + P:T]) \
                            .then_inc(sig("attended").sem, 1)

                    levels(0)
                    decay(0)
                    dve.wait_ge(sig("levels_ready").sem, sig("levels_ready").at(2 * h + 1))
                    levels(1)
                    mask(0)
                    decay(1)
                    mask(1)
                    dve_norms(dve, read, h)
                    dve.wait_ge(sig("normed").sem, sig("normed").at(h + 1))
                    dve_.tensor_tensor(OTH[:, h, :], EX[:, 0:S], SG, ALU.mult).then_inc(sig("read_out").sem, 1)
                    assert chain.n == each, chain.n
                    if beside:
                        dve.wait_ge(sig("mod_flipped").sem, sig("mod_flipped").at(2 * h + 2))
                        dve_.tensor_tensor(MODS[:, 3, bass.ds(8 * h, 8), :],
                                           PB[:, 6, 0:16].rearrange("p (n w) -> p n w", w=2),
                                           V[:, bass.ds(8 * h + VEC["ada_b"][0] + 3 * 48, 8)].unsqueeze(2)
                                           .broadcast_to([P, 8, 2]), ALU.add)

                with dve.Fori(0, sides) as h:
                    head(h, True)
                with dve.Fori(sides, HEADS) as h:
                    head(h, False)
        for s in range(3):
            used[s].passed(HEADS)
            loaded[s].passed((32, 32, 16)[s] * HEADS)
        for s in range(3, SLOTS + 1):
            used[s].passed(sides)
            loaded[s].passed(16 * sides)
        n = HEADS
        passed(drained=2 * sides, mod_flipped=2 * sides, read_out=n, decayed=2 * n, kx_flipped=2 * n, kx_copied=2 * n, state_made=2 * n, levels_ready=2 * n,
               products=4 * n, state_copied=2 * n, attended=2 * n, summed_up=n, summed=n, act_step=1, staged=1,
               gated=n, forgot=n, logged=n, spread=2 * n, exped=2 * n, levelled=2 * n, group_exped=2 * n, squared=n,
               rooted=n, inverted=n, added=1, normed=n, routed=2 * n, absed=2 * n, dve_step=n * each)
        add_product(io["hg_w_o"][0], KD, lambda i: OTH[:, i, :], layer, 2, S)

    def experts(layer, moe, t):
        nt, streams = t // P, t // S
        ATK = BIG[:, 0:NT * D].rearrange("p (a n) -> p a n", a=NT)
        o = NT * D

        def take(n):
            nonlocal o
            o += n
            assert o <= FB * T
            return BIG[:, o - n:o]

        XGS = take(D)
        XGT = take(2 * D).rearrange("p (b k c) -> p b k c", b=2, k=KD)
        HS = take(2 * DE).rearrange("p (j n) -> p j n", j=2)
        HB = take(8 * CAP).rearrange("p (j k c) -> p j k c", j=2, k=4)
        Y2 = take(D)
        SWT = take(T)
        SEL = WORK[:, 0:NT * P].rearrange("p (a c) -> p a c", a=NT)
        SELW = WORK[:, NT * P:2 * NT * P].rearrange("p (a c) -> p a c", a=NT)
        W36 = SIL[:].rearrange("p a b -> p (a b)")[:, 0:KD * NR].rearrange("p (k n) -> p k n", n=NR)
        free = [2 * NT * P]

        def small(*shape):
            n = int(np.prod(shape))
            a = WORK[:, free[0]:free[0] + n]
            free[0] += n
            if len(shape) == 2:
                return a.rearrange("p (a b) -> p a b", a=shape[0])
            if len(shape) == 3:
                return a.rearrange("p (a b c) -> p a b c", a=shape[0], b=shape[1])
            return a

        LG, GS, G1, GW = small(nt, NR), small(nt, NG), small(nt, NG), small(nt, 1)
        M1, M2, E2 = small(nt, 1), small(nt, 1), small(nt, 1)
        PI, LE, LE2, O1, O2 = small(nt, EPG), small(nt, EPG), small(nt, EPG), small(nt, EPG), small(nt, EPG)
        WIDE, MEM, WT, RK = small(nt, NG, EPG), small(nt, NG, EPG), small(nt, NG, EPG), small(nt, NE + 4)
        CNT, NRF = small(1), small(8)
        EXPO = small(nt, NG)

        router_steps = 34

        def wide(x, shape, axis):
            return x.unsqueeze(axis).broadcast_to([P] + shape)

        def across(x, n):
            return x.broadcast_to([P, nt, n])

        with nc.Block() as block:
            @block.sync
            def _(sp):
                sp.dma_start(W36, io["router"][moe].rearrange("(k p) n -> p k n", p=P)).then_inc(sig("bias_in").sem, 16)

            @block.tensor
            def _(pe):
                pe.wait_ge(sig("bias_in").sem, sig("bias_in").at(16))
                for a in range(nt):
                    for k in range(KD):
                        last = pe_.matmul(PB[:, 0, a * NR:(a + 1) * NR], A[:, k, a * P:(a + 1) * P], W36[:, k, :],
                                          start=k == 0, stop=k == KD - 1)
                last.then_inc(sig("projected").sem, 1)
                for a in range(nt):
                    if a >= 2:
                        pe.wait_ge(sig("token_copied").sem, sig("token_copied").at(a - 1))
                    for k in range(KD):
                        last = pe_.transpose(PB[:, 2 + 2 * (a % 2) + k // 4, (k % 4) * P:(k % 4 + 1) * P],
                                             A[:, k, a * P:(a + 1) * P], IDENT)
                    last.then_inc(sig("token_flipped").sem, 1)
                pe.wait_ge(sig("routed").sem, sig("routed").at(1))
                for a in range(nt):
                    for b in range(a + 1):
                        pe_.matmul(PB[:, 1, a * NE:(a + 1) * NE], TRI if b == a else ONES,
                                   MEM[:, b].rearrange("p a b -> p (a b)"), start=b == 0, stop=b == a)
                for b in range(nt):
                    last = pe_.matmul(PB[:, 1, NT * NE:(NT + 1) * NE], ONES, MEM[:, b].rearrange("p a b -> p (a b)"),
                                      start=b == 0, stop=b == nt - 1)
                last.then_inc(sig("ranked").sem, 1)

            @block.scalar
            def _(act):
                for a in range(nt):
                    act.wait_ge(sig("token_flipped").sem, sig("token_flipped").at(a + 1))
                    act_.activation(ATK[:, a, :], PB[:, 2 + 2 * (a % 2):4 + 2 * (a % 2), :].rearrange("p a b -> p (a b)"),
                                    ACT.Copy).then_inc(sig("token_copied").sem, 1)
                act.wait_ge(sig("peaked").sem, sig("peaked").at(1))
                act_.activation(EXPO, EXPO, ACT.Exp).then_inc(sig("group_exped").sem, 1)
                act.wait_ge(sig("picked").sem, sig("picked").at(1))
                act_.activation(E2, E2, ACT.Exp).then_inc(sig("second_exped").sem, 1)

            @block.vector
            def _(dve):
                c = Chain(dve, sig("dve_step"))
                dve.wait_ge(sig("projected").sem, sig("projected").at(1))
                bias = vec("moe_b", moe * NR, (moe + 1) * NR).unsqueeze(1).broadcast_to([P, nt, NR])
                c(dve_.tensor_tensor(LG, PB[:, 0, 0:nt * NR].rearrange("p (a n) -> p a n", a=nt), bias, ALU.add))
                G, L = LG[:, :, 0:NG], LG[:, :, NG:NR].rearrange("p a (g e) -> p a g e", g=NG)
                prior = con("prior").unsqueeze(1).broadcast_to([P, nt, EPG])

                def first_of(src, top, dst, n):
                    c(dve_.tensor_reduce(top, src, AX.X, ALU.max))
                    c(dve_.tensor_tensor(PI[:, :, 0:n], src, across(top, n), ALU.is_equal))
                    c(dve_.tensor_tensor(PI[:, :, 0:n], PI[:, :, 0:n], prior[:, :, 0:n], ALU.mult))
                    c(dve_.tensor_reduce(GS[:, :, 0:1], PI[:, :, 0:n], AX.X, ALU.max))
                    c(dve_.tensor_tensor(dst, PI[:, :, 0:n], across(GS[:, :, 0:1], n), ALU.is_equal))

                first_of(G, M1, G1, NG)
                dve_.tensor_tensor(EXPO, G, across(M1, NG), ALU.subtract).then_inc(sig("peaked").sem, 1)
                dve.wait_ge(sig("group_exped").sem, sig("group_exped").at(1))
                c(dve_.tensor_reduce(GW, EXPO, AX.X, ALU.add))
                c(dve_.reciprocal(GW, GW))
                full = [nt, NG, EPG]
                c(dve_.tensor_tensor(WIDE, L, wide(G1, full, 3), ALU.mult))
                c(dve_.tensor_reduce(LE, WIDE.rearrange("p a g e -> p a e g"), AX.X, ALU.add))
                first_of(LE, M1, O1, EPG)
                c(dve_.scalar_tensor_tensor(out=LE2, in0=O1, scalar=NEG, in1=LE, op0=ALU.mult, op1=ALU.add))
                first_of(LE2, M2, O2, EPG)
                dve_.tensor_tensor(E2, M2, M1, ALU.subtract).then_inc(sig("picked").sem, 1)
                dve.wait_ge(sig("second_exped").sem, sig("second_exped").at(1))
                c(dve_.tensor_scalar(M1, E2, 1.0, None, ALU.add))
                c(dve_.reciprocal(M1, M1))
                c(dve_.tensor_tensor(M1, M1, GW, ALU.mult))
                c(dve_.tensor_tensor(M2, M1, E2, ALU.mult))
                c(dve_.tensor_tensor(LE, O1, across(M1, EPG), ALU.mult))
                c(dve_.tensor_tensor(LE2, O2, across(M2, EPG), ALU.mult))
                c(dve_.tensor_tensor(LE, LE, LE2, ALU.add))
                c(dve_.tensor_tensor(O1, O1, O2, ALU.add))
                for g in range(NG):
                    dve_.tensor_tensor(WT[:, :, g, :], LE, across(G1[:, :, g:g + 1], EPG), ALU.mult)
                    last = dve_.tensor_tensor(MEM[:, :, g, :], O1, across(G1[:, :, g:g + 1], EPG), ALU.mult)
                last.then_inc(sig("routed").sem, 1)
                dve.wait_ge(sig("routed").sem, sig("routed").at(1))
                flat = MEM.rearrange("p a g e -> p a (g e)")
                c(dve_.tensor_scalar(WIDE, MEM, -FAR, FAR, ALU.mult, ALU.add))
                dve.wait_ge(sig("ranked").sem, sig("ranked").at(1))
                c(dve_.tensor_reduce(CNT, PB[:, 1, NT * NE:(NT + 1) * NE], AX.X, ALU.max))
                c(dve_.tensor_scalar(NRF, con("rounds"), CNT, None, ALU.is_lt))
                c(dve_.tensor_reduce(CNT, NRF, AX.X, ALU.add))
                dve_.tensor_copy(ROUNDS[:], CNT[0:1])
                c(dve_.tensor_tensor(RK[:, :, 0:NE], PB[:, 1, 0:nt * NE].rearrange("p (a n) -> p a n", a=nt),
                                     WIDE.rearrange("p a g e -> p a (g e)"), ALU.add))
                dve_.tensor_scalar(RK[:, :, NE:NE + 4], RK[:, :, 0:4], -float(CAP), None, ALU.add) \
                    .then_inc(sig("rank_in").sem, 1)
                assert c.n == router_steps, c.n
        passed(bias_in=16, projected=1, token_flipped=nt, token_copied=nt, routed=1, ranked=1, peaked=1,
               group_exped=1, picked=1, second_exped=1, dve_step=router_steps, rank_in=1)

        w1, w3 = (io[n][moe].rearrange("e (a k p) c -> e p a k c", a=2, p=P) for n in ("moe_w1_2", "moe_w3_2"))
        w2 = io["moe_w2_2"][moe].rearrange("e (a k p) c -> e p a k c", k=2, p=P)
        WTF = WT.rearrange("p a g e -> p a (g e)")
        pairs = NE // 2

        with nc.Block() as block:
            def rounds(eng):
                return eng.value_load(ROUNDS[0:1, 0:1], min_val=1, max_val=t // CAP)

            def slots_of(j):
                return slice(j * CAP, (j + 1) * CAP)

            @block.gpsimd
            def _(pool):
                nc.gpsimd.memset(A[:], 0.0).then_inc(sig("cleared").sem, 1)
                nc.gpsimd.memset(Y2, 0.0).then_inc(sig("cleared").sem, 1)
                nc.gpsimd.memset(SWT, 0.0).then_inc(sig("cleared").sem, 1)

            @block.sync
            def _(sp):
                with sp.Fori(0, rounds(sp)) as r, sp.Fori(0, pairs) as i:
                    for j in range(2):
                        n = 2 * (pairs * r + i) + j
                        for s, src in enumerate((w1, w3, w1, w3, w2, w2)):
                            sp.wait_ge(used[s].sem, used[s].at(n))
                            dst = tile(s, 4, T) if s < 4 else tile(s, 2, D)
                            sp.dma_start(dst, src[2 * i + j, :, s // 2 if s < 4 else s - 4]).then_inc(loaded[s].sem, 16)

            @block.tensor
            def _(pe):
                def gather(g):
                    pe.wait_ge(sig("picked").sem, sig("picked").at(g + 1))
                    for a in range(nt):
                        for m in range(2):
                            last = pe_.matmul(PB[:, 4 + m, :], SEL[:, a, :], ATK[:, a, m * T:(m + 1) * T],
                                              start=a == 0, stop=a == nt - 1)
                    last.then_inc(sig("gathered").sem, 1)

                def turn_gathered(g):
                    pe.wait_ge(sig("gather_copied").sem, sig("gather_copied").at(g + 1))
                    for k in range(KD):
                        last = pe_.transpose(PB[:, 4 + k // 4, (k % 4) * P:(k % 4 + 1) * P], XGS[:, k * P:(k + 1) * P],
                                             IDENT)
                    last.then_inc(sig("xg_flipped").sem, 1)

                def hidden(n, j, b):
                    pe.wait_ge(sig("expert_h").sem, sig("expert_h").at(n))
                    for k in range(KD):
                        for m in range(2):
                            s = 2 * (k // 4) + m
                            if k % 4 == 0:
                                pe.wait_ge(loaded[s].sem, loaded[s].at(16 * (n + 1)))
                            last = pe_.matmul(PB[m * CAP:(m + 1) * CAP, 0, :], XGT[:, b, k, slots_of(j)],
                                              tile(s, 4, T)[:, k % 4, :], start=k == 0, stop=k == KD - 1)
                            if k % 4 == 3:
                                last.then_inc(used[s].sem, 1)

                def turn_hidden(n, j):
                    pe.wait_ge(sig("expert_h").sem, sig("expert_h").at(n + 1))
                    for k in range(4):
                        last = pe_.transpose(PB[:, 1, k * P:(k + 1) * P], HS[:, j, k * P:(k + 1) * P], IDENT)
                    last.then_inc(sig("h_flipped").sem, 1)

                def outputs(n, j):
                    pe.wait_ge(sig("h_copied").sem, sig("h_copied").at(n + 1))
                    pe.wait_ge(sig("y_copied").sem, sig("y_copied").at(n))
                    for k in range(4):
                        s = 4 + k // 2
                        if k % 2 == 0:
                            pe.wait_ge(loaded[s].sem, loaded[s].at(16 * (n + 1)))
                        for m in range(2):
                            last = pe_.matmul(PB[m * CAP:(m + 1) * CAP, 2, :], HB[:, j, k, :],
                                              tile(s, 2, D)[:, k % 2, m * T:(m + 1) * T], start=k == 0, stop=k == 3)
                        if k % 2:
                            last.then_inc(used[s].sem, 1)

                def scatter(g):
                    pe.wait_ge(sig("y_copied").sem, sig("y_copied").at(2 * g))
                    pe.wait_ge(sig("pick_copied").sem, sig("pick_copied").at(g))
                    for m in range(KD):
                        pe.wait_ge(sig("added").sem, sig("added").at(KD * g + m - 1))
                        pe_.matmul(PB[:, 6 + m % 2, 0:t], Y2[:, m * P:(m + 1) * P], SWT[:, 0:t], start=True, stop=True) \
                            .then_inc(sig("scattered").sem, 1)

                pe.wait_ge(sig("cleared").sem, sig("cleared").at(3))
                gather(0)
                turn_gathered(0)
                every = rounds(pe)
                with pe.Fori(0, every) as r, pe.Fori(0, pairs // 2) as i:
                    for b in range(2):
                        g = pairs * r + 2 * i + b
                        pe.wait_ge(sig("xg_copied").sem, sig("xg_copied").at(g + 1))
                        hidden(2 * g, 0, b)
                        scatter(g)
                        turn_hidden(2 * g, 0)
                        gather(g + 1)
                        outputs(2 * g, 0)
                        hidden(2 * g + 1, 1, b)
                        turn_gathered(g + 1)
                        pe.wait_ge(sig("weighed").sem, sig("weighed").at(g + 1))
                        for a in range(nt):
                            last = pe_.transpose(PB[:, 3, a * P:(a + 1) * P], SELW[:, a, :], IDENT)
                        last.then_inc(sig("pick_flipped").sem, 1)
                        turn_hidden(2 * g + 1, 1)
                        outputs(2 * g + 1, 1)
                scatter(every * pairs)

            @block.scalar
            def _(act):
                def gathered(g, b):
                    act.wait_ge(sig("gathered").sem, sig("gathered").at(g + 1))
                    act_.activation(XGS, PB[:, 4:6, :].rearrange("p a b -> p (a b)"), ACT.Copy) \
                        .then_inc(sig("gather_copied").sem, 1)

                def turned(g, b):
                    act.wait_ge(sig("xg_flipped").sem, sig("xg_flipped").at(g + 1))
                    act_.activation(XGT[:, b].rearrange("p k c -> p (k c)"), PB[:, 4:6, :].rearrange("p a b -> p (a b)"),
                                    ACT.Copy).then_inc(sig("xg_copied").sem, 1)

                def silu(n, j):
                    act.wait_ge(used[3].sem, used[3].at(n + 1))
                    act_.activation(HS[CAP:P, j, :], PB[0:CAP, 0, :], ACT.Silu).then_inc(sig("expert_silu").sem, 1)

                def h_turned(n, j):
                    act.wait_ge(sig("h_flipped").sem, sig("h_flipped").at(n + 1))
                    act_.activation(HB[:, j], PB[:, 1, :].rearrange("p (k c) -> p k c", k=4)[:, :, 0:CAP], ACT.Copy) \
                        .then_inc(sig("h_copied").sem, 1)

                def y_out(n, j):
                    act.wait_ge(used[5].sem, used[5].at(n + 1))
                    for m in range(2):
                        last = act_.activation(Y2[slots_of(j), m * T:(m + 1) * T], PB[m * CAP:(m + 1) * CAP, 2, :],
                                               ACT.Copy)
                    last.then_inc(sig("y_copied").sem, 1)

                gathered(0, 0)
                turned(0, 0)
                with act.Fori(0, rounds(act)) as r, act.Fori(0, pairs // 2) as i:
                    for b in range(2):
                        g = pairs * r + 2 * i + b
                        silu(2 * g, 0)
                        h_turned(2 * g, 0)
                        gathered(g + 1, 1 - b)
                        y_out(2 * g, 0)
                        silu(2 * g + 1, 1)
                        turned(g + 1, 1 - b)
                        act.wait_ge(sig("pick_flipped").sem, sig("pick_flipped").at(g + 1))
                        act_.activation(SWT[:, 0:t], PB[:, 3, 0:t], ACT.Copy).then_inc(sig("pick_copied").sem, 1)
                        h_turned(2 * g + 1, 1)
                        y_out(2 * g + 1, 1)

            @block.vector
            def _(dve):
                def pick(p):
                    for j in range(2):
                        for a in range(nt):
                            last = dve_.tensor_scalar(SEL[:, a, slots_of(j)], con("slot"),
                                                      RK[:, a, bass.ds(2 * p + j, 1)], None, ALU.is_equal)
                    last.then_inc(sig("picked").sem, 1)

                def multiply(n, j):
                    dve.wait_ge(sig("expert_silu").sem, sig("expert_silu").at(n + 1))
                    dve_.tensor_tensor(HS[0:CAP, j, :], HS[CAP:P, j, :], PB[CAP:P, 0, :], ALU.mult) \
                        .then_inc(sig("expert_h").sem, 1)

                def add(g):
                    for m in range(KD):
                        dve.wait_ge(sig("scattered").sem, sig("scattered").at(KD * g + m + 1))
                        dve_.tensor_tensor(A[:, m, 0:t], A[:, m, 0:t], PB[:, 6 + m % 2, 0:t], ALU.add) \
                            .then_inc(sig("added").sem, 1)

                dve.wait_ge(sig("cleared").sem, sig("cleared").at(3))
                pick(0)
                dve.wait_ge(sig("gathered").sem, sig("gathered").at(1))
                pick(1)
                every = rounds(dve)
                with dve.Fori(0, every) as r:
                    with dve.Fori(0, pairs // 2) as i:
                        for b in range(2):
                            p = 2 * i + b
                            g = pairs * r + p
                            multiply(2 * g, 0)
                            add(g)
                            dve.wait_ge(sig("pick_flipped").sem, sig("pick_flipped").at(g))
                            for j in range(2):
                                e = bass.ds(2 * p + j, 1)
                                for a in range(nt):
                                    last = dve_.tensor_scalar(SELW[:, a, slots_of(j)], con("slot"), RK[:, a, e],
                                                              WTF[:, a, e], ALU.is_equal, ALU.mult)
                            last.then_inc(sig("weighed").sem, 1)
                            multiply(2 * g + 1, 1)
                            dve.wait_ge(sig("gathered").sem, sig("gathered").at(g + 2))
                            pick(p + 2)
                    dve.wait_ge(sig("picked").sem, sig("picked").at(pairs * r + pairs + 2))
                    dve.wait_ge(sig("weighed").sem, sig("weighed").at(pairs * r + pairs))
                    dve_.tensor_scalar(RK, RK, -float(CAP), None, ALU.add).then_inc(sig("rank_in").sem, 1)
                    dve.wait_ge(sig("rank_in").sem, sig("rank_in").at(r + 1))
                add(every * pairs)
                dve.wait_ge(sig("added").sem, sig("added").at(every * (pairs * KD) + KD))
                for m in range(KD):
                    for c in range(streams):
                        last = dve_.scalar_tensor_tensor(
                            out=X[:, m, half(c)], in0=A[:, m, half(c)], scalar=piece(2 + moe, 5, m, c),
                            in1=X[:, m, half(c)], op0=ALU.mult, op1=ALU.add)
                last.then_inc(sig("normed").sem, 1)
        passed(normed=1, cleared=3)
        counted = used + loaded + [sig(n) for n in ("picked", "gathered", "gather_copied", "xg_flipped", "xg_copied",
                                                    "expert_silu", "expert_h", "h_flipped", "h_copied", "y_copied",
                                                    "weighed", "pick_flipped", "pick_copied", "scattered", "added",
                                                    "rank_in")]
        with nc.Block() as block:
            @block.sync
            def _(sp):
                for s in counted:
                    sp.sem_clear(s.sem)
                    sp.sem_inc(s.sem, FIRST)
        for s in counted:
            s.base = FIRST

    def new_context():
        with nc.Block() as block:
            @block.sync
            def _(sp):
                sp.dma_start(X[:, :, half(1)], io["ctxT_2"].rearrange("(k p) t -> p k t", p=P)) \
                    .then_inc(sig("inputs_in").sem, 16)
                sp.wait_ge(sig("inputs_in").sem, sig("inputs_in").at(16))
        passed(inputs_in=16)

    def final_norm():
        items = [([X[:, k, 0:S] for k in range(KD)], [A[:, k, 0:S] for k in range(KD)],
                  [vec("final", k, k + 1) for k in range(KD)], PB[:, 0, 0:S], ONES, D, P)]
        with nc.Block() as block:
            @block.scalar
            def _(act):
                act_squares(items, 0)
                act_roots(act, items, 0)

            @block.tensor
            def _(pe):
                pe_sums(pe, items, 0)

            @block.vector
            def _(dve):
                dve_norms(dve, items, 0)
        passed(squared=1, summed=1, rooted=1, normed=1, inverted=1)

    stages = [
        lambda: (modulations(), modulated_norm(vec("norm1", 0, KD), 0, 0, 1, T)),
        lambda: mla(0),
        lambda: (modulated_norm(vec("norm2", 0, KD), 0, 3, 4, T),
                 feed_forward(io["ffn_w1"][0], io["ffn_w3"][0], io["ffn_w2"][0], 0, T)),
        lambda: (modulated_norm(vec("norm1", KD, 2 * KD), 1, 0, 1, T), hgrn2(1)),
        lambda: (modulated_norm(vec("norm2", KD, 2 * KD), 1, 3, 4, S),
                 feed_forward(io["ffn_w1"][1], io["ffn_w3"][1], io["ffn_w2"][1], 1, S)),
        lambda: (new_context(), modulated_norm(vec("mix", 0, KD), 2, 0, 1, T), even_mixer(2)),
        lambda: (modulated_norm(vec("ffn", 0, KD), 2, 3, 4, T), experts(2, 0, T)),
        lambda: (modulated_norm(vec("mix", KD, 2 * KD), 3, 0, 1, T), odd_mixer(3)),
        lambda: (modulated_norm(vec("ffn", KD, 2 * KD), 3, 3, 4, S), experts(3, 1, S)),
    ]
    for n, stage in enumerate(stages):
        stage()
        if n == upto:
            store_streams(X[:])
            return
    final_norm()
    store_streams(A[:, :, 0:S])


def layouts(i):
    def blocks(a):
        return np.ascontiguousarray(a.reshape(-1, P).T)

    def twice(a):
        return np.ascontiguousarray(np.tile(a.reshape(-1, HD), (1, 2)).T)

    def everywhere(a):
        return np.ascontiguousarray(np.tile(a.reshape(1, -1), (P, 1)))

    vecs = {
        "norm1": blocks(i["norm1_w"]), "norm2": blocks(i["norm2_w"]), "mla_q": blocks(i["mla_q_norm_w"]),
        "mla_kv": blocks(i["mla_kv_norm_w"]), "mla_qn": blocks(i["mla_qn_w"]), "mla_qr": twice(i["mla_qr_w"]),
        "mla_kn": blocks(i["mla_kn_w"]), "mla_kr": twice(i["mla_kr_w"]), "hg_o": blocks(i["hg_o_norm_w"]),
        "hg_lb": blocks(i["hg_lb_logits"]), "mix": blocks(i["norm_mix_g_2"]), "ffn": blocks(i["norm_ffn_g_2"]),
        "a_q": twice(i["a_q_gain_2"]), "a_k": twice(i["a_k_gain_2"]), "pool": blocks(i["pool_scale_2"]),
        "final": blocks(i["final_g_2"]), "ada_b": np.concatenate([blocks(i["ada_b"]), blocks(i["ada_b_2"])], axis=1),
        "moe_b": everywhere(np.concatenate([i["moe_b_group_2"], i["moe_b_expert_2"]], axis=1)),
    }
    pair = [np.stack([i["c"][0], i["c_ctx"]]), np.stack([i["c_2"][0], i["c_ctx_2"]])]
    padded = np.concatenate([np.stack(pair), np.zeros((2, 30, D), np.float32)], axis=1)
    tok = np.arange(S)
    row = tok[None, :] // GRID - tok[:, None] // GRID + NA_ROWS - 1
    col = np.clip(tok[None, :] % GRID - tok[:, None] % GRID + NA_COLS - 1, 0, 2 * NA_COLS - 2)
    bias = i["na_rel_bias_2"][0][:, row, col]
    given = {
        "xT": i["x"][0].T, "ctxT": i["ctx"][0].T, "ctxT_2": i["ctx_2"][0].T,
        "vecs": np.concatenate([vecs[n] for n, _ in VECS], axis=1),
        "cvec": padded.reshape(2, 32, KD, P).transpose(3, 0, 2, 1).reshape(P, -1),
        "router": np.concatenate([i["moe_w_group_2"], i["moe_w_expert_2"]], axis=2),
        "bias": bias.reshape(2 * 16, P, S),
        "consts": constants(),
    }
    for n in ("ada_w", "ada_w_2", "ffn_w1", "ffn_w3", "ffn_w2", "mla_w_in", "mla_w_uq", "mla_w_ukv", "mla_w_o",
              "hg_w_in", "hg_w_o", "even_w_in_2", "even_w_out_2", "pool_w_2", "odd_w_in_2", "odd_w_out_2",
              "moe_w1_2", "moe_w3_2", "moe_w2_2"):
        given[n] = i[n]
    return {n: np.ascontiguousarray(a) for n, a in given.items()}


def kernel(**inputs):
    import concourse.bacc as bacc
    from concourse.bass_utils import run_bass_kernel_spmd

    arrays = layouts({n: np.asarray(a) for n, a in inputs.items()})
    nc = bacc.Bacc("TRN2", target_bir_lowering=False, num_devices=1)
    io = {n: nc.dram_tensor(n, a.shape, mybir.dt.from_np(a.dtype), kind="ExternalInput").ap()
          for n, a in arrays.items()}
    out = nc.dram_tensor("y", (D, S), F32, kind="ExternalOutput").ap()
    build(nc, io, out)
    r = run_bass_kernel_spmd(nc, [arrays], core_ids=[0])
    return np.ascontiguousarray(r.results[0]["y"].T)[None]
```
